# Optimizing a Trainium2 kernel written in Bass

```python
import jax, jax.numpy as jnp
from jax import lax
import numpy as np

D_MODEL = 1024
BATCH = 1
SEQ = 256
DEPTH = 2
DEC_BATCH = 8
DEC_SEQ = 1
PAST_LEN = 2048
PAGE_SIZE = 128

D_CONV = D_MODEL // 2
CONV_W = 3
RET_HEADS = 4
RET_DK = 128
RET_DV = 128
D_RET = RET_HEADS * RET_DK
RET_CHUNK = 128
ROPE_BASE = 10000.0
D_FF = 3584
N_EXPERTS = 8
TOP_K = 2
D_EXPERT = 3584
D_PLE = 256
EPS = 1e-6
N_IN = 3 * D_CONV + 4 * D_RET + 2 * D_MODEL
N_DENSE = (DEPTH + 1) // 2
N_MOE = DEPTH // 2

kernel_name = "hybrid_conv_retention_moe_decoder_step"

def rms_norm(x, g):
    x32 = x.astype(jnp.float32)
    y = x32 * lax.rsqrt(jnp.mean(x32 * x32, axis=-1, keepdims=True) + EPS) * g.astype(jnp.float32)
    return y.astype(x.dtype)

def rope(x, pos):
    half = x.shape[-1] // 2
    inv = ROPE_BASE ** (-jnp.arange(half, dtype=jnp.float32) / half)
    ang = pos[:, None] * inv[None, :]
    cos = jnp.cos(ang)[None, :, None, :]
    sin = jnp.sin(ang)[None, :, None, :]
    x1, x2 = x[..., :half], x[..., half:]
    return jnp.concatenate([x1 * cos - x2 * sin, x2 * cos + x1 * sin], axis=-1)

def short_conv(u, buf, w):
    T = u.shape[1]
    full = jnp.concatenate([buf.astype(u.dtype), u], axis=1)
    y = w[0] * full[:, 0:T]
    for j in range(1, CONV_W):
        y = y + w[j] * full[:, j:j + T]
    return y, full[:, T:]

def retention_chunk(q, k, v, state, log_gamma):
    L = q.shape[1]
    idx = jnp.arange(L, dtype=jnp.float32)
    diff = idx[:, None] - idx[None, :]
    mask = diff >= 0
    decay = jnp.where(mask[None], jnp.exp(jnp.where(mask, diff, 0.0)[None] * log_gamma[:, None, None]), 0.0)
    scores = jnp.einsum('blhd,bmhd->bhlm', q, k) * decay[None]
    intra = jnp.einsum('bhlm,bmhe->blhe', scores, v)
    q_dec = jnp.exp((idx + 1.0)[:, None] * log_gamma[None, :])
    inter = jnp.einsum('blhd,bhde->blhe', q, state) * q_dec[None, :, :, None]
    k_dec = jnp.exp((L - 1.0 - idx)[:, None] * log_gamma[None, :])
    new_state = jnp.exp(L * log_gamma)[None, :, None, None] * state + jnp.einsum(
        'blhd,blhe->bhde', k * k_dec[None, :, :, None], v)
    return intra + inter, new_state

def retention(q, k, v, state, log_gamma):
    b, T, h, dk = q.shape
    dv = v.shape[-1]
    chunk = RET_CHUNK if T % RET_CHUNK == 0 else T
    n = T // chunk
    if n == 1:
        return retention_chunk(q, k, v, state, log_gamma)
    to_chunks = lambda a: a.reshape(b, n, chunk, h, a.shape[-1]).transpose(1, 0, 2, 3, 4)

    def step(s, inp):
        qc, kc, vc = inp
        o, s2 = retention_chunk(qc, kc, vc, s, log_gamma)
        return s2, o

    s_final, o = lax.scan(step, state, (to_chunks(q), to_chunks(k), to_chunks(v)))
    return o.transpose(1, 0, 2, 3, 4).reshape(b, T, h, dv), s_final

def swiglu(h, w_gu, w_down):
    g, u = jnp.split(h @ w_gu, 2, axis=-1)
    return (jax.nn.silu(g) * u) @ w_down

def moe(h, w_router, w_gu, w_down):
    logits = (h @ w_router).astype(jnp.float32)
    top_v, top_i = lax.top_k(logits, TOP_K)
    top_w = jax.nn.softmax(top_v, axis=-1)
    gates = jnp.sum(jax.nn.one_hot(top_i, N_EXPERTS, dtype=jnp.float32) * top_w[..., None], axis=-2)
    gates = gates.astype(h.dtype)
    out = jnp.zeros_like(h)
    for e in range(N_EXPERTS):
        out = out + gates[:, e:e + 1] * swiglu(h, w_gu[e], w_down[e])
    return out

def mixer(xn, conv_buf, ret_state, pos, w_in, conv_w, w_conv_out, w_ret_out, w_o, log_gamma):
    b, T, _ = xn.shape
    z = xn @ w_in
    cuts = [D_CONV, 2 * D_CONV, 3 * D_CONV,
            3 * D_CONV + D_RET, 3 * D_CONV + 2 * D_RET, 3 * D_CONV + 3 * D_RET, 3 * D_CONV + 4 * D_RET,
            3 * D_CONV + 4 * D_RET + D_MODEL]
    cb, cc, ch, q, k, v, g, ga, gr = jnp.split(z, cuts, axis=-1)
    conv_out, new_buf = short_conv(cc * ch, conv_buf, conv_w)
    a = (cb * conv_out) @ w_conv_out
    q = rope(q.reshape(b, T, RET_HEADS, RET_DK).astype(jnp.float32), pos)
    k = rope(k.reshape(b, T, RET_HEADS, RET_DK).astype(jnp.float32), pos) * (RET_DK ** -0.5)
    v = v.reshape(b, T, RET_HEADS, RET_DV).astype(jnp.float32)
    o, new_state = retention(q, k, v, ret_state.astype(jnp.float32), log_gamma)
    mu = jnp.mean(o, axis=-1, keepdims=True)
    var = jnp.mean(jnp.square(o - mu), axis=-1, keepdims=True)
    o = ((o - mu) * lax.rsqrt(var + EPS)).reshape(b, T, RET_HEADS * RET_DV)
    r = (jax.nn.silu(g.astype(jnp.float32)) * o).astype(xn.dtype) @ w_ret_out
    m = jax.nn.sigmoid(ga) * a + jax.nn.sigmoid(gr) * r
    return m @ w_o, new_buf, new_state

def trunk(x, p, conv_bufs, ret_states, pos0, weights):
    (norm_mix_g, w_in, conv_w, w_conv_out, w_ret_out, w_o, norm_ffn_g,
     w_dense_gu, w_dense_down, w_router, w_exp_gu, w_exp_down,
     norm_ple_g, w_ple, w_ple_gate, norm_final_g) = weights
    b, T, D = x.shape
    pos = pos0 + jnp.arange(T, dtype=jnp.float32)
    log_gamma = jnp.log(1.0 - 2.0 ** (-5.0 - jnp.arange(RET_HEADS, dtype=jnp.float32)))
    new_bufs, new_states = [], []
    for i in range(DEPTH):
        mix, nb, ns = mixer(rms_norm(x, norm_mix_g[i]), conv_bufs[i], ret_states[i], pos,
                            w_in[i], conv_w[i], w_conv_out[i], w_ret_out[i], w_o[i], log_gamma)
        new_bufs.append(nb)
        new_states.append(ns)
        x = x + mix
        hn = rms_norm(x, norm_ffn_g[i])
        if i % 2 == 0:
            f = swiglu(hn, w_dense_gu[i // 2], w_dense_down[i // 2])
        else:
            f = moe(hn.reshape(b * T, D), w_router[i // 2], w_exp_gu[i // 2],
                    w_exp_down[i // 2]).reshape(b, T, D)
        x = x + f
        gate = jax.nn.sigmoid(rms_norm(x, norm_ple_g[i]) @ w_ple_gate[i])
        x = x + gate * (p[i] @ w_ple[i])
    return rms_norm(x, norm_final_g), jnp.stack(new_bufs), jnp.stack(new_states)

def setup_inputs(seed: int = 0) -> dict:
    key = jax.random.key(seed)
    ks = jax.random.split(key, 32)
    f32 = jnp.float32
    nrm = lambda k, shape, scale: jax.random.normal(k, shape, f32) * scale
    gain = lambda k, shape: 1.0 + 0.02 * jax.random.normal(k, shape, f32)
    return {
        "x_prompt": nrm(ks[0], (BATCH, SEQ, D_MODEL), 1.0),
        "x_sample": nrm(ks[1], (DEC_BATCH, DEC_SEQ, D_MODEL), 1.0),
        "state_conv": nrm(ks[2], (DEPTH, DEC_BATCH, CONV_W - 1, D_CONV), 1.0),
        "state_ret": nrm(ks[3], (DEPTH, DEC_BATCH, RET_HEADS, RET_DK, RET_DV), 0.1),
        "p_prompt": nrm(ks[4], (DEPTH, BATCH, SEQ, D_PLE), 1.0),
        "p_sample": nrm(ks[5], (DEPTH, DEC_BATCH, DEC_SEQ, D_PLE), 1.0),
        "norm_mix_g": gain(ks[6], (DEPTH, D_MODEL)),
        "w_in": nrm(ks[7], (DEPTH, D_MODEL, N_IN), D_MODEL ** -0.5),
        "conv_w": nrm(ks[8], (DEPTH, CONV_W, D_CONV), CONV_W ** -0.5),
        "w_conv_out": nrm(ks[9], (DEPTH, D_CONV, D_MODEL), D_CONV ** -0.5),
        "w_ret_out": nrm(ks[10], (DEPTH, RET_HEADS * RET_DV, D_MODEL), (RET_HEADS * RET_DV) ** -0.5),
        "w_o": nrm(ks[11], (DEPTH, D_MODEL, D_MODEL), D_MODEL ** -0.5),
        "norm_ffn_g": gain(ks[12], (DEPTH, D_MODEL)),
        "w_dense_gu": nrm(ks[13], (N_DENSE, D_MODEL, 2 * D_FF), D_MODEL ** -0.5),
        "w_dense_down": nrm(ks[14], (N_DENSE, D_FF, D_MODEL), D_FF ** -0.5),
        "w_router": nrm(ks[15], (N_MOE, D_MODEL, N_EXPERTS), D_MODEL ** -0.5),
        "w_exp_gu": nrm(ks[16], (N_MOE, N_EXPERTS, D_MODEL, 2 * D_EXPERT), D_MODEL ** -0.5),
        "w_exp_down": nrm(ks[17], (N_MOE, N_EXPERTS, D_EXPERT, D_MODEL), D_EXPERT ** -0.5),
        "norm_ple_g": gain(ks[18], (DEPTH, D_MODEL)),
        "w_ple": nrm(ks[19], (DEPTH, D_PLE, D_MODEL), D_PLE ** -0.5),
        "w_ple_gate": nrm(ks[20], (DEPTH, D_MODEL, D_MODEL), D_MODEL ** -0.5),
        "norm_final_g": gain(ks[21], (D_MODEL,)),
    }

def reference(x_prompt, x_sample, state_conv, state_ret, p_prompt, p_sample,
              norm_mix_g, w_in, conv_w, w_conv_out, w_ret_out, w_o, norm_ffn_g,
              w_dense_gu, w_dense_down, w_router, w_exp_gu, w_exp_down,
              norm_ple_g, w_ple, w_ple_gate, norm_final_g):
    weights = (norm_mix_g, w_in, conv_w, w_conv_out, w_ret_out, w_o, norm_ffn_g,
               w_dense_gu, w_dense_down, w_router, w_exp_gu, w_exp_down,
               norm_ple_g, w_ple, w_ple_gate, norm_final_g)
    b = x_prompt.shape[0]
    zero_conv = jnp.zeros((DEPTH, b, CONV_W - 1, D_CONV), x_prompt.dtype)
    zero_ret = jnp.zeros((DEPTH, b, RET_HEADS, RET_DK, RET_DV), jnp.float32)
    y_prompt, conv_prompt, ret_prompt = trunk(x_prompt, p_prompt, zero_conv, zero_ret, 0.0, weights)
    y_sample, conv_sample, ret_sample = trunk(x_sample, p_sample, state_conv, state_ret,
                                              float(PAST_LEN), weights)
    return (y_prompt, y_sample, conv_prompt, ret_prompt, conv_sample, ret_sample)


_drawn_inputs = setup_inputs


def setup_inputs(seed=0):
    import zlib

    import numpy as np

    out = dict(_drawn_inputs(seed))
    spreads = {}
    factors = {'norm_ple_g': 5.186, 'norm_final_g': 2.73}
    for name, (base, spread) in spreads.items():
        noise = np.random.default_rng([zlib.crc32(name.encode()), seed]).standard_normal(out[name].shape)
        drawn = base * np.exp(spread * noise) if base else spread * noise
        out[name] = __import__('jax').numpy.asarray(drawn.astype(out[name].dtype))
    for name, factor in factors.items():
        out[name] = (out[name] * factor).astype(out[name].dtype)
    return out
```

```python
import math

import numpy as np
import concourse.bass as bass
from concourse import mybir
from contextlib import ExitStack

D = 1024
SEQ = 256
NB = 8
T = SEQ + NB
KT = D // 128
DC = 512
NH = 4
DK = 128
DR = NH * DK
DFF = 3584
NE = 8
DPLE = 256
DEPTH = 2
CW = 3
NIN = 3 * DC + 4 * DR + 2 * D
EPS = 1e-6
PAST = 2048
TT = 88
CH = 2048
RAW, CAST = 6, 3
AHEAD = 2
RING = 3

C_ID, C_ONE, C_MEAN = 0, 128, 256
C_COS, C_SIN = 384, 384 + T
C_DEC = C_SIN + T
C_KD = C_DEC + NH * SEQ
C_EYE8 = C_KD + NH * 2
C_IOTA = C_EYE8 + 8
C_TRI = C_IOTA + 128
NCONST = C_TRI + TT

GAMMA = [1.0 - 2.0 ** (-5.0 - h) for h in range(NH)]


def constants():
    c = np.zeros((128, NCONST), np.float32)
    c[:, C_ID:C_ID + 128] = np.eye(128)
    c[:, C_ONE:C_ONE + 128] = 1.0
    c[:, C_MEAN:C_MEAN + 128] = 1.0 / DK
    half = DK // 2
    inv = np.float32(10000.0) ** (-np.arange(half, dtype=np.float32) / np.float32(half))
    pos = np.concatenate([np.arange(SEQ), np.full(NB, PAST)]).astype(np.float32)
    ang = (pos[None, :] * inv[:, None]).astype(np.float32).astype(np.float64)
    c[:half, C_COS:C_COS + T] = np.cos(ang)
    c[half:, C_COS:C_COS + T] = np.cos(ang)
    c[:half, C_SIN:C_SIN + T] = np.sin(ang)
    c[half:, C_SIN:C_SIN + T] = -np.sin(ang)
    m = np.arange(128)[:, None]
    l = np.arange(SEQ)[None, :]
    s = DK ** -0.5
    for h in range(NH):
        lg = float(np.log(np.float32(GAMMA[h])))
        d = np.where(l >= m, np.exp(np.maximum(l - m, 0) * lg), 0.0) * s
        c[:, C_DEC + h * SEQ:C_DEC + (h + 1) * SEQ] = d
        for i in range(2):
            c[:, C_KD + 2 * h + i] = np.exp((SEQ - 1 - 128 * i - m[:, 0]) * lg) * s
    c[:8, C_EYE8:C_EYE8 + 8] = np.eye(8)
    c[:, C_IOTA:C_IOTA + 128] = np.arange(128)[None, :]
    t = np.arange(TT)
    c[:TT, C_TRI:C_TRI + TT] = (t[:, None] < t[None, :])
    return c


def chunk_bases():
    b, at = [], 0
    for l in range(DEPTH):
        s = {}
        for name, n in (("in", 14), ("conv", 2), ("ret", 2), ("gate", 8), ("o", 4)):
            s[name] = at
            at += n
        s["ffn"] = at
        if l == 0:
            at += 44
        s["pw"], s["pg"] = at, at + 1
        at += 5
        b.append(s)
    return b


CB = chunk_bases()
NCHUNK = CB[1]["pg"] + 4
MOE_CHUNKS = 42
MOE_TURNS = MOE_CHUNKS // RAW


def tile_bases():
    b, at = [], 14
    for l in range(DEPTH):
        s = {}
        rows = [("in", 28), ("conv", 8), ("ret", 8), ("gate", 16), ("o", 8)]
        if l == 0:
            rows += [("gu0", 28), ("down0", 8), ("gu1", 28), ("down1", 8)]
        for name, n in rows + [("pw", 8), ("pg", 8)]:
            s[name] = at
            at += n
        b.append(s)
    return b


TB = tile_bases()
NORM_OF = {("in", 0): 0, ("ffn", 0): 1, ("ple", 0): 2, ("in", 1): 3, ("ffn", 1): 4, ("ple", 1): 5}
GAIN = {0: 0, 3: 8, 1: 16, 4: 24, 2: 32, 5: 40, 6: 48}
CONVW = 56


def program(nc, A, O):
    F32, F32R, I32, U32 = mybir.dt.float32, mybir.dt.float32r, mybir.dt.int32, mybir.dt.uint32
    ALU, ACT, AX = mybir.AluOpType, mybir.ActivationFunctionType, mybir.AxisListType
    ds = bass.ds
    es = ExitStack()
    with es:
        def sb(name, shape, dt=F32):
            return es.enter_context(nc.sbuf_tensor(name, shape, dt))

        def sem(name):
            return es.enter_context(nc.semaphore(name))

        raw = sb("raw", [128, RAW, CH])
        whi = sb("whi", [128, CAST, CH], F32R)
        wlo = sb("wlo", [128, CAST, CH], F32R)
        x = sb("x", [128, KT, T])
        xh = sb("xh", [128, KT * T], F32R)
        xl = sb("xl", [128, KT * T], F32R)
        z = sb("z", [128, 28 * T])
        con = sb("con", [128, NCONST])
        idr = sb("idr", [128, 128], F32R)
        vec = sb("vec", [128, 80])
        cst = sb("cst", [128, DEPTH, 4, 16])
        ph = sb("ph", [128, 4, T], F32R)
        pl = sb("pl", [128, 4, T], F32R)
        ub = sb("ub", [128, 4, 2 + SEQ])
        us = sb("us", [128, 4, NB])
        cbt = sb("cbt", [128, 4, 18])
        rstd = sb("rstd", [128, T])
        sq = sb("sq", [128, T])
        sacc = sb("sacc", [128, T])
        FR = 28 * T
        fr_at = nc.sbuf_usable_end - FR * 4
        fr_at -= fr_at % 32
        fr = nc.alloc_sbuf_tensor_at("fr", [128, FR], F32R, offset=fr_at)
        scr = nc.alloc_sbuf_tensor_at("scr", [128, 20 * T], F32, offset=fr_at + 8 * T * 4)
        PS = es.enter_context(nc.psum_tensor("PS", [128, 8, 512], F32))

        ident = con[:, C_ID:C_ID + 128]
        ones = con[:, C_ONE:C_ONE + 128]
        mean = con[:, C_MEAN:C_MEAN + 128]
        cos = con[:, C_COS:C_COS + T]
        sin = con[:, C_SIN:C_SIN + T]
        dec = con[:, C_DEC:C_DEC + NH * SEQ].rearrange("p (h l) -> p h l", h=NH)
        kd = con[:, C_KD:C_KD + 8]
        eye8 = con[0:8, C_EYE8:C_EYE8 + 8]
        iota = con[0:TT, C_IOTA:C_IOTA + 128]
        iota8 = con[0:TT, C_IOTA:C_IOTA + 8]
        tri = con[0:TT, C_TRI:C_TRI + TT]

        zt = z[:, :].rearrange("p (t c) -> p t c", c=T)
        frt = fr[:, :].rearrange("p (t c) -> p t c", c=T)
        xht = xh[:, :].rearrange("p (t c) -> p t c", c=T)
        xlt = xl[:, :].rearrange("p (t c) -> p t c", c=T)
        xtok = z[0:TT, 0:3 * D].rearrange("p (t f) -> p t f", t=3)
        ptok = z[0:TT, 3 * D:3 * D + 3 * 512].rearrange("p (t f) -> p t f", t=3)
        vrow = z[0:80, 4608:4736]
        crow = z[0:16, 4736:4736 + 1024].rearrange("p (l f) -> p l f", l=DEPTH)
        CBt, CCt, CHt = zt[:, 0:4, :], zt[:, 4:8, :], zt[:, 8:12, :]
        Qt, Kt, Vt, Gt = zt[:, 12:16, :], zt[:, 16:20, :], zt[:, 20:24, :], zt[:, 24:28, :]
        rtmp = scr[:, 0:4 * T].rearrange("p (h t) -> p h t", h=4)
        ktok, vtok = scr[:, 0:256], scr[:, 256:512]
        sc = scr[:, 512:896]
        vd = scr[0:8, 896:1920].rearrange("p (b e) -> p b e", b=8)
        kss = scr[0:8, 1920:2048]
        St = [scr[:, 2112 + 1024 * i:3136 + 1024 * i] for i in range(2)]
        so = scr[:, 4160:4672].rearrange("p (h e) -> p h e", h=4)
        cout = scr[0:18, 4672:5184]
        htok_h = fr[0:TT, 0:3072].rearrange("p (t f) -> p t f", t=3)
        htok_l = fr[0:TT, 3072:6144].rearrange("p (t f) -> p t f", t=3)
        actT_h, actT_l = fr[:, 6144:6656], fr[:, 6656:7168]
        gh, gl = xh[:, 0:D], xl[:, 0:D]
        yh, yl = xh[:, D:2 * D], xl[:, D:2 * D]
        sel = ph[0:TT, 0:2, :].rearrange("p a t -> p (a t)")[:, 0:384].rearrange("p (i s) -> p i s", i=3)
        selT = pl[:, 0, :]
        sgm, ggm, aam = z[:, 0:512], z[:, 512:1024], z[:, 1024:1536]
        wrr = sb("wrr", [128, 64])
        rt = z[0:TT, 1600:2200]
        wrh = sb("wrh", [128, 64], F32R)
        wrl = sb("wrl", [128, 64], F32R)
        posm = sb("posm", [TT, 3, 8])
        rg = sb("rg", [TT, 3, 10])
        srg = sb("srg", [128, 10])
        passes = sb("passes", [1, 1], I32)
        idx = sb("idx", [TT, 3, 8], U32)

        raw_landed = [sem(f"raw_landed{i}") for i in range(RAW)]
        hi_done, lo_done, chunk_begun = sem("hi_done"), sem("lo_done"), sem("chunk_begun")
        in_con, in_x, in_misc, in_wr = sem("in_con"), sem("in_x"), sem("in_misc"), sem("in_wr")
        tile_ready, tile_taken = sem("tile_ready"), sem("tile_taken")
        idr_done, pad_done = sem("idr_done"), sem("pad_done")
        p_hi = sem("p_hi")
        x_ready, xh_ready, xl_ready = sem("x_ready"), sem("xh_ready"), sem("xl_ready")
        pool_chain, dve_chain = sem("pool_chain"), sem("dve_chain")
        sq_ready, stat_ready, root_ready, rstd_ready = (sem("sq_ready"), sem("stat_ready"),
                                                        sem("root_ready"), sem("rstd_ready"))
        u_ready, y_conv, a32, a_hi, a_lo = (sem("u_ready"), sem("y_conv"), sem("a32"), sem("a_hi"),
                                            sem("a_lo"))
        cbt_ready, cbT_ready, cout_ready, cout_sent = (sem("cbt_ready"), sem("cbT_ready"),
                                                       sem("cout_ready"), sem("cout_sent"))
        rope_ready, kvT_ready, ktok_ready, vtok_ready = (sem("rope_ready"), sem("kvT_ready"),
                                                         sem("ktok_ready"), sem("vtok_ready"))
        score_ready, sc_ready, so_ready, so_sent = (
            sem("score_ready"), sem("sc_ready"), sem("so_ready"), sem("so_sent"))
        kv_outer, s_new = sem("kv_outer"), sem("s_new")
        s_in = [sem("s_in0"), sem("s_in1")]
        s_sent = [sem("s_sent0"), sem("s_sent1")]
        o_ready, o_taken, mu_ready, oc_ready, osq_ready, var_ready, ort_ready = (
            sem("o_ready"), sem("o_taken"), sem("mu_ready"), sem("oc_ready"), sem("osq_ready"),
            sem("var_ready"), sem("ort_ready"))
        sg_ready, gsl_ready, r32, r_hi, r_lo = (sem("sg_ready"), sem("gsl_ready"), sem("r32"),
                                                sem("r_hi"), sem("r_lo"))
        gsig, m32, m_hi, m_lo = sem("gsig"), sem("m32"), sem("m_hi"), sem("m_lo")
        f_sig, f_silu, f_act, f_hi, f_lo = (sem("f_sig"), sem("f_silu"), sem("f_act"),
                                            sem("f_hi"), sem("f_lo"))
        psig = sem("psig")
        wr_hi, wr_lo = sem("wr_hi"), sem("wr_lo")
        tok_ready, tokh_done, tokl_done = sem("tok_ready"), sem("tokh_done"), sem("tokl_done")
        logit_ready, route_act, route_dve, rank_ready, routed = (
            sem("logit_ready"), sem("route_act"), sem("route_dve"), sem("rank_ready"), sem("routed"))
        sel_ready, gather_ready, slot_taken, gh_done, gl_done = (
            sem("sel_ready"), sem("gather_ready"), sem("slot_taken"), sem("gh_done"), sem("gl_done"))
        g_ready, u_rdy, sg_done, gg_done, aa_done = (sem("g_ready"), sem("u_rdy"), sem("sg_done"),
                                                     sem("gg_done"), sem("aa_done"))
        aT_ready, aTh_done, aTl_done = sem("aT_ready"), sem("aTh_done"), sem("aTl_done")
        y_ready, yh_done, yl_done = sem("y_ready"), sem("yh_done"), sem("yl_done")
        scat_ready, scat_taken, pass_done, moe_done = (sem("scat_ready"), sem("scat_taken"),
                                                       sem("pass_done"), sem("moe_done"))
        fin_ready, finT_ready, out_ready, out_sent = (sem("fin_ready"), sem("finT_ready"),
                                                      sem("out_ready"), sem("out_sent"))

        sq_root = sb("sq_root", [128, T])
        epsb = sb("epsb", [128, 1])
        sgate = sb("sgate", [128, 1])
        eps_done, sgate_done, pprod = sem("eps_done"), sem("sgate_done"), sem("pprod")

        def x_at(norm, j):
            if norm == 5:
                return moe_done, 1
            if norm in (3, 6):
                return x_ready, 8 * (norm // 3 - 1) + j + 1
            base = {0: 2, 1: TB[0]["o"], 2: TB[0]["down1"], 4: TB[1]["o"]}[norm]
            return tile_taken, base + j + 1

        def turn_of(norm):
            return norm if norm < 4 else norm - 1

        assert nc.sbuf_base <= fr_at, (nc.sbuf_base, fr_at)
        block = es.enter_context(nc.Block())

        def ple_loads(sp, load, rows, l, turns):
            b = CB[l]
            load(b["pw"], rows(A["w_ple"][l], 2), turns)
            for i in range(4):
                load(b["pg"] + i, rows(A["w_ple_gate"][l], 8)[:, :, 256 * i:256 * i + 256], turns)


        def moe_loads(sp, load, ps):
            b = CB[1]["ffn"]
            gu = A["w_exp_gu"].rearrange("o e (k p) n -> (o e) p k n", p=128)
            dn = A["w_exp_down"].rearrange("o e (k p) n -> (o e) p k n", p=128)
            with sp.Fori(0, NE) as e:
                t0 = (ps * NE + e) * MOE_TURNS

                def up(c, s, j, turns):
                    col = (s // 2) * DFF
                    src = gu[ds(e, 1), :, 4 * (s % 2):4 * (s % 2) + 4, ds(j * 512 + col, 512)]
                    load(c, src.rearrange("o p k n -> (o p) k n"), turns)

                def down(c, s, j, turns):
                    src = dn[ds(e, 1), :, ds(j * 4 + 2 * s, 2), :]
                    load(c, src.rearrange("o p k n -> (o p) k n"), turns)

                for s in range(4):
                    up(b + s, s, 0, t0)
                with sp.Fori(0, 6) as i:
                    for s in range(4):
                        up(b + 4 + s, s, i + 1, t0 + i)
                    for s in range(2):
                        down(b + 8 + s, s, i, t0 + i)
                for s in range(2):
                    down(b + 40 + s, s, 6, t0)


        def ffn_tiles(q):
            q = q % 3
            return [zt[:, 8 * q + 2 * i:8 * q + 2 * i + 2, :] for i in range(4)]


        @block.sync
        def _(sp):
            def load(c, src, turns=0, width=CH):
                if not (isinstance(turns, int) and c + RAW * turns < RAW):
                    sp.wait_ge(lo_done, (turns - 1) * RAW + c + 1)
                k = src.shape[1] if len(src.shape) == 3 else 1
                dst = raw[:, c % RAW, 0:width].rearrange("p (k n) -> p k n", k=k)
                sp.dma_start(dst, src).then_inc(raw_landed[c % RAW], 16)

            sp.dma_start(con[:, :], A["constants"]).then_inc(in_con, 16)
            xp = A["x_prompt"].rearrange("b t f -> (b t) f")
            xs = A["x_sample"].rearrange("b t f -> (b t) f")
            sp.dma_start(xtok[:, 0:2, :], xp[0:2 * TT, :].rearrange("(i p) f -> p i f", p=TT)).then_inc(in_x, 16)
            sp.dma_start(xtok[0:SEQ - 2 * TT, 2, :], xp[2 * TT:SEQ, :]).then_inc(in_x, 16)
            sp.dma_start(xtok[SEQ - 2 * TT:TT, 2, :], xs).then_inc(in_x, 16)

            def rows(w, nk):
                return w.rearrange("(k p) n -> p k n", p=128)[:, 0:nk, :]

            for l in range(DEPTH):
                b = CB[l]
                win = rows(A["w_in"][l], 8)
                if l == 0:
                    for i in range(14):
                        load(b["in"] + i, win[:, :, 256 * i:256 * i + 256])
                else:
                    for i in range(2):
                        load(b["in"] + i, win[:, :, 256 * i:256 * i + 256])
                    with sp.Fori(0, 2) as it:
                        for s in range(6):
                            load(b["in"] + 2 + s, win[:, :, ds(it * 1536 + 512 + 256 * s, 256)], it)
                for i in range(2):
                    load(b["conv"] + i, rows(A["w_conv_out"][l], 4)[:, :, 512 * i:512 * i + 512])
                for i in range(2):
                    load(b["ret"] + i, rows(A["w_ret_out"][l], 4)[:, :, 512 * i:512 * i + 512])
                for i in range(8):
                    at = 3 * DC + 4 * DR + (i % 2) * D + (i // 2) * 256
                    load(b["gate"] + i, win[:, :, at:at + 256])
                for i in range(4):
                    load(b["o"] + i, rows(A["w_o"][l], 8)[:, :, 256 * i:256 * i + 256])
                if l == 0:
                    gu = rows(A["w_dense_gu"][0], 8)
                    dn = A["w_dense_down"][0].rearrange("(k p) n -> p k n", p=128)
                    for hf in range(2):
                        c0 = b["ffn"] + 22 * hf
                        for i in range(2):
                            load(c0 + i, gu[:, :, DFF * i + 1792 * hf:][:, :, 0:256])
                        with sp.Fori(0, 2) as it:
                            for s in range(6):
                                at = (s % 2) * DFF + 1792 * hf + 256 * (1 + s // 2)
                                load(c0 + 2 + s, gu[:, :, ds(it * 768 + at, 256)], it)
                        for i in range(8):
                            load(c0 + 14 + i, dn[:, 14 * hf:14 * hf + 14, 128 * i:128 * i + 128],
                                 width=14 * 128)
                    ple_loads(sp, load, rows, l, 0)
                else:
                    moe_loads(sp, load, 0)
                    sp.wait_ge(routed, 1)
                    n = sp.value_load(passes[0:1, 0:1], min_val=1, max_val=3)
                    with sp.If(n > 1):
                        with sp.Fori(1, n) as ps:
                            moe_loads(sp, load, ps)
                    with sp.Else():
                        sp.nop()
                    ple_loads(sp, load, rows, l, n * (NE * MOE_TURNS))

        @block.gpsimd
        def _(pool):
            n_chain = [0]

            def link(ins):
                n_chain[0] += 1
                ins.then_inc(pool_chain, 1)
                pool.wait_ge(pool_chain, n_chain[0])

            def squares(norm):
                for j in range(KT):
                    pool.wait_ge(*x_at(norm, j))
                    if j == 0:
                        if norm not in (0, 5):
                            pool.wait_ge(stat_ready, turn_of(norm))
                        link(pool.tensor_tensor(sacc[:, :], x[:, 0, :], x[:, 0, :], ALU.mult))
                    else:
                        link(pool.tensor_tensor(sq[:, :], x[:, j, :], x[:, j, :], ALU.mult))
                        ins = pool.tensor_tensor(sacc[:, :], sacc[:, :], sq[:, :], ALU.add)
                        if j == KT - 1:
                            ins.then_inc(sq_ready, 1)
                            pool.wait_ge(sq_ready, norm + 1)
                        else:
                            link(ins)

            pool.dma_start(vrow[0:16, :], A["norm_mix_g"].rearrange("l (k p) -> (l k) p", p=128)).then_inc(in_misc, 16)
            pool.dma_start(vrow[16:32, :], A["norm_ffn_g"].rearrange("l (k p) -> (l k) p", p=128)).then_inc(in_misc, 16)
            pool.dma_start(vrow[32:48, :], A["norm_ple_g"].rearrange("l (k p) -> (l k) p", p=128)).then_inc(in_misc, 16)
            pool.dma_start(vrow[48:56, :], A["norm_final_g"].rearrange("(k p) -> k p", p=128)).then_inc(in_misc, 16)
            pool.dma_start(vrow[56:80, :], A["conv_w"].rearrange("l w (k p) -> (l w k) p", p=128)).then_inc(in_misc, 16)
            pool.dma_start(crow, A["state_conv"].rearrange("l b w c -> (b w) l c")).then_inc(in_misc, 16)
            pp = A["p_prompt"].rearrange("l b t f -> (b t) l f")
            ps_ = A["p_sample"].rearrange("l b t f -> (b t) l f")
            for i in range(2):
                pool.dma_start(ptok[:, i, :].rearrange("p (l f) -> p l f", l=2), pp[TT * i:TT * i + TT]).then_inc(in_misc, 16)
            pool.dma_start(ptok[0:80, 2, :].rearrange("p (l f) -> p l f", l=2), pp[2 * TT:SEQ]).then_inc(in_misc, 16)
            pool.dma_start(ptok[80:88, 2, :].rearrange("p (l f) -> p l f", l=2), ps_).then_inc(in_misc, 16)
            pool.dma_start(wrr[:, :].rearrange("p (k n) -> p k n", n=NE), A["w_router"][0].rearrange("(k p) n -> p k n", p=128)).then_inc(in_wr, 16)
            pool.memset(ub[:, :, 0:2], 0.0).then_inc(pad_done, 1)
            pool.wait_ge(pad_done, 1)
            squares(0)
            for l in range(DEPTH):
                t = TB[l]
                if l > 0:
                    pool.wait_ge(chunk_begun, CB[l]["in"] + 1)
                    pool.wait_ge(so_sent, 16 * l)
                    pool.wait_ge(cout_sent, 32 * l)

                def load_state(h):
                    r = 4 * l + h
                    if r >= 2:
                        pool.wait_ge(s_sent[r % 2], 16 * (r // 2))
                        pool.wait_ge(o_ready, r - 1)
                    pool.dma_start(St[r % 2].rearrange("p (b e) -> p b e", b=8),
                                   A["state_ret"][l, :, h, :, :].rearrange("b d e -> d b e")).then_inc(s_in[r % 2], 16)

                load_state(0)
                load_state(1)
                pool.wait_ge(tile_taken, t["in"] + 12)
                if l > 0:
                    pool.wait_ge(y_conv, l)
                    pool.wait_ge(cbt_ready, l)
                pool.tensor_tensor(ub[:, :, 2:2 + SEQ], CCt[:, :, 0:SEQ], CHt[:, :, 0:SEQ], ALU.mult).then_inc(u_ready, 1)
                pool.tensor_tensor(us[:, :, :], CCt[:, :, SEQ:T], CHt[:, :, SEQ:T], ALU.mult).then_inc(u_ready, 1)
                pool.wait_ge(u_ready, 2 * l + 2)
                if l > 0:
                    pool.wait_ge(cbT_ready, l)
                new = cbt[:, :, 2:18].rearrange("p k (b w) -> p k b w", w=2)
                old = cst[:, l, :, :].rearrange("p k (b w) -> p k b w", w=2)
                pool.tensor_copy(cbt[:, :, 0:2], ub[:, :, SEQ:SEQ + 2]).then_inc(pad_done, 1)
                pool.tensor_copy(new[:, :, :, 0], old[:, :, :, 1]).then_inc(pad_done, 1)
                pool.tensor_copy(new[:, :, :, 1], us[:, :, :]).then_inc(pad_done, 1)
                pool.wait_ge(pad_done, 1 + 3 * (l + 1))
                pool.nop().then_inc(cbt_ready, 1)
                pool.wait_ge(y_conv, l + 1)
                pool.tensor_tensor(CHt, CBt, CCt, ALU.mult).then_inc(a32, 1)
                pool.wait_ge(cout_ready, l + 1)
                pool.dma_start(O["conv_prompt"][l, 0, :, :], cout[0:2, :]).then_inc(cout_sent, 16)
                pool.dma_start(O["conv_sample"][l].rearrange("b w c -> (b w) c"), cout[2:18, :]).then_inc(cout_sent, 16)
                for h in range(NH):
                    r = 4 * l + h
                    pool.wait_ge(s_new, 2 * r + 2)
                    pool.dma_start(O["ret_sample"][l, :, h, :, :].rearrange("b d e -> d b e"),
                                   St[r % 2].rearrange("p (b e) -> p b e", b=8)).then_inc(s_sent[r % 2], 16)
                    if h + 2 < NH:
                        load_state(h + 2)
                pool.wait_ge(so_ready, 4 * l + 4)
                pool.dma_start(O["ret_prompt"][l, 0, :, :, :].rearrange("h d e -> d h e"), so).then_inc(so_sent, 16)
                pool.wait_ge(sg_ready, l + 1)
                pool.tensor_tensor(Gt, Gt, Vt, ALU.mult).then_inc(gsl_ready, 1)
                pool.wait_ge(oc_ready, l + 1)
                pool.tensor_tensor(rtmp, Qt, Qt, ALU.mult).then_inc(osq_ready, 1)
                squares(1 + 3 * l)
                if l == 0:
                    def silu(q, turns=0):
                        gb, sb_ = ffn_tiles(q)[0:2]
                        pool.wait_ge(f_sig, 1 + q + turns)
                        pool.tensor_tensor(gb, gb, sb_, ALU.mult).then_inc(f_silu, 1)
                    for hf in range(2):
                        silu(7 * hf)
                        with pool.Fori(0, 2) as it:
                            for q in range(3):
                                silu(7 * hf + 1 + q, 3 * it)
                    squares(2)
                    squares(3)
            squares(5)
            squares(6)
            for i in range(3):
                pool.wait_ge(out_ready, 2 * i + 2)
                if i < 2:
                    pool.dma_start(O["y_prompt"][0, TT * i:TT * i + TT, :], xtok[:, i, :]).then_inc(out_sent, 16)
                else:
                    pool.dma_start(O["y_prompt"][0, 2 * TT:SEQ, :], xtok[0:80, 2, :]).then_inc(out_sent, 16)
                    pool.dma_start(O["y_sample"][:, 0, :], xtok[80:88, 2, :]).then_inc(out_sent, 16)
            pool.wait_ge(out_sent, 64)
            pool.wait_ge(cout_sent, 32 * DEPTH)
            pool.wait_ge(so_sent, 16 * DEPTH)
            for i in range(2):
                pool.wait_ge(s_sent[i], 16 * 2 * DEPTH)

        def gt_in(n):
            return zt[:, 20 + n % 8, :]


        def dense_act(act, cast, root, split_x):
            b, t = CB[0], TB[0]

            def pair(q, c, tile, turns=0, t3=0):
                gb, sb_, ub_, ab = ffn_tiles(q)
                cast(c + AHEAD, turns)
                act.wait_ge(tile_taken, tile + 2 + 12 * turns)
                nc.scalar.activation(sb_, gb, ACT.Sigmoid).then_inc(f_sig, 1)
                cast(c + 1 + AHEAD, turns)

            for i in range(2):
                act.wait_ge(s_sent[i], 32)
            act.wait_ge(so_sent, 16)
            act.wait_ge(cout_sent, 32)

            def hi(q, pos, turns=0):
                act.wait_ge(f_act, 1 + q + 3 * turns)
                dst = frt[:, ds(turns * 6 + 2 * pos, 2), :]
                nc.scalar.activation(dst, ffn_tiles(q)[3], ACT.Copy).then_inc(f_hi, 1)

            for hf in range(2):
                c0 = b["ffn"] + 22 * hf
                t0 = t[f"gu{hf}"]
                if hf == 0:
                    cast(c0 + AHEAD)
                    root(1)
                    act.wait_ge(tile_taken, t0 + 2)
                    nc.scalar.activation(ffn_tiles(0)[1], ffn_tiles(0)[0], ACT.Sigmoid).then_inc(f_sig, 1)
                    cast(c0 + 1 + AHEAD)
                else:
                    pair(7, c0, t0)
                with act.Fori(0, 2) as it:
                    for q in range(3):
                        pair(7 * hf + 1 + q, c0 + 2 + 2 * q, t0 + 4 + 4 * q, it)
                        hi(7 * hf + q, q, it)
                hi(7 * hf + 6, 6)
                for i in range(8):
                    cast(c0 + 14 + i + AHEAD)
                    if hf == 1:
                        split_x(2, (i,))


        def ple_act(act, cast, root, split_x, l, turns=0):
            b, t = CB[l], TB[l]
            last = l == DEPTH - 1
            cast(b["pw"] + AHEAD, turns)
            norm = NORM_OF["ple", l]
            for i in range(4):
                if not (last and i + 1 + AHEAD > 4):
                    cast(b["pg"] + i + AHEAD, turns)
                if i == 0:
                    root(norm)
                for s in range(2):
                    j = 2 * i + s
                    act.wait_ge(tile_taken, t["pg"] + j + 1)
                    nc.scalar.activation(zt[:, 8 + j, :], zt[:, 8 + j, :], ACT.Sigmoid).then_inc(psig, 1)
            if not last:
                act.wait_ge(tile_ready, t["pg"] + 8)
                split_x(3)


        def moe_act(act, cast, root, split_x):
            b = CB[1]["ffn"]
            act.wait_ge(in_wr, 16)
            nc.scalar.activation(wrh[:, :], wrr[:, :], ACT.Copy).then_inc(wr_hi, 1)
            act.wait_ge(logit_ready, 1)
            nc.scalar.activation(rt[:, 0:3], PS[0:TT, 7, 24:27], ACT.Sqrt, bias=epsb[0:TT, :],
                                 scale=1.0 / D).then_inc(route_act, 1)
            for i in range(2):
                act.wait_ge(s_sent[i], 64)
            act.wait_ge(so_sent, 32)
            act.wait_ge(cout_sent, 64)
            for i in range(6):
                act.wait_ge(tok_ready, 2 * i + 1)
                nc.scalar.activation(htok_h[:, i // 2, 512 * (i % 2):512 * (i % 2) + 512],
                                     PS[0:TT, 3, :], ACT.Copy).then_inc(tokh_done, 1)
            act.wait_ge(route_dve, 1)
            nc.scalar.activation(rt[:, 60:66], rt[:, 54:60], ACT.Exp).then_inc(route_act, 1)
            act.wait_ge(routed, 1)
            n = act.value_load(passes[0:1, 0:1], min_val=1, max_val=3)
            with act.Fori(0, n) as ps:
                with act.Fori(0, NE) as e:
                    it = ps * NE + e
                    t0 = it * MOE_TURNS
                    act.wait_ge(gather_ready, it * 3 + 1)
                    for i in range(2):
                        nc.scalar.activation(gh[:, 512 * i:512 * i + 512], PS[:, 2 + i, :],
                                             ACT.Copy).then_inc(gh_done, 1)
                    act.wait_ge(gather_ready, it * 3 + 3)
                    nc.scalar.activation(selT, PS[:, 6, 0:T], ACT.Copy).then_inc(slot_taken, 1)

                    def gate(m):
                        act.wait_ge(g_ready, m + 1)
                        nc.scalar.activation(sgm, PS[:, 2, :], ACT.Sigmoid, scale=srg[:, 0:1]).then_inc(sg_done, 1)

                    def hi(m):
                        act.wait_ge(aT_ready, m + 1)
                        nc.scalar.activation(actT_h, PS[:, 4, :], ACT.Copy).then_inc(aTh_done, 1)

                    def full(c, turns, m):
                        for s in range(6):
                            cast(c + s + AHEAD, turns)
                            if s == 1:
                                act.wait_ge(gg_done, m)
                                gate(m)
                        hi(m)

                    for s in range(4):
                        cast(b + s + AHEAD, t0)
                        if s == 1:
                            act.wait_ge(slot_taken, it * 2 + 2)
                            gate(it * 7)
                    hi(it * 7)
                    full(b + 4, t0, it * 7 + 1)
                    with act.Fori(0, 5) as j:
                        full(b + 10, t0 + j, it * 7 + 2 + j)
                    for s in range(2):
                        cast(b + 40 + s + AHEAD, t0)
                    act.wait_ge(y_ready, it + 1)
                    act.wait_ge(sgate_done, it + 1)
                    for i in range(2):
                        nc.scalar.activation(yh[:, 512 * i:512 * i + 512], PS[:, i, :], ACT.Copy,
                                             scale=sgate[:, 0:1]).then_inc(yh_done, 1)
            turns = n * (NE * MOE_TURNS)
            split_x(5)
            ple_act(act, cast, root, split_x, 1, turns)


        @block.scalar
        def _(act):
            def cast(c, turns=0):
                if isinstance(turns, int) and turns == 0 and c >= NCHUNK:
                    return
                act.wait_ge(raw_landed[c % RAW], 16 * (c // RAW + 1) + 16 * turns)
                if not (isinstance(turns, int) and c + RAW * turns < CAST):
                    act.wait_ge(chunk_begun, RAW * turns + c - CAST + 2)
                nc.scalar.activation(whi[:, c % CAST, :], raw[:, c % RAW, :], ACT.Copy).then_inc(hi_done, 1)

            def split_x(norm, tiles=range(KT)):
                for j in tiles:
                    act.wait_ge(*x_at(norm, j))
                    nc.scalar.activation(xht[:, j, :], x[:, j, :], ACT.Copy,
                                         scale=vec[:, GAIN[norm] + j:GAIN[norm] + j + 1]).then_inc(xh_ready, 1)

            def root(norm):
                k = turn_of(norm)
                act.wait_ge(stat_ready, k + 1)
                if k > 0:
                    act.wait_ge(rstd_ready, k)
                nc.scalar.activation(sq_root[:, :], PS[:, 3, 0:T], ACT.Sqrt, bias=epsb[:, :],
                                     scale=1.0 / D).then_inc(root_ready, 1)

            act.wait_ge(in_con, 16)
            nc.scalar.activation(idr[:, :], ident, ACT.Copy).then_inc(idr_done, 1)
            act.wait_ge(eps_done, 1)
            cast(0)
            cast(1)
            act.wait_ge(tile_taken, 1)
            split_x(0)
            for j in range(4):
                act.wait_ge(tile_ready, 10 + j + 1)
                nc.scalar.activation(ph[:, j, :], PS[:, (10 + j) % RING, 0:T], ACT.Copy).then_inc(p_hi, 1)
            for l in range(DEPTH):
                b, t = CB[l], TB[l]
                mixn = NORM_OF["in", l]
                cast(b["in"] + AHEAD)
                root(mixn)
                for i in range(1, 14):
                    cast(b["in"] + i + AHEAD)
                act.wait_ge(a32, l + 1)
                nc.scalar.activation(fr[:, 0:4 * T], CHt, ACT.Copy).then_inc(a_hi, 1)
                for i in range(2):
                    cast(b["conv"] + i + AHEAD)
                act.wait_ge(cbT_ready, l + 1)
                if l > 0:
                    act.wait_ge(cout_sent, 32 * l)
                    act.wait_ge(so_sent, 16 * l)
                nc.scalar.activation(cout, PS[0:18, 3, 0:512], ACT.Copy).then_inc(cout_ready, 1)
                for h in range(NH):
                    r = 4 * l + h
                    act.wait_ge(kvT_ready, r + 1)
                    if h == 0:
                        act.wait_ge(rope_ready, 2 * l + 2)
                    nc.scalar.activation(ktok[:, 0:128], PS[:, 3, 0:128], ACT.Copy,
                                         scale=kd[:, 2 * h:2 * h + 1]).then_inc(ktok_ready, 1)
                    nc.scalar.activation(ktok[:, 128:256], PS[:, 3, 128:256], ACT.Copy,
                                         scale=kd[:, 2 * h + 1:2 * h + 2]).then_inc(ktok_ready, 1)
                    nc.scalar.activation(kss, PS[0:8, 3, 256:384], ACT.Copy, scale=float(DK ** -0.5)).then_inc(ktok_ready, 1)
                    act.wait_ge(o_ready, r + 1)
                    nc.scalar.activation(so[:, h, :], PS[:, 5, 384:512], ACT.Copy).then_inc(so_ready, 1)
                    nc.scalar.activation(Qt[:, h, :], PS[:, 5, 0:T], ACT.Copy).then_inc(o_taken, 1)
                act.wait_ge(tile_taken, t["in"] + 28)
                act.wait_ge(vtok_ready, 8 * l + 8)
                nc.scalar.activation(Vt, Gt, ACT.Sigmoid).then_inc(sg_ready, 1)
                act.wait_ge(var_ready, l + 1)
                nc.scalar.activation(rtmp, PS[:, 4:8, 0:T], ACT.Sqrt, bias=epsb[:, :]).then_inc(ort_ready, 1)
                act.wait_ge(r32, l + 1)
                nc.scalar.activation(fr[:, 0:4 * T], Qt, ACT.Copy).then_inc(r_hi, 1)
                for i in range(2):
                    cast(b["ret"] + i + AHEAD)
                for i in range(4):
                    cast(b["gate"] + 2 * i + AHEAD)
                    cast(b["gate"] + 2 * i + 1 + AHEAD)
                    for s in range(4):
                        n = 16 * l + 4 * i + s
                        act.wait_ge(tile_taken, t["gate"] + 4 * i + s + 1)
                        nc.scalar.activation(gt_in(n), gt_in(n), ACT.Sigmoid).then_inc(gsig, 1)
                    for s in range(2):
                        j = 2 * i + s
                        act.wait_ge(m32, 8 * l + j + 1)
                        nc.scalar.activation(frt[:, j, :], zt[:, 16 + j % 2, :], ACT.Copy).then_inc(m_hi, 1)
                for i in range(4):
                    cast(b["o"] + i + AHEAD)
                    split_x(NORM_OF["ffn", l], (2 * i, 2 * i + 1))
                if l == 0:
                    dense_act(act, cast, root, split_x)
                    ple_act(act, cast, root, split_x, 0)
                else:
                    moe_act(act, cast, root, split_x)
            root(6)
            for i in range(3):
                for hf in range(2):
                    act.wait_ge(finT_ready, 2 * i + hf + 1)
                    nc.scalar.activation(xtok[:, i, 512 * hf:512 * hf + 512],
                                         PS[0:TT, 4 + hf, :], ACT.Copy).then_inc(out_ready, 1)


        def dense_dve(dve, v, cast, recip, take, split_x):
            b, t = CB[0], TB[0]

            def pair(q, c, p, turns=0, first=False):
                gb, sb_, ub_, ab = ffn_tiles(q)
                cast(c + AHEAD, turns)
                if first:
                    recip(1)
                for s in range(2):
                    take(p + s, gb[:, s, :], rstd[:, :], turns12=12 * turns)
                cast(c + 1 + AHEAD, turns)
                for s in range(2):
                    take(p + 2 + s, ub_[:, s, :], rstd[:, :], turns12=12 * turns)

            def product(q, pos, p, turns=0):
                gb, sb_, ub_, ab = ffn_tiles(q)
                dve.wait_ge(f_silu, q + 1 + 3 * turns)
                dve.wait_ge(tile_taken, p + 4 + 12 * turns)
                v.tensor_tensor(ab, gb, ub_, ALU.mult).then_inc(f_act, 1)
                dve.wait_ge(f_act, q + 1 + 3 * turns)
                dve.wait_ge(f_hi, q + 1 + 3 * turns)
                v.tensor_tensor(frt[:, ds(turns * 6 + 14 + 2 * pos, 2), :], ab,
                                frt[:, ds(turns * 6 + 2 * pos, 2), :].bitcast(F32), ALU.subtract).then_inc(f_lo, 1)

            for hf in range(2):
                c0, t0 = b["ffn"] + 22 * hf, t[f"gu{hf}"]
                pair(7 * hf, c0, t0, first=(hf == 0))
                with dve.Fori(0, 2) as it:
                    for q in range(3):
                        pair(7 * hf + 1 + q, c0 + 2 + 2 * q, t0 + 4 + 4 * q, it)
                        product(7 * hf + q, q, t0 + 4 * q, it)
                product(7 * hf + 6, 6, t0 + 24)
                for i in range(8):
                    cast(c0 + 14 + i + AHEAD)
                    p = t[f"down{hf}"] + i
                    dve.wait_ge(tile_ready, p + 1)
                    v.tensor_tensor(x[:, i, :], PS[:, p % RING, 0:T], x[:, i, :], ALU.add).then_inc(tile_taken, 1)
                    dve.wait_ge(tile_taken, p + 1)
                    if hf == 1:
                        split_x(16, 2, i)


        def ple_dve(dve, v, cast, recip, take, split_x, l, turns=0):
            b, t = CB[l], TB[l]
            last = l == DEPTH - 1
            cast(b["pw"] + AHEAD, turns)
            for j in range(KT):
                p = t["pw"] + j
                dve.wait_ge(tile_ready, p + 1)
                v.tensor_copy(zt[:, j, :], PS[:, p % RING, 0:T]).then_inc(tile_taken, 1)
            for i in range(4):
                if not (last and i + 1 + AHEAD > 4):
                    cast(b["pg"] + i + AHEAD, turns)
                if i == 0:
                    recip(NORM_OF["ple", l])
                for s in range(2):
                    j = 2 * i + s
                    take(t["pg"] + j, zt[:, 8 + j, :], rstd[:, :])
                for s in range(2):
                    j = 2 * i + s
                    n = 8 * l + j
                    dve.wait_ge(psig, n + 1)
                    v.tensor_tensor(zt[:, j, :], zt[:, j, :], zt[:, 8 + j, :], ALU.mult).then_inc(pprod, 1)
                    dve.wait_ge(pprod, n + 1)
                    v.tensor_tensor(x[:, j, :], x[:, j, :], zt[:, j, :], ALU.add).then_inc(x_ready, 1)
                    dve.wait_ge(x_ready, n + 1)
            if not last:
                for j in range(KT):
                    split_x(24, 3, j)



        def moe_dve(dve, v, cast, recip, take, split_x, link, n_chain):
            b = CB[1]["ffn"]
            recip_cols = rt[:, 0:3]
            dve.wait_ge(wr_hi, 1)
            v.tensor_tensor(wrl[:, :], wrr[:, :], wrh[:, :].bitcast(F32), ALU.subtract).then_inc(wr_lo, 1)
            dve.wait_ge(route_act, 1)
            v.memset(rg[:, :, 1:2], 0.0).then_inc(dve_chain, 1)
            n_chain[0] += 1
            link(v.reciprocal(rg[:, :, 0], recip_cols))
            lg = rt[:, 3:27].rearrange("p (t e) -> p t e", t=3)
            top = rt[:, 27:51].rearrange("p (t e) -> p t e", t=3)
            dif = rt[:, 54:60].rearrange("p (t e) -> p t e", t=3)
            ex = rt[:, 60:66].rearrange("p (t e) -> p t e", t=3)
            idf = rt[:, 66:90].rearrange("p (t e) -> p t e", t=3)
            den, rden = rt[:, 90:93], rt[:, 93:96]
            gt = rt[:, 96:102].rearrange("p (t e) -> p t e", t=3)
            eq = rt[:, 102:150].rearrange("p (i t e) -> p i t e", i=2, t=3)
            mask = rt[:, 150:174].rearrange("p (t e) -> p t e", t=3)
            gm = rt[:, 174:222].rearrange("p (i t e) -> p i t e", i=2, t=3)
            cnt = rt[0:1, 222:232]
            link(v.tensor_tensor(lg, PS[0:TT, 7, 0:24].rearrange("p (t e) -> p t e", t=3),
                                 rg[:, :, 0:1].to_broadcast([TT, 3, 8]), ALU.mult))
            for i in range(3):
                v.max(top[:, i, :], lg[:, i, :]).then_inc(dve_chain, 1)
            n_chain[0] += 3
            dve.wait_ge(dve_chain, n_chain[0])
            for i in range(3):
                v.max_index(idx[:, i, :], top[:, i, :], lg[:, i, :]).then_inc(dve_chain, 1)
            n_chain[0] += 3
            v.tensor_tensor(dif, top[:, :, 0:2], top[:, :, 0:1].to_broadcast([TT, 3, 2]),
                            ALU.subtract).then_inc(route_dve, 1)
            dve.wait_ge(dve_chain, n_chain[0])
            link(v.tensor_copy(idf[:, :, :], idx[:, :, :]))
            for i in range(6):
                dve.wait_ge(tok_ready, 2 * i + 2)
                dve.wait_ge(tokh_done, i + 1)
                v.tensor_copy(htok_l[:, i // 2, 512 * (i % 2):512 * (i % 2) + 512],
                              PS[0:TT, 4, :]).then_inc(tokl_done, 1)
            dve.wait_ge(route_act, 2)
            link(v.tensor_tensor(den, ex[:, :, 0], ex[:, :, 1], ALU.add))
            link(v.reciprocal(rden, den))
            link(v.tensor_tensor(gt, ex, rden.unsqueeze(2).to_broadcast([TT, 3, 2]), ALU.mult))
            for i in range(2):
                link(v.tensor_tensor(eq[:, i], iota8.unsqueeze(1).to_broadcast([TT, 3, 8]),
                                     idf[:, :, i:i + 1].to_broadcast([TT, 3, 8]), ALU.is_equal))
                link(v.tensor_tensor(gm[:, i], eq[:, i], gt[:, :, i:i + 1].to_broadcast([TT, 3, 8]), ALU.mult))
            link(v.tensor_tensor(rg[:, :, 2:10], gm[:, 0], gm[:, 1], ALU.add))
            v.tensor_tensor(mask, eq[:, 0], eq[:, 1], ALU.add).then_inc(route_dve, 1)
            dve.wait_ge(route_dve, 2)
            dve.wait_ge(rank_ready, 1)
            link(v.tensor_scalar(posm[:, :, :], PS[0:TT, 7, 32:56].rearrange("p (t e) -> p t e", t=3),
                                 10000.0, None, ALU.add))
            link(v.tensor_tensor(posm[:, :, :], posm[:, :, :], mask, ALU.mult))
            v.tensor_scalar(posm[:, :, :], posm[:, :, :], -10000.0, None, ALU.add).then_inc(pass_done, 1)
            link(v.max(cnt[:, 0:8], PS[0:1, 7, 64:72]))
            link(v.tensor_scalar(cnt[:, 8:9], cnt[:, 0:1], 128.5, 1.0, ALU.is_gt, ALU.add))
            link(v.scalar_tensor_tensor(cnt[:, 9:10], cnt[:, 0:1], 256.5, cnt[:, 8:9], ALU.is_gt, ALU.add))
            v.tensor_copy(passes[:, :], cnt[:, 9:10]).then_inc(routed, 1)
            dve.wait_ge(routed, 1)
            n = dve.value_load(passes[0:1, 0:1], min_val=1, max_val=3)
            with dve.Fori(0, n) as ps:
                with dve.Fori(0, NE) as e:
                    it = ps * NE + e
                    t0 = it * MOE_TURNS
                    dve.wait_ge(pass_done, ps + 1)
                    for i in range(3):
                        v.tensor_scalar(sel[:, i, :], iota, posm[:, i, ds(e, 1)], None,
                                        ALU.is_equal).then_inc(sel_ready, 1)
                    dve.wait_ge(gather_ready, it * 3 + 2)
                    for i in range(2):
                        v.tensor_copy(gl[:, 512 * i:512 * i + 512], PS[:, 4 + i, :]).then_inc(gl_done, 1)
                    dve.wait_ge(gather_ready, it * 3 + 3)
                    v.tensor_copy(srg[:, :], PS[:, 7, 0:10]).then_inc(slot_taken, 1)
                    v.tensor_copy(sgate[:, :], PS[:, 7, ds(e + 2, 1)]).then_inc(sgate_done, 1)
                    dve.wait_ge(slot_taken, it * 2 + 2)

                    def gated(m):
                        dve.wait_ge(sg_done, m + 1)
                        v.scalar_tensor_tensor(ggm, PS[:, 2, :], srg[:, 0:1], sgm, ALU.mult, ALU.mult).then_inc(gg_done, 1)

                    def product(m):
                        dve.wait_ge(u_rdy, m + 1)
                        dve.wait_ge(gg_done, m + 1)
                        v.scalar_tensor_tensor(aam, PS[:, 3, :], srg[:, 0:1], ggm, ALU.mult, ALU.mult).then_inc(aa_done, 1)

                    def lo(m):
                        dve.wait_ge(aTh_done, m + 1)
                        v.tensor_tensor(actT_l, PS[:, 4, :], actT_h.bitcast(F32), ALU.subtract).then_inc(aTl_done, 1)

                    def full(c, turns, m):
                        for s in range(6):
                            cast(c + s + AHEAD, turns)
                            if s == 1:
                                gated(m)
                            if s == 3:
                                product(m)
                        lo(m)

                    for s in range(4):
                        cast(b + s + AHEAD, t0)
                        if s == 1:
                            gated(it * 7)
                    product(it * 7)
                    lo(it * 7)
                    full(b + 4, t0, it * 7 + 1)
                    with dve.Fori(0, 5) as j:
                        full(b + 10, t0 + j, it * 7 + 2 + j)
                    for s in range(2):
                        cast(b + 40 + s + AHEAD, t0)
                    for i in range(2):
                        dve.wait_ge(yh_done, it * 2 + i + 1)
                        v.scalar_tensor_tensor(yl[:, 512 * i:512 * i + 512], PS[:, i, :], sgate[:, 0:1],
                                               yh[:, 512 * i:512 * i + 512].bitcast(F32),
                                               ALU.mult, ALU.subtract).then_inc(yl_done, 1)
                    for j in range(KT):
                        dve.wait_ge(scat_ready, it * 8 + j + 1)
                        v.tensor_tensor(x[:, j, :], PS[:, 5 + j % 3, 0:T], x[:, j, :], ALU.add).then_inc(scat_taken, 1)
                v.tensor_scalar(posm[:, :, :], posm[:, :, :], -128.0, None, ALU.add).then_inc(pass_done, 1)
            turns = n * (NE * MOE_TURNS)
            dve.wait_ge(scat_taken, n * 64)
            dve.nop().then_inc(moe_done, 1)
            for j in range(KT):
                split_x(40, 5, j)
            ple_dve(dve, v, cast, recip, take, split_x, 1, turns)



        @block.vector
        def _(dve):
            v = nc.vector
            n_chain = [0]

            def link(ins):
                n_chain[0] += 1
                ins.then_inc(dve_chain, 1)
                dve.wait_ge(dve_chain, n_chain[0])

            def cast(c, turns=0):
                if isinstance(turns, int) and turns == 0 and c >= NCHUNK:
                    return
                dve.wait_ge(hi_done, RAW * turns + c + 1)
                v.tensor_tensor(wlo[:, c % CAST, :], raw[:, c % RAW, :],
                                whi[:, c % CAST, :].bitcast(F32), ALU.subtract).then_inc(lo_done, 1)

            def split_x(n8, norm, j):
                dve.wait_ge(xh_ready, n8 + j + 1)
                v.scalar_tensor_tensor(xlt[:, j, :], x[:, j, :], vec[:, GAIN[norm] + j:GAIN[norm] + j + 1],
                                       xht[:, j, :].bitcast(F32), ALU.mult, ALU.subtract).then_inc(xl_ready, 1)

            def recip(norm):
                k = turn_of(norm)
                dve.wait_ge(root_ready, k + 1)
                v.reciprocal(rstd[:, :], sq_root[:, :]).then_inc(rstd_ready, 1)
                dve.wait_ge(rstd_ready, k + 1)

            def take(p, dst, in1, op=ALU.mult, turns12=0):
                dve.wait_ge(tile_ready, p + 1 + turns12)
                v.tensor_tensor(dst, PS[:, p % RING, 0:T], in1, op).then_inc(tile_taken, 1)

            v.memset(epsb[:, :], EPS).then_inc(eps_done, 1)
            dve.wait_ge(tile_ready, 1)
            v.tensor_copy(vec[:, :], PS[:, 0, 0:80]).then_inc(tile_taken, 1)
            dve.wait_ge(tile_ready, 2)
            v.tensor_copy(cst[:, :, :, :].rearrange("p l k c -> p (l k c)"), PS[:, 1, 0:128]).then_inc(tile_taken, 1)
            cast(0)
            for j in range(KT):
                dve.wait_ge(tile_ready, 3 + j)
                v.tensor_copy(x[:, j, :], PS[:, (2 + j) % RING, 0:T]).then_inc(tile_taken, 1)
                dve.wait_ge(tile_taken, 3 + j)
            for j in range(KT):
                split_x(0, 0, j)
            cast(1)
            for j in range(4):
                dve.wait_ge(p_hi, j + 1)
                v.tensor_tensor(pl[:, j, :], PS[:, (10 + j) % RING, 0:T], ph[:, j, :].bitcast(F32),
                                ALU.subtract).then_inc(tile_taken, 1)

            for l in range(DEPTH):
                b, t = CB[l], TB[l]
                mixn = NORM_OF["in", l]

                def w_in(i):
                    cast(b["in"] + i + AHEAD)
                    if i == 0:
                        recip(mixn)
                    for s in range(2):
                        take(t["in"] + 2 * i + s, zt[:, 2 * i + s, :], rstd[:, :])

                def rope(X, n):
                    def tab(a, lo):
                        return a[lo:lo + 64, :].unsqueeze(1).to_broadcast([64, 4, T])
                    v.tensor_tensor(rtmp[0:64], X[64:128], tab(sin, 64), ALU.mult).then_inc(dve_chain, 1)
                    n_chain[0] += 1
                    link(v.tensor_tensor(rtmp[64:128], X[0:64], tab(sin, 0), ALU.mult))
                    link(v.tensor_tensor(X, X, cos.unsqueeze(1).to_broadcast([128, 4, T]), ALU.mult))
                    v.tensor_tensor(X, X, rtmp, ALU.add).then_inc(rope_ready, 1)
                    dve.wait_ge(rope_ready, n)

                for i in range(9):
                    w_in(i)
                dve.wait_ge(u_ready, 2 * l + 2)
                old = cst[:, l, :, :].rearrange("p k (b w) -> p k b w", w=2)
                for tap in (2, 1, 0):
                    for j in range(4):
                        w = vec[:, CONVW + 12 * l + 4 * tap + j:CONVW + 12 * l + 4 * tap + j + 1]
                        yp, ys = CCt[:, j, 0:SEQ], CCt[:, j, SEQ:T]
                        if tap == 2:
                            v.tensor_scalar(yp, ub[:, j, 2:2 + SEQ], w, None, ALU.mult).then_inc(dve_chain, 1)
                            ins = v.tensor_scalar(ys, us[:, j, :], w, None, ALU.mult)
                        else:
                            v.scalar_tensor_tensor(yp, ub[:, j, tap:tap + SEQ], w, yp, ALU.mult, ALU.add).then_inc(dve_chain, 1)
                            ins = v.scalar_tensor_tensor(ys, old[:, j, :, tap], w, ys, ALU.mult, ALU.add)
                        n_chain[0] += 2
                        ins.then_inc(dve_chain, 1)
                    dve.wait_ge(dve_chain, n_chain[0])
                dve.nop().then_inc(y_conv, 1)
                w_in(9)
                rope(Qt, 2 * l + 1)
                w_in(10)
                rope(Kt, 2 * l + 2)
                w_in(11)
                dve.wait_ge(a_hi, l + 1)
                v.tensor_tensor(fr[:, 4 * T:8 * T].rearrange("p (k t) -> p k t", k=4), CHt,
                                frt[:, 0:4, :].bitcast(F32), ALU.subtract).then_inc(a_lo, 1)
                w_in(12)
                w_in(13)
                for i in range(2):
                    cast(b["conv"] + i + AHEAD)
                    for s in range(4):
                        p = t["conv"] + 4 * i + s
                        dve.wait_ge(tile_ready, p + 1)
                        if s == 0 and i == 0:
                            dve.wait_ge(a32, l + 1)
                        v.tensor_copy(zt[:, 4 * i + s, :], PS[:, p % RING, 0:T]).then_inc(tile_taken, 1)
                for h in range(NH):
                    r = 4 * l + h
                    dve.wait_ge(kvT_ready, r + 1)
                    v.tensor_copy(vtok, PS[:, 6, 0:256]).then_inc(vtok_ready, 1)
                    dve.wait_ge(kvT_ready, r + 1)
                    v.tensor_tensor(vd, PS[0:8, 6, 256:384].unsqueeze(1).to_broadcast([8, 8, 128]),
                                    eye8.unsqueeze(2).to_broadcast([8, 8, 128]), ALU.mult).then_inc(vtok_ready, 1)
                    dve.wait_ge(score_ready, r + 1)
                    v.tensor_tensor(sc[:, 0:256], PS[:, 4, 0:256], dec[:, h, :], ALU.mult).then_inc(sc_ready, 1)
                    v.tensor_tensor(sc[:, 256:384], PS[:, 4, 256:384], dec[:, h, 0:128], ALU.mult).then_inc(sc_ready, 1)
                    dve.wait_ge(s_in[r % 2], 16 * (r // 2 + 1))
                    for hf in range(2):
                        dve.wait_ge(kv_outer, 2 * r + hf + 1)
                        S = St[r % 2][:, 512 * hf:512 * hf + 512]
                        v.scalar_tensor_tensor(S, S, float(np.float32(GAMMA[h])), PS[:, 7, :],
                                               ALU.mult, ALU.add).then_inc(s_new, 1)
                dve.wait_ge(mu_ready, l + 1)
                v.tensor_tensor(Qt, Qt, PS[:, 4:8, 0:T], ALU.subtract).then_inc(oc_ready, 1)
                dve.wait_ge(oc_ready, l + 1)
                dve.wait_ge(ort_ready, l + 1)
                link(v.reciprocal(rtmp, rtmp))
                link(v.tensor_tensor(Qt, Qt, rtmp, ALU.mult))
                dve.wait_ge(gsl_ready, l + 1)
                v.tensor_tensor(Qt, Qt, Gt, ALU.mult).then_inc(r32, 1)
                dve.wait_ge(r32, l + 1)
                dve.wait_ge(r_hi, l + 1)
                v.tensor_tensor(fr[:, 4 * T:8 * T].rearrange("p (k t) -> p k t", k=4), Qt,
                                frt[:, 0:4, :].bitcast(F32), ALU.subtract).then_inc(r_lo, 1)
                for i in range(2):
                    cast(b["ret"] + i + AHEAD)
                    for s in range(4):
                        p = t["ret"] + 4 * i + s
                        dve.wait_ge(tile_ready, p + 1)
                        if i == 0 and s == 0:
                            dve.wait_ge(r_lo, l + 1)
                        v.tensor_copy(zt[:, 8 + 4 * i + s, :], PS[:, p % RING, 0:T]).then_inc(tile_taken, 1)
                for i in range(4):
                    for s in range(4):
                        if s % 2 == 0:
                            cast(b["gate"] + 2 * i + s // 2 + AHEAD)
                        n = 16 * l + 4 * i + s
                        take(t["gate"] + 4 * i + s, gt_in(n), rstd[:, :])
                    for s in range(2):
                        j = 2 * i + s
                        n = 16 * l + 4 * i + s
                        dve.wait_ge(gsig, n + 3)
                        link(v.tensor_tensor(zt[:, j, :], zt[:, j, :], gt_in(n), ALU.mult))
                        link(v.tensor_tensor(zt[:, 8 + j, :], zt[:, 8 + j, :], gt_in(n + 2), ALU.mult))
                        if 8 * l + j >= 2:
                            dve.wait_ge(m_hi, 8 * l + j - 1)
                        v.tensor_tensor(zt[:, 16 + j % 2, :], zt[:, j, :], zt[:, 8 + j, :], ALU.add).then_inc(m32, 1)
                        dve.wait_ge(m32, 8 * l + j + 1)
                        dve.wait_ge(m_hi, 8 * l + j + 1)
                        v.tensor_tensor(frt[:, 8 + j, :], zt[:, 16 + j % 2, :], frt[:, j, :].bitcast(F32),
                                        ALU.subtract).then_inc(m_lo, 1)
                fn = NORM_OF["ffn", l]
                for i in range(4):
                    cast(b["o"] + i + AHEAD)
                    for j in (2 * i, 2 * i + 1):
                        p = t["o"] + j
                        dve.wait_ge(tile_ready, p + 1)
                        v.tensor_tensor(x[:, j, :], PS[:, p % RING, 0:T], x[:, j, :], ALU.add).then_inc(tile_taken, 1)
                        dve.wait_ge(tile_taken, p + 1)
                    for j in (2 * i, 2 * i + 1):
                        split_x(8 * (1 + 3 * l), fn, j)
                if l == 0:
                    dense_dve(dve, v, cast, recip, take, split_x)
                    ple_dve(dve, v, cast, recip, take, split_x, 0)
                else:
                    moe_dve(dve, v, cast, recip, take, split_x, link, n_chain)
            recip(6)
            for j in range(KT):
                g = vec[:, GAIN[6] + j:GAIN[6] + j + 1]
                v.scalar_tensor_tensor(x[:, j, :], x[:, j, :], g, rstd[:, :], ALU.mult, ALU.mult).then_inc(fin_ready, 1)


        def ple_pe(pe, chunk, stat, l, turns=0):
            b, t = CB[l], TB[l]
            chunk(b["pw"], t["pw"], 2, 8, ph[:, 2 * l:2 * l + 2, :], pl[:, 2 * l:2 * l + 2, :], turns=turns)
            for i in range(4):
                chunk(b["pg"] + i, t["pg"] + 2 * i, 8, 2, xht, xlt, turns=turns,
                      x8=({0: 16, 1: 40}[l] if i == 0 else None))
                if i == 0:
                    stat(NORM_OF["ple", l])


        def moe_pe(pe, ready, three, chunk, stat):
            mm = nc.tensor.matmul
            b = CB[1]["ffn"]
            pe.wait_ge(xl_ready, 40)
            pe.wait_ge(wr_lo, 1)
            pe.wait_ge(idr_done, 1)
            pe.wait_ge(tile_taken, TB[1]["pw"])
            for i in range(3):
                for k in range(KT):
                    cols = slice(TT * i, TT * i + TT)
                    three(PS[0:TT, 7, 8 * i:8 * i + 8], xht[:, k, cols], xlt[:, k, cols],
                          wrh[:, 8 * k:8 * k + 8], wrl[:, 8 * k:8 * k + 8], k == 0, k == KT - 1)
            pe.wait_ge(sq_ready, 5)
            for i in range(3):
                ins = mm(PS[0:TT, 7, 24 + i:25 + i], sacc[:, TT * i:TT * i + TT], ones[:, 0:1], start=True, stop=True)
            ins.then_inc(logit_ready, 1)
            for i in range(6):
                for (src, bank, done) in ((xht, 3, tokh_done), (xlt, 4, tokl_done)):
                    if i > 0:
                        pe.wait_ge(done, i)
                    for k in range(4):
                        ins = mm(PS[0:TT, bank, 128 * k:128 * k + 128],
                                 src[:, 4 * (i % 2) + k, TT * (i // 2):TT * (i // 2) + TT], idr[:, :],
                                 start=True, stop=True)
                    ins.then_inc(tok_ready, 1)
                if i == 0:
                    pass
            pe.wait_ge(route_dve, 2)
            mask = rt[:, 150:174].rearrange("p (t e) -> p t e", t=3)
            for i in range(3):
                for j in range(i + 1):
                    mm(PS[0:TT, 7, 32 + 8 * i:40 + 8 * i], tri if j == i else con[0:TT, C_ONE:C_ONE + TT],
                       mask[:, j, :], start=j == 0, stop=j == i)
            for j in range(3):
                ins = mm(PS[0:TT, 7, 64:72], con[0:TT, C_ONE:C_ONE + TT], mask[:, j, :], start=j == 0, stop=j == 2)
            ins.then_inc(rank_ready, 1)
            pe.wait_ge(routed, 1)
            pe.wait_ge(tokh_done, 6)
            n = pe.value_load(passes[0:1, 0:1], min_val=1, max_val=3)
            with pe.Fori(0, n) as ps:
                with pe.Fori(0, NE) as e:
                    it = ps * NE + e
                    t0 = it * MOE_TURNS
                    pe.wait_ge(sel_ready, it * 3 + 3)
                    for tok, bank in ((htok_h, 2), (htok_l, 4)):
                        for k in range(KT):
                            for i in range(3):
                                ins = mm(PS[:, bank + k // 4, 128 * (k % 4):128 * (k % 4) + 128],
                                         tok[:, i, 128 * k:128 * k + 128], sel[:, i, :],
                                         start=i == 0, stop=i == 2)
                        ins.then_inc(gather_ready, 1)
                    for i in range(3):
                        mm(PS[:, 6, TT * i:TT * i + TT], sel[:, i, :], idr[0:TT, 0:TT], start=True, stop=True)
                    for i in range(3):
                        ins = mm(PS[:, 7, 0:10], sel[:, i, :].bitcast(F32), rg[:, i, :], start=i == 0, stop=i == 2)
                    ins.then_inc(gather_ready, 1)
                    pe.wait_ge(gh_done, it * 2 + 2)
                    pe.wait_ge(gl_done, it * 2 + 2)
                    pe.wait_ge(slot_taken, it * 2 + 2)
                    pe.wait_ge(sgate_done, it + 1)

                    def up(c, bank, turns, sem_):
                        for s in range(2):
                            ready(c + s, turns)
                            for k in range(4):
                                kk = 4 * s + k
                                wh = whi[:, (c + s) % CAST, 512 * k:512 * k + 512]
                                wl = wlo[:, (c + s) % CAST, 512 * k:512 * k + 512]
                                ins = mm(PS[:, bank, :], gh[:, 128 * kk:128 * kk + 128], wh, start=kk == 0, stop=False)
                                if k == 0:
                                    ins.then_inc(chunk_begun, 1)
                                mm(PS[:, bank, :], gh[:, 128 * kk:128 * kk + 128], wl, start=False, stop=False)
                                ins = mm(PS[:, bank, :], gl[:, 128 * kk:128 * kk + 128], wh, start=False, stop=kk == 7)
                        ins.then_inc(sem_, 1)

                    def down(c, turns, first, last):
                        for s in range(2):
                            ready(c + s, turns)
                            for k in range(2):
                                kk = 2 * s + k
                                ah = actT_h[:, 128 * kk:128 * kk + 128]
                                al = actT_l[:, 128 * kk:128 * kk + 128]
                                for h in range(2):
                                    at = 1024 * k + 512 * h
                                    wh, wl = whi[:, (c + s) % CAST, at:at + 512], wlo[:, (c + s) % CAST, at:at + 512]
                                    ins = mm(PS[:, h, :], ah, wh, start=first and kk == 0, stop=False)
                                    if k == 0 and h == 0:
                                        ins.then_inc(chunk_begun, 1)
                                    mm(PS[:, h, :], ah, wl, start=False, stop=False)
                                    ins = mm(PS[:, h, :], al, wh, start=False, stop=last and kk == 3)
                        if last:
                            ins.then_inc(y_ready, 1)

                    def turn(m):
                        pe.wait_ge(aa_done, m + 1)
                        for k in range(4):
                            ins = nc.tensor.transpose(PS[:, 4, 128 * k:128 * k + 128], aam[:, 128 * k:128 * k + 128], ident)
                        ins.then_inc(aT_ready, 1)

                    def full(c, turns, m, first):
                        pe.wait_ge(gg_done, m)
                        up(c, 2, turns, g_ready)
                        pe.wait_ge(aa_done, m)
                        up(c + 2, 3, turns, u_rdy)
                        pe.wait_ge(aTl_done, m)
                        down(c + 4, turns, first, False)
                        turn(m)

                    up(b, 2, t0, g_ready)
                    up(b + 2, 3, t0, u_rdy)
                    turn(it * 7)
                    full(b + 4, t0, it * 7 + 1, True)
                    with pe.Fori(0, 5) as j:
                        full(b + 10, t0 + j, it * 7 + 2 + j, False)
                    pe.wait_ge(aTl_done, it * 7 + 7)
                    down(b + 40, t0, False, True)
                    pe.wait_ge(yl_done, it * 2 + 2)
                    for j in range(KT):
                        if j >= 3:
                            pe.wait_ge(scat_taken, it * 8 + j - 2)
                        mm(PS[:, 5 + j % 3, 0:T], yh[:, 128 * j:128 * j + 128], selT, start=True, stop=False)
                        mm(PS[:, 5 + j % 3, 0:T], yl[:, 128 * j:128 * j + 128], selT, start=False, stop=True).then_inc(scat_ready, 1)
                    pe.wait_ge(scat_taken, it * 8 + 8)
            pe.wait_ge(moe_done, 1)
            ple_pe(pe, chunk, stat, 1, n * (NE * MOE_TURNS))


        @block.tensor
        def _(pe):
            mm = nc.tensor.matmul

            def ready(c, turns=0):
                pe.wait_ge(lo_done, RAW * turns + c + 1)

            def free(p, turns12=0):
                if p >= RING:
                    pe.wait_ge(tile_taken, p - RING + 1 + turns12)
                return PS[:, p % RING, 0:T]

            def three(out, wh, wl, ah, al, first, last, begins=False):
                ins = mm(out, wh, ah, start=first, stop=False)
                if begins:
                    ins.then_inc(chunk_begun, 1)
                mm(out, wh, al, start=False, stop=False)
                return mm(out, wl, ah, start=False, stop=last)

            def chunk(c, p, nk, nt, ah, al, turns=0, turns12=0, x8=None):
                ready(c, turns)
                W = nt * 128
                for n in range(nt):
                    out = free(p + n, turns12)
                    for k in range(nk):
                        if x8 is not None and n == 0:
                            pe.wait_ge(xl_ready, x8 + k + 1)
                        at = k * W + n * 128
                        ins = three(out, whi[:, c % CAST, at:at + 128], wlo[:, c % CAST, at:at + 128],
                                    ah[:, k, :], al[:, k, :], k == 0, k == nk - 1, n == 0 and k == 0)
                    ins.then_inc(tile_ready, 1)

            def stat(norm):
                pe.wait_ge(sq_ready, norm + 1)
                if norm > 0:
                    pe.wait_ge(root_ready, turn_of(norm))
                mm(PS[:, 3, 0:T], ones, sacc[:, :], start=True, stop=True).then_inc(stat_ready, 1)

            pe.wait_ge(in_con, 16)
            pe.wait_ge(in_misc, 160)
            nc.tensor.transpose(PS[:, 0, 0:80], vrow, con[0:80, C_ID:C_ID + 80]).then_inc(tile_ready, 1)
            for l in range(DEPTH):
                for k in range(4):
                    ins = nc.tensor.transpose(PS[:, 1, (4 * l + k) * 16:(4 * l + k) * 16 + 16],
                                              crow[:, l, 128 * k:128 * k + 128], con[0:16, C_ID:C_ID + 16])
            ins.then_inc(tile_ready, 1)
            pe.wait_ge(in_x, 48)
            for j in range(KT):
                out = free(2 + j)
                for i in range(3):
                    ins = nc.tensor.transpose(out[:, TT * i:TT * i + TT], xtok[:, i, 128 * j:128 * j + 128],
                                              con[0:TT, C_ID:C_ID + TT])
                ins.then_inc(tile_ready, 1)
            for j in range(4):
                out = free(10 + j)
                for i in range(3):
                    ins = nc.tensor.transpose(out[:, TT * i:TT * i + TT], ptok[:, i, 128 * j:128 * j + 128],
                                              con[0:TT, C_ID:C_ID + TT])
                ins.then_inc(tile_ready, 1)

            n_x = 0
            for l in range(DEPTH):
                b, t = CB[l], TB[l]
                x8 = {0: 0, 1: 24}[l]
                chunk(b["in"], t["in"], 8, 2, xht, xlt, x8=x8)
                stat(NORM_OF["in", l])
                chunk(b["in"] + 1, t["in"] + 2, 8, 2, xht, xlt)
                with pe.Fori(0, 2) as it:
                    for s in range(6):
                        chunk(b["in"] + 2 + s, t["in"] + 4 + 2 * s, 8, 2, xht, xlt, turns=it, turns12=12 * it)
                pe.wait_ge(root_ready, turn_of(NORM_OF["in", l]) + 1)
                pe.wait_ge(cbt_ready, l + 1)
                for k in range(4):
                    ins = nc.tensor.transpose(PS[0:18, 3, 128 * k:128 * k + 128], cbt[:, k, :], ident)
                ins.then_inc(cbT_ready, 1)
                pe.wait_ge(a_lo, l + 1)
                for i in range(2):
                    chunk(b["conv"] + i, t["conv"] + 4 * i, 4, 4, frt[:, 0:4, :], frt[:, 4:8, :])
                pe.wait_ge(rope_ready, 2 * l + 2)
                pe.wait_ge(tile_taken, t["in"] + 28)
                for h in range(NH):
                    r = 4 * l + h
                    if h == 0:
                        pe.wait_ge(cout_ready, l + 1)
                    else:
                        pe.wait_ge(ktok_ready, 3 * r)
                        pe.wait_ge(vtok_ready, 2 * r)
                        pe.wait_ge(so_ready, r)
                    for i in range(2):
                        nc.tensor.transpose(PS[:, 3, 128 * i:128 * i + 128], Kt[:, h, 128 * i:128 * i + 128], ident)
                        nc.tensor.transpose(PS[:, 6, 128 * i:128 * i + 128], Vt[:, h, 128 * i:128 * i + 128], ident)
                    nc.tensor.transpose(PS[0:8, 3, 256:384], Kt[:, h, SEQ:T], ident)
                    nc.tensor.transpose(PS[0:8, 6, 256:384], Vt[:, h, SEQ:T], ident).then_inc(kvT_ready, 1)
                    if h > 0:
                        pe.wait_ge(sc_ready, 2 * r)
                    mm(PS[:, 4, 0:256], Kt[:, h, 0:128], Qt[:, h, 0:256], start=True, stop=True)
                    mm(PS[:, 4, 256:384], Kt[:, h, 128:256], Qt[:, h, 128:256], start=True, stop=True).then_inc(score_ready, 1)
                    pe.wait_ge(ktok_ready, 3 * r + 3)
                    pe.wait_ge(vtok_ready, 2 * r + 2)
                    for hf in range(2):
                        if 2 * r + hf > 0:
                            pe.wait_ge(s_new, 2 * r + hf)
                        mm(PS[:, 7, :].rearrange("p (b e) -> p b e", b=4), kss, vd[:, 4 * hf:4 * hf + 4, :],
                           start=True, stop=True).then_inc(kv_outer, 1)
                    if r > 0:
                        pe.wait_ge(o_taken, r)
                    for i in range(2):
                        mm(PS[:, 5, 384:512], ktok[:, 128 * i:128 * i + 128], vtok[:, 128 * i:128 * i + 128],
                           start=i == 0, stop=i == 1)
                    pe.wait_ge(sc_ready, 2 * r + 2)
                    mm(PS[:, 5, 0:256], vtok[:, 0:128], sc[:, 0:256], start=True, stop=False, skip_group_check=True)
                    mm(PS[:, 5, 128:256], vtok[:, 128:256], sc[:, 256:384], start=False, stop=True, skip_group_check=True)
                    pe.wait_ge(s_new, 2 * r + 2)
                    for i in range(NB):
                        ins = mm(PS[:, 5, SEQ + i:SEQ + i + 1], St[r % 2][:, 128 * i:128 * i + 128],
                                 Qt[:, h, SEQ + i:SEQ + i + 1], start=True, stop=True, skip_group_check=True)
                    ins.then_inc(o_ready, 1)
                pe.wait_ge(o_taken, 4 * l + 4)
                pe.wait_ge(so_ready, 4 * l + 4)
                for h in range(NH):
                    ins = mm(PS[:, 4 + h, 0:T], mean, Qt[:, h, :], start=True, stop=True)
                ins.then_inc(mu_ready, 1)
                pe.wait_ge(osq_ready, l + 1)
                for h in range(NH):
                    ins = mm(PS[:, 4 + h, 0:T], mean, rtmp[:, h, :], start=True, stop=True)
                ins.then_inc(var_ready, 1)
                pe.wait_ge(r_lo, l + 1)
                for i in range(2):
                    chunk(b["ret"] + i, t["ret"] + 4 * i, 4, 4, frt[:, 0:4, :], frt[:, 4:8, :])
                for i in range(8):
                    chunk(b["gate"] + i, t["gate"] + 2 * i, 8, 2, xht, xlt)
                pe.wait_ge(m_lo, 8 * l + 8)
                for i in range(4):
                    chunk(b["o"] + i, t["o"] + 2 * i, 8, 2, frt[:, 0:8, :], frt[:, 8:16, :])
                if l == 0:
                    for hf in range(2):
                        c0, t0 = b["ffn"] + 22 * hf, t[f"gu{hf}"]
                        if hf == 0:
                            chunk(c0, t0, 8, 2, xht, xlt, x8=8)
                            stat(1)
                        else:
                            chunk(c0, t0, 8, 2, xht, xlt)
                        chunk(c0 + 1, t0 + 2, 8, 2, xht, xlt)
                        with pe.Fori(0, 2) as it:
                            for s in range(6):
                                chunk(c0 + 2 + s, t0 + 4 + 2 * s, 8, 2, xht, xlt, turns=it, turns12=12 * it)
                        pe.wait_ge(f_lo, 7 * hf + 7)
                        for i in range(8):
                            chunk(c0 + 14 + i, t[f"down{hf}"] + i, 14, 1, frt[:, 0:14, :], frt[:, 14:28, :])
                    ple_pe(pe, chunk, stat, 0)
                else:
                    moe_pe(pe, ready, three, chunk, stat)
            stat(6)
            pe.wait_ge(fin_ready, 8)
            for i in range(3):
                for hf in range(2):
                    if i > 0:
                        pe.wait_ge(out_ready, 2 * i + hf - 1)
                    for k in range(4):
                        ins = nc.tensor.transpose(PS[0:TT, 4 + hf, 128 * k:128 * k + 128],
                                                  x[:, 4 * hf + k, TT * i:TT * i + TT], ident)
                    ins.then_inc(finT_ready, 1)


_INS = ["x_prompt", "x_sample", "state_conv", "state_ret", "p_prompt", "p_sample", "norm_mix_g", "w_in",
        "conv_w", "w_conv_out", "w_ret_out", "w_o", "norm_ffn_g", "w_dense_gu", "w_dense_down",
        "w_router", "w_exp_gu", "w_exp_down", "norm_ple_g", "w_ple", "w_ple_gate", "norm_final_g"]
_OUTS = [("y_prompt", (1, SEQ, D)), ("y_sample", (NB, 1, D)), ("conv_prompt", (DEPTH, 1, CW - 1, DC)),
         ("ret_prompt", (DEPTH, 1, NH, DK, DK)), ("conv_sample", (DEPTH, NB, CW - 1, DC)),
         ("ret_sample", (DEPTH, NB, NH, DK, DK))]


def kernel(**inputs):
    import concourse.bacc as bacc
    from concourse.bass_utils import run_bass_kernel_spmd

    nc = bacc.Bacc("TRN2", target_bir_lowering=False, num_devices=1)
    arrays, A, O = {}, {}, {}
    given = {name: np.ascontiguousarray(inputs[name]) for name in _INS}
    given["constants"] = constants()
    for name, a in given.items():
        arrays[f"in_{name}"] = a
        A[name] = nc.dram_tensor(f"in_{name}", a.shape, mybir.dt.from_np(a.dtype), kind="ExternalInput").ap()
    for name, shape in _OUTS:
        O[name] = nc.dram_tensor(f"out_{name}", shape, mybir.dt.float32, kind="ExternalOutput").ap()
    program(nc, A, O)
    r = run_bass_kernel_spmd(nc, [arrays], core_ids=[0])
    return tuple(r.results[0][f"out_{name}"] for name, _ in _OUTS)
```

```python
import math

import numpy as np
import concourse.bass as bass
from concourse import mybir
from contextlib import ExitStack

D = 1024
SEQ = 256
NB = 8
T = SEQ + NB
KT = D // 128
DC = 512
NH = 4
DK = 128
DR = NH * DK
DFF = 3584
NE = 8
DPLE = 256
DEPTH = 2
CW = 3
NIN = 3 * DC + 4 * DR + 2 * D
EPS = 1e-6
PAST = 2048
TT = 88
CH = 2048
RAW, CAST = 6, 3
AHEAD = 2
RING = 3

C_ID, C_ONE, C_CENT = 0, 128, 256
C_COS, C_SIN = 384, 384 + T
C_DEC = C_SIN + T
C_KD = C_DEC + NH * SEQ
C_EYE8 = C_KD + NH * 2
C_IOTA = C_EYE8 + 8
C_TRI = C_IOTA + 128
NCONST = C_TRI + TT

GAMMA = [1.0 - 2.0 ** (-5.0 - h) for h in range(NH)]


def constants():
    c = np.zeros((128, NCONST), np.float32)
    c[:, C_ID:C_ID + 128] = np.eye(128)
    c[:, C_ONE:C_ONE + 128] = 1.0
    c[:, C_CENT:C_CENT + 128] = np.eye(128) - 1.0 / DK
    half = DK // 2
    inv = np.float32(10000.0) ** (-np.arange(half, dtype=np.float32) / np.float32(half))
    pos = np.concatenate([np.arange(SEQ), np.full(NB, PAST)]).astype(np.float32)
    ang = (pos[None, :] * inv[:, None]).astype(np.float32).astype(np.float64)
    c[:half, C_COS:C_COS + T] = np.cos(ang)
    c[half:, C_COS:C_COS + T] = np.cos(ang)
    c[:half, C_SIN:C_SIN + T] = np.sin(ang)
    c[half:, C_SIN:C_SIN + T] = -np.sin(ang)
    m = np.arange(128)[:, None]
    l = np.arange(SEQ)[None, :]
    s = DK ** -0.5
    for h in range(NH):
        lg = float(np.log(np.float32(GAMMA[h])))
        d = np.where(l >= m, np.exp(np.maximum(l - m, 0) * lg), 0.0) * s
        c[:, C_DEC + h * SEQ:C_DEC + (h + 1) * SEQ] = d
        for i in range(2):
            c[:, C_KD + 2 * h + i] = np.exp((SEQ - 1 - 128 * i - m[:, 0]) * lg) * s
    c[:8, C_EYE8:C_EYE8 + 8] = np.eye(8)
    c[:, C_IOTA:C_IOTA + 128] = np.arange(128)[None, :]
    t = np.arange(TT)
    c[:TT, C_TRI:C_TRI + TT] = (t[:, None] < t[None, :])
    return c


def chunk_bases():
    b, at = [], 0
    for l in range(DEPTH):
        s = {}
        for name, n in (("in", 14), ("conv", 2), ("gate", 8), ("ret", 2), ("o", 4)):
            s[name] = at
            at += n
        if l == 0:
            s["ffn"] = at
            s["pw"], s["pg"] = at + 44, at + 45
            at += 49
        else:
            s["pw"], s["ffn"], s["pg"] = at, at + 1, at + 1
        b.append(s)
    return b


CB = chunk_bases()
NCHUNK = CB[1]["pg"] + 4
MOE_CHUNKS = 42
MOE_TURNS = MOE_CHUNKS // RAW
SLOTS = 10
ITEMS = 3 * NE


def tile_bases():
    b, at = [], 14
    for l in range(DEPTH):
        s = {}
        rows = [("in", 28), ("conv", 8), ("gate", 16), ("ret", 8), ("o", 8)]
        if l == 0:
            rows += [("gu0", 28), ("down0", 8), ("gu1", 28), ("down1", 8)]
        for name, n in rows + [("pw", 8), ("pg", 8)]:
            s[name] = at
            at += n
        b.append(s)
    return b


TB = tile_bases()
NORM_OF = {("in", 0): 0, ("ffn", 0): 1, ("ple", 0): 2, ("in", 1): 3, ("ffn", 1): 4, ("ple", 1): 5}
GAIN = {0: 0, 3: 8, 1: 16, 4: 24, 2: 32, 5: 40, 6: 48}
CONVW = 56


def program(nc, A, O):
    F32, F32R, I32, U32 = mybir.dt.float32, mybir.dt.float32r, mybir.dt.int32, mybir.dt.uint32
    ALU, ACT, AX = mybir.AluOpType, mybir.ActivationFunctionType, mybir.AxisListType
    ds = bass.ds
    es = ExitStack()
    with es:
        def sb(name, shape, dt=F32):
            return es.enter_context(nc.sbuf_tensor(name, shape, dt))

        def sem(name):
            return es.enter_context(nc.semaphore(name))

        raw = sb("raw", [128, RAW, CH])
        whi = sb("whi", [128, CAST, CH], F32R)
        wlo = sb("wlo", [128, CAST, CH], F32R)
        x = sb("x", [128, KT, T])
        xh = sb("xh", [128, KT * T], F32R)
        xl = sb("xl", [128, KT * T], F32R)
        z = sb("z", [128, 28 * T])
        con = sb("con", [128, NCONST])
        idr = sb("idr", [128, 128], F32R)
        vec = sb("vec", [128, 80])
        cst = sb("cst", [128, DEPTH, 4, 16])
        ph = sb("ph", [128, 4, T], F32R)
        pl = sb("pl", [128, 4, T], F32R)
        ub = sb("ub", [128, 4, 2 + SEQ])
        us = sb("us", [128, 4, NB])
        cbt = sb("cbt", [128, 4, 18])
        rstd = sb("rstd", [128, T])
        sq = sb("sq", [128, T])
        sacc = sb("sacc", [128, T])
        FR = 28 * T
        fr_at = nc.sbuf_usable_end - FR * 4
        fr_at -= fr_at % 32
        fr = nc.alloc_sbuf_tensor_at("fr", [128, FR], F32R, offset=fr_at)
        scr = nc.alloc_sbuf_tensor_at("scr", [128, 20 * T], F32, offset=fr_at + 8 * T * 4)
        PS = es.enter_context(nc.psum_tensor("PS", [128, 8, 512], F32))

        ident = con[:, C_ID:C_ID + 128]
        ones = con[:, C_ONE:C_ONE + 128]
        centre = con[:, C_CENT:C_CENT + 128]
        cos = con[:, C_COS:C_COS + T]
        sin = con[:, C_SIN:C_SIN + T]
        dec = con[:, C_DEC:C_DEC + NH * SEQ].rearrange("p (h l) -> p h l", h=NH)
        kd = con[:, C_KD:C_KD + 8]
        eye8 = con[0:8, C_EYE8:C_EYE8 + 8]
        iota = con[0:TT, C_IOTA:C_IOTA + 128]
        iota8 = con[0:TT, C_IOTA:C_IOTA + 8]
        tri = con[0:TT, C_TRI:C_TRI + TT]

        zt = z[:, :].rearrange("p (t c) -> p t c", c=T)
        frt = fr[:, :].rearrange("p (t c) -> p t c", c=T)
        xht = xh[:, :].rearrange("p (t c) -> p t c", c=T)
        xlt = xl[:, :].rearrange("p (t c) -> p t c", c=T)
        xtok = z[0:TT, 0:3 * D].rearrange("p (t f) -> p t f", t=3)
        ptok = z[0:TT, 3 * D:3 * D + 3 * 512].rearrange("p (t f) -> p t f", t=3)
        vrow = z[0:80, 4608:4736]
        crow = z[0:16, 4736:4736 + 1024].rearrange("p (l f) -> p l f", l=DEPTH)
        CBt, CCt, CHt = zt[:, 0:4, :], zt[:, 4:8, :], zt[:, 8:12, :]
        Qt, Kt, Vt, Gt = zt[:, 12:16, :], zt[:, 16:20, :], zt[:, 20:24, :], zt[:, 24:28, :]
        rtmp = scr[:, 0:4 * T].rearrange("p (h t) -> p h t", h=4)
        ktok, vtok = scr[:, 0:256], scr[:, 256:512]
        sc = scr[:, 512:896]
        vd = scr[0:8, 896:1920].rearrange("p (b e) -> p b e", b=8)
        kss = scr[0:8, 1920:2048]
        St = [scr[:, 2112 + 1024 * i:3136 + 1024 * i] for i in range(2)]
        so = scr[:, 4160:4672].rearrange("p (h e) -> p h e", h=4)
        cout = scr[0:18, 4672:5184]
        diag = scr[0:TT, 1056:2112].rearrange("p (n c) -> p n c", c=TT)
        gstat = sb("gstat", [TT, 2, 12])
        htok_h = fr[0:TT, 0:3072].rearrange("p (t f) -> p t f", t=3)
        htok_l = fr[0:TT, 3072:6144].rearrange("p (t f) -> p t f", t=3)
        actT_h, actT_l = fr[:, 6144:6656], fr[:, 6656:7168]
        gh, gl = xh[:, 0:D], xl[:, 0:D]
        yh, yl = xh[:, D:2 * D], xl[:, D:2 * D]
        sel = ph[0:TT, 0:2, :].rearrange("p a t -> p (a t)")[:, 0:384].rearrange("p (i s) -> p i s", i=3)
        selT = pl[:, 0, :]
        sgm, aam = z[:, 0:512], z[:, 512:1024]
        wrr = sb("wrr", [128, 64])
        rt = z[0:TT, 1600:2200]
        wrh = sb("wrh", [128, 64], F32R)
        wrl = sb("wrl", [128, 64], F32R)
        posm = sb("posm", [TT, 3, ITEMS + 1])
        rg = sb("rg", [TT, 3, 2 + ITEMS])
        srs = sb("srs", [128, 1])
        passes = sb("passes", [1, 2], I32)
        idx = sb("idx", [TT, 3, 8], U32)

        raw_landed = [sem(f"raw_landed{i}") for i in range(RAW)]
        hi_done, lo_done, chunk_begun = sem("hi_done"), sem("lo_done"), sem("chunk_begun")
        in_con, in_x, in_misc, in_wr = sem("in_con"), sem("in_x"), sem("in_misc"), sem("in_wr")
        tile_ready, tile_taken = sem("tile_ready"), sem("tile_taken")
        idr_done, pad_done = sem("idr_done"), sem("pad_done")
        p_hi = sem("p_hi")
        x_ready, xh_ready, xl_ready = sem("x_ready"), sem("xh_ready"), sem("xl_ready")
        pool_chain, dve_chain = sem("pool_chain"), sem("dve_chain")
        sq_ready, stat_ready, root_ready, rstd_ready = (sem("sq_ready"), sem("stat_ready"),
                                                        sem("root_ready"), sem("rstd_ready"))
        u_ready, y_conv, a32, a_hi, a_lo = (sem("u_ready"), sem("y_conv"), sem("a32"), sem("a_hi"),
                                            sem("a_lo"))
        cbt_ready, cbT_ready, cout_ready, cout_sent = (sem("cbt_ready"), sem("cbT_ready"),
                                                       sem("cout_ready"), sem("cout_sent"))
        rope_ready, bank3_ready, vT_ready, ktok_ready, vtok_ready = (
            sem("rope_ready"), sem("bank3_ready"), sem("vT_ready"), sem("ktok_ready"), sem("vtok_ready"))
        score_ready, sc_ready, so_ready, so_sent = (
            sem("score_ready"), sem("sc_ready"), sem("so_ready"), sem("so_sent"))
        kv_outer, s_new = sem("kv_outer"), sem("s_new")
        s_in = [sem("s_in0"), sem("s_in1")]
        s_sent = [sem("s_sent0"), sem("s_sent1")]
        o_ready, o_taken, os_taken, cent_ready, oc_ready, osq_ready, og_ready = (
            sem("o_ready"), sem("o_taken"), sem("os_taken"), sem("cent_ready"), sem("oc_ready"),
            sem("osq_ready"), sem("og_ready"))
        var_ready, groot_ready, diag_ready, rsb_ready = (
            sem("var_ready"), sem("groot_ready"), sem("diag_ready"), sem("rsb_ready"))
        gsilu_ready, r32, r_hi, r_lo = sem("gsilu_ready"), sem("r32"), sem("r_hi"), sem("r_lo")
        gsig, a_gated, m32, m_hi, m_lo = sem("gsig"), sem("a_gated"), sem("m32"), sem("m_hi"), sem("m_lo")
        f_silu, f_act, f_hi, f_lo = sem("f_silu"), sem("f_act"), sem("f_hi"), sem("f_lo")
        psig = sem("psig")
        wr_hi, wr_lo = sem("wr_hi"), sem("wr_lo")
        tok_ready, tokh_done, tokl_done = sem("tok_ready"), sem("tokh_done"), sem("tokl_done")
        logit_ready, route_act, route_dve, rank_ready, routed = (
            sem("logit_ready"), sem("route_act"), sem("route_dve"), sem("rank_ready"), sem("routed"))
        sel_ready, gath_hi, gath_lo, gh_done, gl_done = (
            sem("sel_ready"), sem("gath_hi"), sem("gath_lo"), sem("gh_done"), sem("gl_done"))
        table_ready, slot_rs, slot_gate, selT_ready, selT_done = (
            sem("table_ready"), sem("slot_rs"), sem("slot_gate"), sem("selT_ready"), sem("selT_done"))
        g_ready, u_rdy, sg_done, aa_done = (sem("g_ready"), sem("u_rdy"), sem("sg_done"), sem("aa_done"))
        aT_ready, aTh_done, aTl_done = sem("aT_ready"), sem("aTh_done"), sem("aTl_done")
        y_ready, yh_done, yl_done = sem("y_ready"), sem("yh_done"), sem("yl_done")
        scat_ready, scat_taken, moe_done = sem("scat_ready"), sem("scat_taken"), sem("moe_done")
        fin_ready, finT_ready, out_ready, out_sent = (sem("fin_ready"), sem("finT_ready"),
                                                      sem("out_ready"), sem("out_sent"))

        sq_root = sb("sq_root", [128, T])
        nwt = sb("nwt", [128, T])
        epsb = sb("epsb", [128, 1])
        sgate = sb("sgate", [128, 1])
        eps_done, pprod = sem("eps_done"), sem("pprod")
        ms_ready = sem("ms_ready")

        def x_at(norm, j):
            if norm == 5:
                return moe_done, 1
            if norm in (3, 6):
                return x_ready, 8 * (norm // 3 - 1) + j + 1
            base = {0: 2, 1: TB[0]["o"], 2: TB[0]["down1"], 4: TB[1]["o"]}[norm]
            return tile_taken, base + j + 1

        def turn_of(norm):
            return norm if norm < 4 else norm - 1

        assert nc.sbuf_base <= fr_at, (nc.sbuf_base, fr_at)
        block = es.enter_context(nc.Block())

        def ple_loads(sp, load, rows, l, turns):
            b = CB[l]
            if l == 0:
                load(b["pw"], rows(A["w_ple"][l], 2), turns)
            for i in range(4):
                load(b["pg"] + i, rows(A["w_ple_gate"][l], 8)[:, :, 256 * i:256 * i + 256], turns)


        def moe_loads(sp, load, ps):
            b = CB[1]["ffn"]
            gu = A["w_exp_gu"].rearrange("o e (k p) n -> (o e) p k n", p=128)
            dn = A["w_exp_down"].rearrange("o e (k p) n -> (o e) p k n", p=128)
            with sp.Fori(0, NE) as e:
                t0 = (ps * NE + e) * MOE_TURNS

                def up(c, s, j, turns):
                    col = (s // 2) * DFF
                    src = gu[ds(e, 1), :, 4 * (s % 2):4 * (s % 2) + 4, ds(j * 512 + col, 512)]
                    load(c, src.rearrange("o p k n -> (o p) k n"), turns)

                def down(c, s, j, turns):
                    src = dn[ds(e, 1), :, ds(j * 4 + 2 * s, 2), :]
                    load(c, src.rearrange("o p k n -> (o p) k n"), turns)

                for s in range(4):
                    up(b + s, s, 0, t0)
                with sp.Fori(0, 6) as i:
                    for s in range(4):
                        up(b + 4 + s, s, i + 1, t0 + i)
                    for s in range(2):
                        down(b + 8 + s, s, i, t0 + i)
                for s in range(2):
                    down(b + 40 + s, s, 6, t0)


        def ffn_tiles(q):
            q = q % 3
            return [zt[:, 6 * q + 2 * i:6 * q + 2 * i + 2, :] for i in range(3)]


        @block.sync
        def _(sp):
            def load(c, src, turns=0, width=CH):
                if not (isinstance(turns, int) and c + RAW * turns < RAW):
                    sp.wait_ge(lo_done, (turns - 1) * RAW + c + 1)
                k = src.shape[1] if len(src.shape) == 3 else 1
                dst = raw[:, c % RAW, 0:width].rearrange("p (k n) -> p k n", k=k)
                sp.dma_start(dst, src).then_inc(raw_landed[c % RAW], 16)

            sp.dma_start(con[:, :], A["constants"]).then_inc(in_con, 16)
            xp = A["x_prompt"].rearrange("b t f -> (b t) f")
            xs = A["x_sample"].rearrange("b t f -> (b t) f")
            sp.dma_start(xtok[:, 0:2, :], xp[0:2 * TT, :].rearrange("(i p) f -> p i f", p=TT)).then_inc(in_x, 16)
            sp.dma_start(xtok[0:SEQ - 2 * TT, 2, :], xp[2 * TT:SEQ, :]).then_inc(in_x, 16)
            sp.dma_start(xtok[SEQ - 2 * TT:TT, 2, :], xs).then_inc(in_x, 16)

            def rows(w, nk):
                return w.rearrange("(k p) n -> p k n", p=128)[:, 0:nk, :]

            for l in range(DEPTH):
                b = CB[l]
                win = rows(A["w_in"][l], 8)
                if l == 0:
                    for i in range(14):
                        load(b["in"] + i, win[:, :, 256 * i:256 * i + 256])
                else:
                    for i in range(2):
                        load(b["in"] + i, win[:, :, 256 * i:256 * i + 256])
                    with sp.Fori(0, 2) as it:
                        for s in range(6):
                            load(b["in"] + 2 + s, win[:, :, ds(it * 1536 + 512 + 256 * s, 256)], it)
                for i in range(2):
                    load(b["conv"] + i, rows(A["w_conv_out"][l], 4)[:, :, 512 * i:512 * i + 512])
                for i in range(8):
                    at = 3 * DC + 4 * DR + 256 * i
                    load(b["gate"] + i, win[:, :, at:at + 256])
                for i in range(2):
                    load(b["ret"] + i, rows(A["w_ret_out"][l], 4)[:, :, 512 * i:512 * i + 512])
                for i in range(4):
                    load(b["o"] + i, rows(A["w_o"][l], 8)[:, :, 256 * i:256 * i + 256])
                if l == 0:
                    gu = rows(A["w_dense_gu"][0], 8)
                    dn = A["w_dense_down"][0].rearrange("(k p) n -> p k n", p=128)
                    for hf in range(2):
                        c0 = b["ffn"] + 22 * hf
                        for i in range(2):
                            load(c0 + i, gu[:, :, DFF * i + 1792 * hf:][:, :, 0:256])
                        with sp.Fori(0, 2) as it:
                            for s in range(6):
                                at = (s % 2) * DFF + 1792 * hf + 256 * (1 + s // 2)
                                load(c0 + 2 + s, gu[:, :, ds(it * 768 + at, 256)], it)
                        for i in range(8):
                            load(c0 + 14 + i, dn[:, 14 * hf:14 * hf + 14, 128 * i:128 * i + 128],
                                 width=14 * 128)
                    ple_loads(sp, load, rows, l, 0)
                else:
                    load(b["pw"], rows(A["w_ple"][l], 2))
                    moe_loads(sp, load, 0)
                    sp.wait_ge(routed, 1)
                    n = sp.value_load(passes[0:1, 0:1], min_val=1, max_val=3)
                    with sp.If(n > 1):
                        with sp.Fori(1, n) as ps:
                            moe_loads(sp, load, ps)
                    with sp.Else():
                        sp.nop()
                    ple_loads(sp, load, rows, l, n * (NE * MOE_TURNS))

        @block.gpsimd
        def _(pool):
            n_chain = [0]

            def link(ins):
                n_chain[0] += 1
                ins.then_inc(pool_chain, 1)
                pool.wait_ge(pool_chain, n_chain[0])

            def squares(norm):
                for j in range(KT):
                    pool.wait_ge(*x_at(norm, j))
                    if j == 0:
                        if norm not in (0, 5):
                            pool.wait_ge(stat_ready, turn_of(norm))
                        link(pool.tensor_tensor(sacc[:, :], x[:, 0, :], x[:, 0, :], ALU.mult))
                    else:
                        link(pool.tensor_tensor(sq[:, :], x[:, j, :], x[:, j, :], ALU.mult))
                        ins = pool.tensor_tensor(sacc[:, :], sacc[:, :], sq[:, :], ALU.add)
                        if j == KT - 1:
                            ins.then_inc(sq_ready, 1)
                            pool.wait_ge(sq_ready, norm + 1)
                        else:
                            link(ins)

            pool.dma_start(vrow[0:16, :], A["norm_mix_g"].rearrange("l (k p) -> (l k) p", p=128)).then_inc(in_misc, 16)
            pool.dma_start(vrow[16:32, :], A["norm_ffn_g"].rearrange("l (k p) -> (l k) p", p=128)).then_inc(in_misc, 16)
            pool.dma_start(vrow[32:48, :], A["norm_ple_g"].rearrange("l (k p) -> (l k) p", p=128)).then_inc(in_misc, 16)
            pool.dma_start(vrow[48:56, :], A["norm_final_g"].rearrange("(k p) -> k p", p=128)).then_inc(in_misc, 16)
            pool.dma_start(vrow[56:80, :], A["conv_w"].rearrange("l w (k p) -> (l w k) p", p=128)).then_inc(in_misc, 16)
            pool.dma_start(crow, A["state_conv"].rearrange("l b w c -> (b w) l c")).then_inc(in_misc, 16)
            pp = A["p_prompt"].rearrange("l b t f -> (b t) l f")
            ps_ = A["p_sample"].rearrange("l b t f -> (b t) l f")
            for i in range(2):
                pool.dma_start(ptok[:, i, :].rearrange("p (l f) -> p l f", l=2), pp[TT * i:TT * i + TT]).then_inc(in_misc, 16)
            pool.dma_start(ptok[0:80, 2, :].rearrange("p (l f) -> p l f", l=2), pp[2 * TT:SEQ]).then_inc(in_misc, 16)
            pool.dma_start(ptok[80:88, 2, :].rearrange("p (l f) -> p l f", l=2), ps_).then_inc(in_misc, 16)
            pool.dma_start(wrr[:, :].rearrange("p (k n) -> p k n", n=NE), A["w_router"][0].rearrange("(k p) n -> p k n", p=128)).then_inc(in_wr, 16)
            pool.memset(ub[:, :, 0:2], 0.0).then_inc(pad_done, 1)
            pool.wait_ge(pad_done, 1)
            squares(0)
            for l in range(DEPTH):
                t = TB[l]
                if l > 0:
                    pool.wait_ge(chunk_begun, CB[l]["in"] + 1)
                    pool.wait_ge(so_sent, 16 * l)
                    pool.wait_ge(cout_sent, 32 * l)

                def load_state(h):
                    r = 4 * l + h
                    if r >= 2:
                        pool.wait_ge(s_sent[r % 2], 16 * (r // 2))
                        pool.wait_ge(bank3_ready, 6 * l + h + 1 if h >= 2 else 6 * l - 6 + h + 5)
                    pool.dma_start(St[r % 2].rearrange("p (b e) -> p b e", b=8),
                                   A["state_ret"][l, :, h, :, :].rearrange("b d e -> d b e")).then_inc(s_in[r % 2], 16)

                load_state(0)
                load_state(1)
                pool.wait_ge(tile_taken, t["in"] + 12)
                if l > 0:
                    pool.wait_ge(y_conv, l)
                    pool.wait_ge(cbt_ready, l)
                pool.tensor_tensor(ub[:, :, 2:2 + SEQ], CCt[:, :, 0:SEQ], CHt[:, :, 0:SEQ], ALU.mult).then_inc(u_ready, 1)
                pool.tensor_tensor(us[:, :, :], CCt[:, :, SEQ:T], CHt[:, :, SEQ:T], ALU.mult).then_inc(u_ready, 1)
                pool.wait_ge(u_ready, 2 * l + 2)
                if l > 0:
                    pool.wait_ge(cbT_ready, l)
                new = cbt[:, :, 2:18].rearrange("p k (b w) -> p k b w", w=2)
                old = cst[:, l, :, :].rearrange("p k (b w) -> p k b w", w=2)
                pool.tensor_copy(cbt[:, :, 0:2], ub[:, :, SEQ:SEQ + 2]).then_inc(pad_done, 1)
                pool.tensor_copy(new[:, :, :, 0], old[:, :, :, 1]).then_inc(pad_done, 1)
                pool.tensor_copy(new[:, :, :, 1], us[:, :, :]).then_inc(pad_done, 1)
                pool.wait_ge(pad_done, 1 + 3 * (l + 1))
                pool.nop().then_inc(cbt_ready, 1)
                pool.wait_ge(y_conv, l + 1)
                pool.tensor_tensor(CHt, CBt, CCt, ALU.mult).then_inc(a32, 1)
                pool.wait_ge(cout_ready, l + 1)
                pool.dma_start(O["conv_prompt"][l, 0, :, :], cout[0:2, :]).then_inc(cout_sent, 16)
                pool.dma_start(O["conv_sample"][l].rearrange("b w c -> (b w) c"), cout[2:18, :]).then_inc(cout_sent, 16)
                for h in range(NH):
                    r = 4 * l + h
                    pool.wait_ge(s_new, 2 * r + 2)
                    pool.dma_start(O["ret_sample"][l, :, h, :, :].rearrange("b d e -> d b e"),
                                   St[r % 2].rearrange("p (b e) -> p b e", b=8)).then_inc(s_sent[r % 2], 16)
                    if h + 2 < NH:
                        load_state(h + 2)
                pool.wait_ge(so_ready, 4 * l + 4)
                pool.dma_start(O["ret_prompt"][l, 0, :, :, :].rearrange("h d e -> d h e"), so).then_inc(so_sent, 16)
                pool.wait_ge(oc_ready, l + 1)
                pool.tensor_tensor(rtmp, Qt, Qt, ALU.mult).then_inc(osq_ready, 1)
                pool.wait_ge(gsilu_ready, l + 1)
                pool.tensor_tensor(Qt, Qt, Gt, ALU.mult).then_inc(og_ready, 1)
                squares(1 + 3 * l)
                if l == 0:
                    squares(2)
                    squares(3)
            squares(5)
            squares(6)
            for i in range(3):
                pool.wait_ge(out_ready, 2 * i + 2)
                if i < 2:
                    pool.dma_start(O["y_prompt"][0, TT * i:TT * i + TT, :], xtok[:, i, :]).then_inc(out_sent, 16)
                else:
                    pool.dma_start(O["y_prompt"][0, 2 * TT:SEQ, :], xtok[0:80, 2, :]).then_inc(out_sent, 16)
                    pool.dma_start(O["y_sample"][:, 0, :], xtok[80:88, 2, :]).then_inc(out_sent, 16)
            pool.wait_ge(out_sent, 64)
            pool.wait_ge(cout_sent, 32 * DEPTH)
            pool.wait_ge(so_sent, 16 * DEPTH)
            for i in range(2):
                pool.wait_ge(s_sent[i], 16 * 2 * DEPTH)

        def dense_act(act, cast, root, split_x):
            b, t = CB[0], TB[0]

            def pair(q, c, tile, turns=0, t3=0):
                gb = ffn_tiles(q)[0]
                cast(c + AHEAD, turns)
                act.wait_ge(tile_taken, tile + 2 + 12 * turns)
                nc.scalar.activation(gb, gb, ACT.Silu).then_inc(f_silu, 1)
                cast(c + 1 + AHEAD, turns)

            def hi(q, pos, turns=0):
                act.wait_ge(f_act, 1 + q + 3 * turns)
                dst = frt[:, ds(turns * 6 + 2 * pos, 2), :]
                nc.scalar.activation(dst, ffn_tiles(q)[2], ACT.Copy).then_inc(f_hi, 1)

            for hf in range(2):
                c0 = b["ffn"] + 22 * hf
                t0 = t[f"gu{hf}"]
                if hf == 0:
                    cast(c0 + AHEAD)
                    root(1)
                    act.wait_ge(tile_taken, t0 + 2)
                    nc.scalar.activation(ffn_tiles(0)[0], ffn_tiles(0)[0], ACT.Silu).then_inc(f_silu, 1)
                    cast(c0 + 1 + AHEAD)
                else:
                    pair(7, c0, t0)
                with act.Fori(0, 2) as it:
                    for q in range(3):
                        pair(7 * hf + 1 + q, c0 + 2 + 2 * q, t0 + 4 + 4 * q, it)
                        hi(7 * hf + q, q, it)
                hi(7 * hf + 6, 6)
                for i in range(8):
                    cast(c0 + 14 + i + AHEAD)
                    if hf == 1:
                        split_x(2, (i,))


        def ple_act(act, cast, root, split_x, l, turns=0):
            b, t = CB[l], TB[l]
            last = l == DEPTH - 1
            norm = NORM_OF["ple", l]
            for i in range(4):
                if not (last and i + AHEAD >= 4):
                    cast(b["pg"] + i + AHEAD, turns)
                if i == 0:
                    root(norm)
                for s in range(2):
                    j = 2 * i + s
                    act.wait_ge(tile_taken, t["pg"] + j + 1)
                    nc.scalar.activation(zt[:, 8 + j, :], zt[:, 8 + j, :], ACT.Sigmoid).then_inc(psig, 1)
            if not last:
                act.wait_ge(tile_ready, t["pg"] + 8)
                split_x(3)


        def after(eng, sem_, n):
            if not (isinstance(n, int) and n <= 0):
                eng.wait_ge(sem_, n)


        def moe_act(act, cast, root, split_x):
            b = CB[1]["ffn"]
            act.wait_ge(in_wr, 16)
            nc.scalar.activation(wrh[:, :], wrr[:, :], ACT.Copy).then_inc(wr_hi, 1)
            act.wait_ge(logit_ready, 1)
            nc.scalar.activation(rt[:, 0:3], PS[0:TT, 7, 24:27], ACT.Sqrt, bias=epsb[0:TT, :],
                                 scale=1.0 / D).then_inc(route_act, 1)
            cast(CB[1]["pw"] + AHEAD)
            act.wait_ge(route_dve, 1)
            nc.scalar.activation(rt[:, 60:66], rt[:, 54:60], ACT.Exp).then_inc(route_act, 1)
            for i in range(6):
                act.wait_ge(tok_ready, 2 * i + 1)
                nc.scalar.activation(htok_h[:, i // 2, 512 * (i % 2):512 * (i % 2) + 512],
                                     PS[0:TT, 3, :], ACT.Copy).then_inc(tokh_done, 1)

            def gathered(it):
                act.wait_ge(gath_hi, it + 1)
                for i in range(2):
                    nc.scalar.activation(gh[:, 512 * i:512 * i + 512], PS[:, 2 + i, :], ACT.Copy).then_inc(gh_done, 1)

            def gate(m):
                act.wait_ge(g_ready, m + 1)
                nc.scalar.activation(sgm, PS[:, 2, :], ACT.Silu, scale=srs[:, 0:1]).then_inc(sg_done, 1)

            def hi(m):
                act.wait_ge(aT_ready, m + 1)
                nc.scalar.activation(actT_h, PS[:, 4, :], ACT.Copy).then_inc(aTh_done, 1)

            def full(c, turns, m):
                for s in range(6):
                    cast(c + s + AHEAD, turns)
                    if s == 1:
                        act.wait_ge(aa_done, m)
                        gate(m)
                        hi(m - 1)

            def item(it, before):
                t0 = it * MOE_TURNS
                if before is not None:
                    act.wait_ge(y_ready, before + 1)
                    for i in range(2):
                        nc.scalar.activation(yh[:, 512 * i:512 * i + 512], PS[:, i, :], ACT.Copy,
                                             scale=sgate[:, 0:1]).then_inc(yh_done, 1)
                for s in range(4):
                    cast(b + s + AHEAD, t0)
                    if s == 1:
                        act.wait_ge(slot_rs, it + 1)
                        after(act, aa_done, it * 7)
                        gate(it * 7)
                full(b + 4, t0, it * 7 + 1)
                with act.Fori(0, 5) as j:
                    full(b + 10, t0 + j, it * 7 + 2 + j)
                hi(it * 7 + 6)
                gathered(it + 1)
                for s in range(2):
                    cast(b + 40 + s + AHEAD, t0)

            act.wait_ge(routed, 1)
            n = act.value_load(passes[0:1, 0:1], min_val=1, max_val=3)
            last = act.value_load(passes[0:1, 1:2], min_val=NE - 1, max_val=ITEMS - 1)
            gathered(0)
            item(0, None)
            with act.Fori(0, last) as before:
                item(before + 1, before)
            act.wait_ge(y_ready, last + 1)
            for i in range(2):
                nc.scalar.activation(yh[:, 512 * i:512 * i + 512], PS[:, i, :], ACT.Copy,
                                     scale=sgate[:, 0:1]).then_inc(yh_done, 1)
            split_x(5)
            ple_act(act, cast, root, split_x, 1, n * (NE * MOE_TURNS))


        def slot_chunk(b, s):
            return (b["conv"] if s < 2 else b["gate"] - 2) + s


        def gate_tile(n):
            return zt[:, 8 + n % 4, :] if n < 8 else zt[:, 8 + n, :]


        @block.scalar
        def _(act):
            def cast(c, turns=0):
                act.wait_ge(raw_landed[c % RAW], 16 * (c // RAW + 1) + 16 * turns)
                if not (isinstance(turns, int) and c + RAW * turns < CAST):
                    act.wait_ge(chunk_begun, RAW * turns + c - CAST + 2)
                nc.scalar.activation(whi[:, c % CAST, :], raw[:, c % RAW, :], ACT.Copy).then_inc(hi_done, 1)

            def split_x(norm, tiles=range(KT)):
                for j in tiles:
                    act.wait_ge(*x_at(norm, j))
                    nc.scalar.activation(xht[:, j, :], x[:, j, :], ACT.Copy,
                                         scale=vec[:, GAIN[norm] + j:GAIN[norm] + j + 1]).then_inc(xh_ready, 1)

            def root(norm):
                k = turn_of(norm)
                act.wait_ge(stat_ready, k + 1)
                if k > 0:
                    act.wait_ge(rstd_ready, k)
                nc.scalar.activation(sq_root[:, :], PS[:, 3, 0:T], ACT.Sqrt, bias=epsb[:, :],
                                     scale=1.0 / D).then_inc(root_ready, 1)

            act.wait_ge(in_con, 16)
            nc.scalar.activation(idr[:, :], ident, ACT.Copy).then_inc(idr_done, 1)
            act.wait_ge(eps_done, 1)
            cast(0)
            cast(1)
            act.wait_ge(tile_taken, 1)
            split_x(0)
            for j in range(4):
                act.wait_ge(tile_ready, 10 + j + 1)
                nc.scalar.activation(ph[:, j, :], PS[:, (10 + j) % RING, 0:T], ACT.Copy).then_inc(p_hi, 1)
            for l in range(DEPTH):
                b, t = CB[l], TB[l]
                mixn = NORM_OF["in", l]
                cast(b["in"] + AHEAD)
                root(mixn)
                for i in range(1, 14):
                    cast(b["in"] + i + AHEAD)
                act.wait_ge(a32, l + 1)
                nc.scalar.activation(fr[:, 0:4 * T], CHt, ACT.Copy).then_inc(a_hi, 1)
                act.wait_ge(cbT_ready, l + 1)
                if l > 0:
                    act.wait_ge(cout_sent, 32 * l)
                    act.wait_ge(so_sent, 16 * l)
                nc.scalar.activation(cout, PS[0:18, 7, 0:512], ACT.Copy).then_inc(cout_ready, 1)

                def sigmoids(s):
                    for n in (2 * s - 4, 2 * s - 3):
                        act.wait_ge(tile_taken, t["gate"] + n + 1)
                        g = gate_tile(n)
                        nc.scalar.activation(g, g, ACT.Sigmoid).then_inc(gsig, 1)

                for s in range(SLOTS):
                    if s < NH:
                        h = s
                        act.wait_ge(bank3_ready, 6 * l + s + 1)
                        for i in range(2):
                            nc.scalar.activation(ktok[:, 128 * i:128 * i + 128], PS[:, 3, 128 * i:128 * i + 128], ACT.Copy,
                                                 scale=kd[:, 2 * h + i:2 * h + i + 1]).then_inc(ktok_ready, 1)
                        nc.scalar.activation(kss, PS[0:8, 3, 256:384], ACT.Copy, scale=float(DK ** -0.5)).then_inc(ktok_ready, 1)
                    if 2 <= s < NH + 2:
                        act.wait_ge(bank3_ready, 6 * l + s + 1)
                        nc.scalar.activation(Qt[:, s - 2, SEQ:T], PS[:, 3, 384:384 + NB], ACT.Copy).then_inc(os_taken, 1)
                    if 1 <= s < NH + 1:
                        act.wait_ge(o_ready, 4 * l + s)
                        nc.scalar.activation(so[:, s - 1, :], PS[:, 5, 384:512], ACT.Copy).then_inc(so_ready, 1)
                        nc.scalar.activation(Qt[:, s - 1, 0:SEQ], PS[:, 5, 0:SEQ], ACT.Copy).then_inc(o_taken, 1)
                    if s == 6:
                        act.wait_ge(cent_ready, l + 1)
                        nc.scalar.activation(Qt, PS[:, 4:8, 0:T], ACT.Copy).then_inc(oc_ready, 1)
                    if s == 7:
                        act.wait_ge(var_ready, l + 1)
                        nc.scalar.activation(gstat[:, 0, :], PS[0:TT, 3, 0:12], ACT.Sqrt, bias=epsb[0:TT, :],
                                             scale=1.0 / DK).then_inc(groot_ready, 1)
                    cast(slot_chunk(b, s) + AHEAD)
                    if s > 2:
                        sigmoids(s - 1)
                    if s == 4:
                        nc.scalar.activation(Gt, Gt, ACT.Silu).then_inc(gsilu_ready, 1)
                    if s == 8:
                        act.wait_ge(r32, l + 1)
                        nc.scalar.activation(fr[:, 0:4 * T], Qt, ACT.Copy).then_inc(r_hi, 1)
                sigmoids(9)
                for i in range(2):
                    act.wait_ge(s_sent[i], 32 * (l + 1))
                act.wait_ge(so_sent, 16 * (l + 1))
                act.wait_ge(cout_sent, 32 * (l + 1))
                for i in range(2):
                    cast(b["ret"] + i + AHEAD)
                    for j in range(4 * i, 4 * i + 4):
                        act.wait_ge(m32, 8 * l + j + 1)
                        nc.scalar.activation(frt[:, 8 + j, :], zt[:, 16 + j, :], ACT.Copy).then_inc(m_hi, 1)
                for i in range(4):
                    cast(b["o"] + i + AHEAD)
                    split_x(NORM_OF["ffn", l], (2 * i, 2 * i + 1))
                if l == 0:
                    dense_act(act, cast, root, split_x)
                    cast(b["pw"] + AHEAD)
                    ple_act(act, cast, root, split_x, 0)
                else:
                    moe_act(act, cast, root, split_x)
            root(6)
            for i in range(3):
                for hf in range(2):
                    act.wait_ge(finT_ready, 2 * i + hf + 1)
                    nc.scalar.activation(xtok[:, i, 512 * hf:512 * hf + 512],
                                         PS[0:TT, 4 + hf, :], ACT.Copy).then_inc(out_ready, 1)


        def dense_dve(dve, v, cast, recip, take, split_x):
            b, t = CB[0], TB[0]

            def pair(q, c, p, turns=0, first=False):
                gb, ub_, ab = ffn_tiles(q)
                cast(c + AHEAD, turns)
                if first:
                    recip(1)
                for s in range(2):
                    take(p + s, gb[:, s, :], rstd[:, :], turns12=12 * turns)
                cast(c + 1 + AHEAD, turns)
                for s in range(2):
                    take(p + 2 + s, ub_[:, s, :], rstd[:, :], turns12=12 * turns)

            def product(q, pos, p, turns=0):
                gb, ub_, ab = ffn_tiles(q)
                dve.wait_ge(f_silu, q + 1 + 3 * turns)
                dve.wait_ge(tile_taken, p + 4 + 12 * turns)
                v.tensor_tensor(ab, gb, ub_, ALU.mult).then_inc(f_act, 1)
                dve.wait_ge(f_act, q + 1 + 3 * turns)
                dve.wait_ge(f_hi, q + 1 + 3 * turns)
                v.tensor_tensor(frt[:, ds(turns * 6 + 14 + 2 * pos, 2), :], ab,
                                frt[:, ds(turns * 6 + 2 * pos, 2), :].bitcast(F32), ALU.subtract).then_inc(f_lo, 1)

            for hf in range(2):
                c0, t0 = b["ffn"] + 22 * hf, t[f"gu{hf}"]
                pair(7 * hf, c0, t0, first=(hf == 0))
                with dve.Fori(0, 2) as it:
                    for q in range(3):
                        pair(7 * hf + 1 + q, c0 + 2 + 2 * q, t0 + 4 + 4 * q, it)
                        product(7 * hf + q, q, t0 + 4 * q, it)
                product(7 * hf + 6, 6, t0 + 24)
                for i in range(8):
                    cast(c0 + 14 + i + AHEAD)
                    p = t[f"down{hf}"] + i
                    dve.wait_ge(tile_ready, p + 1)
                    v.tensor_tensor(x[:, i, :], PS[:, p % RING, 0:T], x[:, i, :], ALU.add).then_inc(tile_taken, 1)
                    dve.wait_ge(tile_taken, p + 1)
                    if hf == 1:
                        split_x(16, 2, i)


        def pw_dve(v, dve, cast, l):
            b, t = CB[l], TB[l]
            cast(b["pw"] + AHEAD)
            for j in range(KT):
                p = t["pw"] + j
                dve.wait_ge(tile_ready, p + 1)
                v.tensor_copy(zt[:, 20 + j, :], PS[:, p % RING, 0:T]).then_inc(tile_taken, 1)


        def ple_dve(dve, v, cast, recip, take, split_x, l, turns=0):
            b, t = CB[l], TB[l]
            last = l == DEPTH - 1
            for i in range(4):
                if not (last and i + AHEAD >= 4):
                    cast(b["pg"] + i + AHEAD, turns)
                if i == 0:
                    recip(NORM_OF["ple", l])
                for s in range(2):
                    j = 2 * i + s
                    take(t["pg"] + j, zt[:, 8 + j, :], rstd[:, :])
                for s in range(2):
                    j = 2 * i + s
                    n = 8 * l + j
                    dve.wait_ge(psig, n + 1)
                    v.tensor_tensor(zt[:, 8 + j, :], zt[:, 20 + j, :], zt[:, 8 + j, :], ALU.mult).then_inc(pprod, 1)
                    dve.wait_ge(pprod, n + 1)
                    v.tensor_tensor(x[:, j, :], x[:, j, :], zt[:, 8 + j, :], ALU.add).then_inc(x_ready, 1)
                    dve.wait_ge(x_ready, n + 1)
            if not last:
                for j in range(KT):
                    split_x(24, 3, j)


        def moe_dve(dve, v, cast, recip, take, split_x, link, n_chain, newton):
            b = CB[1]["ffn"]
            recip_cols = rt[:, 0:3]
            dve.wait_ge(wr_hi, 1)
            v.tensor_tensor(wrl[:, :], wrr[:, :], wrh[:, :].bitcast(F32), ALU.subtract).then_inc(wr_lo, 1)
            dve.wait_ge(route_act, 1)
            v.memset(rg[:, :, 1:2], 0.0).then_inc(dve_chain, 1)
            n_chain[0] += 1
            link(v.tensor_scalar(rt[:, 232:235], PS[0:TT, 7, 24:27], 1.0 / D, EPS, ALU.mult, ALU.add))
            link(v.reciprocal(rg[:, :, 0], recip_cols))
            newton(rg[:, :, 0], rt[:, 232:235])
            lg = rt[:, 3:27].rearrange("p (t e) -> p t e", t=3)
            top = rt[:, 27:51].rearrange("p (t e) -> p t e", t=3)
            dif = rt[:, 54:60].rearrange("p (t e) -> p t e", t=3)
            ex = rt[:, 60:66].rearrange("p (t e) -> p t e", t=3)
            idf = rt[:, 66:90].rearrange("p (t e) -> p t e", t=3)
            den, rden = rt[:, 90:93], rt[:, 93:96]
            gt = rt[:, 96:102].rearrange("p (t e) -> p t e", t=3)
            eq = rt[:, 102:150].rearrange("p (i t e) -> p i t e", i=2, t=3)
            mask = rt[:, 150:174].rearrange("p (t e) -> p t e", t=3)
            gm = rt[:, 174:222].rearrange("p (i t e) -> p i t e", i=2, t=3)
            cnt = rt[0:1, 222:232]
            link(v.tensor_tensor(lg, PS[0:TT, 7, 0:24].rearrange("p (t e) -> p t e", t=3),
                                 rg[:, :, 0:1].to_broadcast([TT, 3, 8]), ALU.mult))
            for i in range(3):
                v.max(top[:, i, :], lg[:, i, :]).then_inc(dve_chain, 1)
            n_chain[0] += 3
            dve.wait_ge(dve_chain, n_chain[0])
            for i in range(3):
                v.max_index(idx[:, i, :], top[:, i, :], lg[:, i, :]).then_inc(dve_chain, 1)
            n_chain[0] += 3
            v.tensor_tensor(dif, top[:, :, 0:2], top[:, :, 0:1].to_broadcast([TT, 3, 2]),
                            ALU.subtract).then_inc(route_dve, 1)
            dve.wait_ge(dve_chain, n_chain[0])
            link(v.tensor_copy(idf[:, :, :], idx[:, :, :]))
            pw_dve(v, dve, cast, 1)
            dve.wait_ge(route_act, 2)
            link(v.tensor_tensor(den, ex[:, :, 0], ex[:, :, 1], ALU.add))
            link(v.reciprocal(rden, den))
            link(v.tensor_tensor(gt, ex, rden.unsqueeze(2).to_broadcast([TT, 3, 2]), ALU.mult))
            for i in range(2):
                link(v.tensor_tensor(eq[:, i], iota8.unsqueeze(1).to_broadcast([TT, 3, 8]),
                                     idf[:, :, i:i + 1].to_broadcast([TT, 3, 8]), ALU.is_equal))
                link(v.tensor_tensor(gm[:, i], eq[:, i], gt[:, :, i:i + 1].to_broadcast([TT, 3, 8]), ALU.mult))
            v.tensor_tensor(mask, eq[:, 0], eq[:, 1], ALU.add).then_inc(route_dve, 1)
            for ps in range(3):
                v.tensor_tensor(rg[:, :, 2 + NE * ps:2 + NE * ps + NE], gm[:, 0], gm[:, 1], ALU.add).then_inc(dve_chain, 1)
            n_chain[0] += 3
            for i in range(6):
                dve.wait_ge(tok_ready, 2 * i + 2)
                dve.wait_ge(tokh_done, i + 1)
                v.tensor_copy(htok_l[:, i // 2, 512 * (i % 2):512 * (i % 2) + 512],
                              PS[0:TT, 4, :]).then_inc(tokl_done, 1)
            dve.wait_ge(route_dve, 2)
            dve.wait_ge(rank_ready, 1)
            link(v.tensor_scalar(posm[:, :, 0:NE], PS[0:TT, 7, 32:56].rearrange("p (t e) -> p t e", t=3),
                                 10000.0, None, ALU.add))
            link(v.tensor_tensor(posm[:, :, 0:NE], posm[:, :, 0:NE], mask, ALU.mult))
            link(v.tensor_scalar(posm[:, :, 0:NE], posm[:, :, 0:NE], -10000.0, None, ALU.add))

            def select(it):
                for i in range(3):
                    v.tensor_scalar(sel[:, i, :], iota, posm[:, i, it if isinstance(it, slice) else ds(it, 1)],
                                    None, ALU.is_equal).then_inc(sel_ready, 1)

            select(slice(0, 1))
            link(v.max(cnt[:, 0:8], PS[0:1, 7, 64:72]))
            link(v.tensor_scalar(cnt[:, 8:9], cnt[:, 0:1], 128.5, 1.0, ALU.is_gt, ALU.add))
            link(v.scalar_tensor_tensor(cnt[:, 9:10], cnt[:, 0:1], 256.5, cnt[:, 8:9], ALU.is_gt, ALU.add))
            v.tensor_scalar(passes[:, 1:2], cnt[:, 9:10], float(NE), -1.0, ALU.mult, ALU.add).then_inc(dve_chain, 1)
            v.tensor_copy(passes[:, 0:1], cnt[:, 9:10]).then_inc(dve_chain, 1)
            for ps in range(1, 3):
                v.tensor_scalar(posm[:, :, NE * ps:NE * ps + NE], posm[:, :, 0:NE], -128.0 * ps, None,
                                ALU.add).then_inc(dve_chain, 1)
            v.tensor_scalar(posm[:, :, ITEMS:ITEMS + 1], posm[:, :, 0:1], -384.0, None, ALU.add).then_inc(dve_chain, 1)
            n_chain[0] += 5
            dve.wait_ge(dve_chain, n_chain[0])
            dve.nop().then_inc(routed, 1)

            def gathered(it):
                dve.wait_ge(gath_lo, it + 1)
                for i in range(2):
                    v.tensor_copy(gl[:, 512 * i:512 * i + 512], PS[:, 5 + i, :]).then_inc(gl_done, 1)

            def outputs(it):
                for i in range(2):
                    dve.wait_ge(yh_done, it * 2 + i + 1)
                    v.scalar_tensor_tensor(yl[:, 512 * i:512 * i + 512], PS[:, i, :], sgate[:, 0:1],
                                           yh[:, 512 * i:512 * i + 512].bitcast(F32),
                                           ALU.mult, ALU.subtract).then_inc(yl_done, 1)

            def scattered(it, tiles):
                for j in tiles:
                    dve.wait_ge(scat_ready, it * 8 + j + 1)
                    v.tensor_tensor(x[:, j, :], PS[:, 5 + j % 2, 0:T], x[:, j, :], ALU.add).then_inc(scat_taken, 1)

            def product(m):
                dve.wait_ge(u_rdy, m + 1)
                dve.wait_ge(sg_done, m + 1)
                v.scalar_tensor_tensor(aam, PS[:, 3, :], srs[:, 0:1], sgm, ALU.mult, ALU.mult).then_inc(aa_done, 1)

            def lo(m):
                dve.wait_ge(aTh_done, m + 1)
                v.tensor_tensor(actT_l, PS[:, 4, :], actT_h.bitcast(F32), ALU.subtract).then_inc(aTl_done, 1)

            def full(c, turns, m):
                for s in range(6):
                    if s == 2:
                        lo(m - 1)
                    cast(c + s + AHEAD, turns)
                    if s == 4:
                        product(m)

            def item(it, before):
                t0 = it * MOE_TURNS
                back = (lambda tiles: scattered(before, tiles)) if before is not None else (lambda tiles: None)
                if before is not None:
                    outputs(before)
                cast(b + AHEAD, t0)
                cast(b + 1 + AHEAD, t0)
                back((0, 1))
                dve.wait_ge(table_ready, it + 1)
                v.tensor_copy(srs[:, :], PS[:, 7, 0:1]).then_inc(slot_rs, 1)
                v.tensor_copy(sgate[:, :], PS[:, 7, 2:3] if before is None else PS[:, 7, ds(it + 2, 1)]).then_inc(slot_gate, 1)
                cast(b + 2 + AHEAD, t0)
                back((2, 3))
                cast(b + 3 + AHEAD, t0)
                dve.wait_ge(slot_rs, it + 1)
                product(it * 7)
                back((4, 5))
                cast(b + 4 + AHEAD, t0)
                back((6, 7))
                dve.wait_ge(selT_ready, it + 1)
                v.tensor_copy(selT, PS[:, 7, 128:128 + T]).then_inc(selT_done, 1)
                select(slice(1, 2) if before is None else it + 1)
                cast(b + 5 + AHEAD, t0)
                lo(it * 7)
                for s in range(2, 6):
                    cast(b + 4 + s + AHEAD, t0)
                    if s == 4:
                        product(it * 7 + 1)
                with dve.Fori(0, 5) as j:
                    full(b + 10, t0 + j, it * 7 + 2 + j)
                lo(it * 7 + 6)
                gathered(it + 1)
                for s in range(2):
                    cast(b + 40 + s + AHEAD, t0)

            dve.wait_ge(routed, 1)
            n = dve.value_load(passes[0:1, 0:1], min_val=1, max_val=3)
            last = dve.value_load(passes[0:1, 1:2], min_val=NE - 1, max_val=ITEMS - 1)
            gathered(0)
            item(0, None)
            with dve.Fori(0, last) as before:
                item(before + 1, before)
            outputs(last)
            scattered(last, range(KT))
            dve.wait_ge(scat_taken, last * 8 + 8)
            dve.nop().then_inc(moe_done, 1)
            for j in range(KT):
                split_x(40, 5, j)
            ple_dve(dve, v, cast, recip, take, split_x, 1, n * (NE * MOE_TURNS))


        @block.vector
        def _(dve):
            v = nc.vector
            n_chain = [0]

            def link(ins):
                n_chain[0] += 1
                ins.then_inc(dve_chain, 1)
                dve.wait_ge(dve_chain, n_chain[0])

            def cast(c, turns=0):
                dve.wait_ge(hi_done, RAW * turns + c + 1)
                v.tensor_tensor(wlo[:, c % CAST, :], raw[:, c % RAW, :],
                                whi[:, c % CAST, :].bitcast(F32), ALU.subtract).then_inc(lo_done, 1)

            def split_x(n8, norm, j):
                dve.wait_ge(xh_ready, n8 + j + 1)
                v.scalar_tensor_tensor(xlt[:, j, :], x[:, j, :], vec[:, GAIN[norm] + j:GAIN[norm] + j + 1],
                                       xht[:, j, :].bitcast(F32), ALU.mult, ALU.subtract).then_inc(xl_ready, 1)

            def newton(y, ms, last=None):
                link(v.tensor_tensor(ms, ms, y, ALU.mult))
                link(v.scalar_tensor_tensor(ms, ms, -0.5, y, ALU.mult, ALU.mult))
                if last is None:
                    link(v.scalar_tensor_tensor(y, ms, 1.5, y, ALU.add, ALU.mult))
                else:
                    v.scalar_tensor_tensor(y, ms, 1.5, y, ALU.add, ALU.mult).then_inc(last, 1)

            def recip(norm):
                k = turn_of(norm)
                dve.wait_ge(root_ready, k + 1)
                v.tensor_scalar(nwt[:, :], PS[:, 3, 0:T], 1.0 / D, EPS, ALU.mult, ALU.add).then_inc(ms_ready, 1)
                link(v.reciprocal(rstd[:, :], sq_root[:, :]))
                dve.wait_ge(ms_ready, k + 1)
                newton(rstd[:, :], nwt[:, :], rstd_ready)
                dve.wait_ge(rstd_ready, k + 1)

            def take(p, dst, in1, op=ALU.mult, turns12=0):
                dve.wait_ge(tile_ready, p + 1 + turns12)
                v.tensor_tensor(dst, PS[:, p % RING, 0:T], in1, op).then_inc(tile_taken, 1)

            v.memset(epsb[:, :], EPS).then_inc(eps_done, 1)
            dve.wait_ge(tile_ready, 1)
            v.tensor_copy(vec[:, :], PS[:, 0, 0:80]).then_inc(tile_taken, 1)
            dve.wait_ge(tile_ready, 2)
            v.tensor_copy(cst[:, :, :, :].rearrange("p l k c -> p (l k c)"), PS[:, 1, 0:128]).then_inc(tile_taken, 1)
            cast(0)
            for j in range(KT):
                dve.wait_ge(tile_ready, 3 + j)
                v.tensor_copy(x[:, j, :], PS[:, (2 + j) % RING, 0:T]).then_inc(tile_taken, 1)
                dve.wait_ge(tile_taken, 3 + j)
            for j in range(KT):
                split_x(0, 0, j)
            cast(1)
            for j in range(4):
                dve.wait_ge(p_hi, j + 1)
                v.tensor_tensor(pl[:, j, :], PS[:, (10 + j) % RING, 0:T], ph[:, j, :].bitcast(F32),
                                ALU.subtract).then_inc(tile_taken, 1)

            for l in range(DEPTH):
                b, t = CB[l], TB[l]
                mixn = NORM_OF["in", l]

                def w_in(i):
                    cast(b["in"] + i + AHEAD)
                    if i == 0:
                        recip(mixn)
                    for s in range(2):
                        take(t["in"] + 2 * i + s, zt[:, 2 * i + s, :], rstd[:, :])

                def rope(X, n):
                    def tab(a, lo):
                        return a[lo:lo + 64, :].unsqueeze(1).to_broadcast([64, 4, T])
                    v.tensor_tensor(rtmp[0:64], X[64:128], tab(sin, 64), ALU.mult).then_inc(dve_chain, 1)
                    n_chain[0] += 1
                    link(v.tensor_tensor(rtmp[64:128], X[0:64], tab(sin, 0), ALU.mult))
                    link(v.tensor_tensor(X, X, cos.unsqueeze(1).to_broadcast([128, 4, T]), ALU.mult))
                    v.tensor_tensor(X, X, rtmp, ALU.add).then_inc(rope_ready, 1)
                    dve.wait_ge(rope_ready, n)

                for i in range(9):
                    w_in(i)
                dve.wait_ge(u_ready, 2 * l + 2)
                old = cst[:, l, :, :].rearrange("p k (b w) -> p k b w", w=2)
                for tap in (2, 1, 0):
                    for j in range(4):
                        w = vec[:, CONVW + 12 * l + 4 * tap + j:CONVW + 12 * l + 4 * tap + j + 1]
                        yp, ys = CCt[:, j, 0:SEQ], CCt[:, j, SEQ:T]
                        if tap == 2:
                            v.tensor_scalar(yp, ub[:, j, 2:2 + SEQ], w, None, ALU.mult).then_inc(dve_chain, 1)
                            ins = v.tensor_scalar(ys, us[:, j, :], w, None, ALU.mult)
                        else:
                            v.scalar_tensor_tensor(yp, ub[:, j, tap:tap + SEQ], w, yp, ALU.mult, ALU.add).then_inc(dve_chain, 1)
                            ins = v.scalar_tensor_tensor(ys, old[:, j, :, tap], w, ys, ALU.mult, ALU.add)
                        n_chain[0] += 2
                        ins.then_inc(dve_chain, 1)
                    dve.wait_ge(dve_chain, n_chain[0])
                dve.nop().then_inc(y_conv, 1)
                w_in(9)
                rope(Qt, 2 * l + 1)
                w_in(10)
                rope(Kt, 2 * l + 2)
                w_in(11)
                dve.wait_ge(a_hi, l + 1)
                v.tensor_tensor(fr[:, 4 * T:8 * T].rearrange("p (k t) -> p k t", k=4), CHt,
                                frt[:, 0:4, :].bitcast(F32), ALU.subtract).then_inc(a_lo, 1)
                w_in(12)
                w_in(13)

                def gated(s):
                    for n in (2 * s - 4, 2 * s - 3):
                        dve.wait_ge(gsig, 16 * l + n + 1)
                        v.tensor_tensor(zt[:, n, :], zt[:, n, :], gate_tile(n), ALU.mult).then_inc(a_gated, 1)

                for s in range(SLOTS):
                    if 1 <= s < NH + 1:
                        r = 4 * l + s - 1
                        def state(hf):
                            dve.wait_ge(kv_outer, 2 * r + hf + 1)
                            S = St[r % 2][:, 512 * hf:512 * hf + 512]
                            v.scalar_tensor_tensor(S, S, float(np.float32(GAMMA[s - 1])), PS[:, 7, :],
                                                   ALU.mult, ALU.add).then_inc(s_new, 1)
                        dve.wait_ge(s_in[r % 2], 16 * (r // 2 + 1))
                        state(0)
                    if s < NH:
                        dve.wait_ge(vT_ready, 4 * l + s + 1)
                        v.tensor_copy(vtok, PS[:, 6, 0:256]).then_inc(vtok_ready, 1)
                        v.tensor_tensor(vd, PS[0:8, 6, 256:384].unsqueeze(1).to_broadcast([8, 8, 128]),
                                        eye8.unsqueeze(2).to_broadcast([8, 8, 128]), ALU.mult).then_inc(vtok_ready, 1)
                        dve.wait_ge(score_ready, 4 * l + s + 1)
                        v.tensor_tensor(sc[:, 0:256], PS[:, 4, 0:256], dec[:, s, :], ALU.mult).then_inc(sc_ready, 1)
                        v.tensor_tensor(sc[:, 256:384], PS[:, 4, 256:384], dec[:, s, 0:128], ALU.mult).then_inc(sc_ready, 1)
                    if 1 <= s < NH + 1:
                        state(1)
                    if s == 7:
                        dve.wait_ge(groot_ready, l + 1)
                        link(v.reciprocal(gstat[:, 1, :], gstat[:, 0, :]))
                        link(v.tensor_scalar(gstat[:, 0, :], PS[0:TT, 3, 0:12], 1.0 / DK, EPS, ALU.mult, ALU.add))
                        newton(gstat[:, 1, :], gstat[:, 0, :])
                        v.tensor_tensor(diag, ident[0:TT, 0:TT].unsqueeze(1).to_broadcast([TT, 12, TT]),
                                        gstat[:, 1, :].unsqueeze(2).to_broadcast([TT, 12, TT]), ALU.mult).then_inc(diag_ready, 1)
                    if s == 8:
                        dve.wait_ge(rsb_ready, l + 1)
                        dve.wait_ge(og_ready, l + 1)
                        v.tensor_tensor(Qt, Qt, PS[:, 4:8, 0:T], ALU.mult).then_inc(r32, 1)
                    cast(slot_chunk(b, s) + AHEAD)
                    if 3 <= s < 7:
                        gated(s - 1)
                    if s == 0:
                        dve.wait_ge(a32, l + 1)
                    if s == 9:
                        dve.wait_ge(r32, l + 1)
                        dve.wait_ge(r_hi, l + 1)
                        v.tensor_tensor(fr[:, 4 * T:8 * T].rearrange("p (k t) -> p k t", k=4), Qt,
                                        frt[:, 0:4, :].bitcast(F32), ALU.subtract).then_inc(r_lo, 1)
                    if s < 2:
                        for j in range(4 * s, 4 * s + 4):
                            p = t["conv"] + j
                            dve.wait_ge(tile_ready, p + 1)
                            v.tensor_copy(zt[:, j, :], PS[:, p % RING, 0:T]).then_inc(tile_taken, 1)
                    else:
                        for n in (2 * s - 4, 2 * s - 3):
                            take(t["gate"] + n, gate_tile(n), rstd[:, :])
                def m_rest(j):
                    dve.wait_ge(m_hi, 8 * l + j + 1)
                    v.tensor_tensor(frt[:, 16 + j, :], zt[:, 16 + j, :], frt[:, 8 + j, :].bitcast(F32),
                                    ALU.subtract).then_inc(m_lo, 1)

                dve.wait_ge(a_gated, 8 * (l + 1))
                for i in range(2):
                    cast(b["ret"] + i + AHEAD)
                    for j in range(4 * i, 4 * i + 4):
                        p = t["ret"] + j
                        m = zt[:, 16 + j, :]
                        dve.wait_ge(gsig, 16 * l + 8 + j + 1)
                        dve.wait_ge(tile_ready, p + 1)
                        v.tensor_tensor(m, PS[:, p % RING, 0:T], m, ALU.mult).then_inc(tile_taken, 1)
                        dve.wait_ge(tile_taken, p + 1)
                        v.tensor_tensor(m, m, zt[:, j, :], ALU.add).then_inc(m32, 1)
                        dve.wait_ge(m32, 8 * l + j + 1)
                        if j > 0:
                            m_rest(j - 1)
                m_rest(7)
                fn = NORM_OF["ffn", l]
                for i in range(4):
                    cast(b["o"] + i + AHEAD)
                    for j in (2 * i, 2 * i + 1):
                        p = t["o"] + j
                        dve.wait_ge(tile_ready, p + 1)
                        v.tensor_tensor(x[:, j, :], PS[:, p % RING, 0:T], x[:, j, :], ALU.add).then_inc(tile_taken, 1)
                        dve.wait_ge(tile_taken, p + 1)
                    for j in (2 * i, 2 * i + 1):
                        split_x(8 * (1 + 3 * l), fn, j)
                if l == 0:
                    dense_dve(dve, v, cast, recip, take, split_x)
                    pw_dve(v, dve, cast, 0)
                    ple_dve(dve, v, cast, recip, take, split_x, 0)
                else:
                    moe_dve(dve, v, cast, recip, take, split_x, link, n_chain, newton)
            recip(6)
            for j in range(KT):
                g = vec[:, GAIN[6] + j:GAIN[6] + j + 1]
                v.scalar_tensor_tensor(x[:, j, :], x[:, j, :], g, rstd[:, :], ALU.mult, ALU.mult).then_inc(fin_ready, 1)


        def x_split(n8):
            return xl_ready, [n8 + k + 1 for k in range(KT)]


        def pw_pe(chunk, l):
            b, t = CB[l], TB[l]
            chunk(b["pw"], t["pw"], 2, 8, ph[:, 2 * l:2 * l + 2, :], pl[:, 2 * l:2 * l + 2, :])


        def ple_pe(pe, chunk, stat, l, turns=0):
            b, t = CB[l], TB[l]
            for i in range(4):
                chunk(b["pg"] + i, t["pg"] + 2 * i, 8, 2, xht, xlt, turns=turns,
                      each=(x_split({0: 16, 1: 40}[l]) if i == 0 else None))
                if i == 0:
                    stat(NORM_OF["ple", l])


        def moe_pe(pe, ready, three, chunk, stat):
            mm = nc.tensor.matmul
            b = CB[1]["ffn"]
            pe.wait_ge(xl_ready, 40)
            pe.wait_ge(wr_lo, 1)
            pe.wait_ge(idr_done, 1)
            for i in range(3):
                for k in range(KT):
                    cols = slice(TT * i, TT * i + TT)
                    three(PS[0:TT, 7, 8 * i:8 * i + 8], xht[:, k, cols], xlt[:, k, cols],
                          wrh[:, 8 * k:8 * k + 8], wrl[:, 8 * k:8 * k + 8], k == 0, k == KT - 1)
            pe.wait_ge(sq_ready, 5)
            for i in range(3):
                ins = mm(PS[0:TT, 7, 24 + i:25 + i], sacc[:, TT * i:TT * i + TT], ones[:, 0:1], start=True, stop=True)
            ins.then_inc(logit_ready, 1)
            pw_pe(chunk, 1)

            def places():
                pe.wait_ge(route_dve, 2)
                mask = rt[:, 150:174].rearrange("p (t e) -> p t e", t=3)
                for i in range(3):
                    for j in range(i + 1):
                        mm(PS[0:TT, 7, 32 + 8 * i:40 + 8 * i], tri if j == i else con[0:TT, C_ONE:C_ONE + TT],
                           mask[:, j, :], start=j == 0, stop=j == i)
                for j in range(3):
                    ins = mm(PS[0:TT, 7, 64:72], con[0:TT, C_ONE:C_ONE + TT], mask[:, j, :], start=j == 0, stop=j == 2)
                ins.then_inc(rank_ready, 1)

            for i in range(6):
                for (src, bank, done) in ((xht, 3, tokh_done), (xlt, 4, tokl_done)):
                    if i > 0:
                        pe.wait_ge(done, i)
                    for k in range(4):
                        ins = mm(PS[0:TT, bank, 128 * k:128 * k + 128],
                                 src[:, 4 * (i % 2) + k, TT * (i // 2):TT * (i // 2) + TT], idr[:, :],
                                 start=True, stop=True)
                    ins.then_inc(tok_ready, 1)
                if i == 0:
                    places()

            def gather(it):
                pe.wait_ge(sel_ready, it * 3 + 3)
                for tok, bank, done in ((htok_h, 2, gath_hi), (htok_l, 5, gath_lo)):
                    for k in range(KT):
                        for i in range(3):
                            ins = mm(PS[:, bank + k // 4, 128 * (k % 4):128 * (k % 4) + 128],
                                     tok[:, i, 128 * k:128 * k + 128], sel[:, i, :],
                                     start=i == 0, stop=i == 2)
                    ins.then_inc(done, 1)

            def up(c, s, bank, turns, done=None):
                ready(c + s, turns)
                for k in range(4):
                    kk = 4 * s + k
                    wh = whi[:, (c + s) % CAST, 512 * k:512 * k + 512]
                    wl = wlo[:, (c + s) % CAST, 512 * k:512 * k + 512]
                    ins = mm(PS[:, bank, :], gh[:, 128 * kk:128 * kk + 128], wh, start=kk == 0, stop=False)
                    if k == 0:
                        ins.then_inc(chunk_begun, 1)
                    mm(PS[:, bank, :], gh[:, 128 * kk:128 * kk + 128], wl, start=False, stop=False)
                    ins = mm(PS[:, bank, :], gl[:, 128 * kk:128 * kk + 128], wh, start=False, stop=kk == 7)
                if s == 1:
                    ins.then_inc(done, 1)

            def down(c, turns, first, last):
                for s in range(2):
                    ready(c + s, turns)
                    for k in range(2):
                        kk = 2 * s + k
                        ah = actT_h[:, 128 * kk:128 * kk + 128]
                        al = actT_l[:, 128 * kk:128 * kk + 128]
                        for h in range(2):
                            at = 1024 * k + 512 * h
                            wh, wl = whi[:, (c + s) % CAST, at:at + 512], wlo[:, (c + s) % CAST, at:at + 512]
                            ins = mm(PS[:, h, :], ah, wh, start=first and kk == 0, stop=False)
                            if k == 0 and h == 0:
                                ins.then_inc(chunk_begun, 1)
                            mm(PS[:, h, :], ah, wl, start=False, stop=False)
                            ins = mm(PS[:, h, :], al, wh, start=False, stop=last and kk == 3)
                if last:
                    ins.then_inc(y_ready, 1)

            def turn(m):
                pe.wait_ge(aa_done, m + 1)
                for k in range(4):
                    ins = nc.tensor.transpose(PS[:, 4, 128 * k:128 * k + 128], aam[:, 128 * k:128 * k + 128], ident)
                ins.then_inc(aT_ready, 1)

            def scatter(it, tiles):
                for j in tiles:
                    if j >= 2:
                        pe.wait_ge(scat_taken, it * 8 + j - 1)
                    mm(PS[:, 5 + j % 2, 0:T], yh[:, 128 * j:128 * j + 128], selT, start=True, stop=False)
                    mm(PS[:, 5 + j % 2, 0:T], yl[:, 128 * j:128 * j + 128], selT, start=False, stop=True).then_inc(scat_ready, 1)

            def rest(c, turns, m, first):
                turn(m - 1)
                pe.wait_ge(aa_done, m)
                up(c + 2, 0, 3, turns)
                up(c + 2, 1, 3, turns, u_rdy)
                pe.wait_ge(aTl_done, m)
                down(c + 4, turns, first, False)

            def item(it, before):
                t0 = it * MOE_TURNS
                back = (lambda tiles: scatter(before, tiles)) if before is not None else (lambda tiles: None)
                pe.wait_ge(gh_done, it * 2 + 2)
                pe.wait_ge(gl_done, it * 2 + 2)
                up(b, 0, 2, t0)
                up(b, 1, 2, t0, g_ready)
                if before is not None:
                    pe.wait_ge(yl_done, before * 2 + 2)
                    pe.wait_ge(selT_done, it)
                back((0, 1))
                for i in range(3):
                    ins = mm(PS[:, 7, 0:2 + ITEMS], sel[:, i, :].bitcast(F32), rg[:, i, :], start=i == 0, stop=i == 2)
                ins.then_inc(table_ready, 1)
                up(b + 2, 0, 3, t0)
                back((2, 3))
                up(b + 2, 1, 3, t0, u_rdy)
                back((4, 5))
                pe.wait_ge(sg_done, it * 7 + 1)
                up(b + 4, 0, 2, t0)
                back((6, 7))
                pe.wait_ge(slot_gate, it + 1)
                for i in range(3):
                    ins = mm(PS[:, 7, 128 + TT * i:128 + TT * i + TT], sel[:, i, :], idr[0:TT, 0:TT], start=True, stop=True)
                ins.then_inc(selT_ready, 1)
                up(b + 4, 1, 2, t0, g_ready)
                rest(b + 4, t0, it * 7 + 1, True)
                with pe.Fori(0, 5) as j:
                    pe.wait_ge(sg_done, it * 7 + 2 + j)
                    up(b + 10, 0, 2, t0 + j)
                    up(b + 10, 1, 2, t0 + j, g_ready)
                    rest(b + 10, t0 + j, it * 7 + 2 + j, False)
                turn(it * 7 + 6)
                after(pe, scat_taken, it * 8)
                gather(it + 1)
                pe.wait_ge(aTl_done, it * 7 + 7)
                down(b + 40, t0, False, True)

            pe.wait_ge(tile_taken, TB[1]["pw"] + 8)
            pe.wait_ge(tokh_done, 6)
            pe.wait_ge(tokl_done, 6)
            gather(0)
            pe.wait_ge(routed, 1)
            n = pe.value_load(passes[0:1, 0:1], min_val=1, max_val=3)
            last = pe.value_load(passes[0:1, 1:2], min_val=NE - 1, max_val=ITEMS - 1)
            item(0, None)
            with pe.Fori(0, last) as before:
                item(before + 1, before)
            pe.wait_ge(yl_done, last * 2 + 2)
            scatter(last, range(KT))
            pe.wait_ge(moe_done, 1)
            ple_pe(pe, chunk, stat, 1, n * (NE * MOE_TURNS))


        @block.tensor
        def _(pe):
            mm = nc.tensor.matmul

            def ready(c, turns=0):
                pe.wait_ge(lo_done, RAW * turns + c + 1)

            def free(p, turns12=0):
                if p >= RING:
                    pe.wait_ge(tile_taken, p - RING + 1 + turns12)
                return PS[:, p % RING, 0:T]

            def three(out, wh, wl, ah, al, first, last, begins=False):
                ins = mm(out, wh, ah, start=first, stop=False)
                if begins:
                    ins.then_inc(chunk_begun, 1)
                mm(out, wh, al, start=False, stop=False)
                return mm(out, wl, ah, start=False, stop=last)

            def chunk(c, p, nk, nt, ah, al, turns=0, turns12=0, each=None):
                ready(c, turns)
                W = nt * 128
                for n in range(nt):
                    out = free(p + n, turns12)
                    for k in range(nk):
                        if each is not None and n == 0:
                            pe.wait_ge(each[0], each[1][k])
                        at = k * W + n * 128
                        ins = three(out, whi[:, c % CAST, at:at + 128], wlo[:, c % CAST, at:at + 128],
                                    ah[:, k, :], al[:, k, :], k == 0, k == nk - 1, n == 0 and k == 0)
                    ins.then_inc(tile_ready, 1)

            def stat(norm):
                pe.wait_ge(sq_ready, norm + 1)
                if norm > 0:
                    pe.wait_ge(ms_ready, turn_of(norm))
                mm(PS[:, 3, 0:T], ones, sacc[:, :], start=True, stop=True).then_inc(stat_ready, 1)

            pe.wait_ge(in_con, 16)
            pe.wait_ge(in_misc, 160)
            nc.tensor.transpose(PS[:, 0, 0:80], vrow, con[0:80, C_ID:C_ID + 80]).then_inc(tile_ready, 1)
            for l in range(DEPTH):
                for k in range(4):
                    ins = nc.tensor.transpose(PS[:, 1, (4 * l + k) * 16:(4 * l + k) * 16 + 16],
                                              crow[:, l, 128 * k:128 * k + 128], con[0:16, C_ID:C_ID + 16])
            ins.then_inc(tile_ready, 1)
            pe.wait_ge(in_x, 48)
            for j in range(KT):
                out = free(2 + j)
                for i in range(3):
                    ins = nc.tensor.transpose(out[:, TT * i:TT * i + TT], xtok[:, i, 128 * j:128 * j + 128],
                                              con[0:TT, C_ID:C_ID + TT])
                ins.then_inc(tile_ready, 1)
            for j in range(4):
                out = free(10 + j)
                for i in range(3):
                    ins = nc.tensor.transpose(out[:, TT * i:TT * i + TT], ptok[:, i, 128 * j:128 * j + 128],
                                              con[0:TT, C_ID:C_ID + TT])
                ins.then_inc(tile_ready, 1)

            n_x = 0
            for l in range(DEPTH):
                b, t = CB[l], TB[l]
                chunk(b["in"], t["in"], 8, 2, xht, xlt, each=x_split(24 * l))
                stat(NORM_OF["in", l])
                chunk(b["in"] + 1, t["in"] + 2, 8, 2, xht, xlt)
                with pe.Fori(0, 2) as it:
                    for s in range(6):
                        chunk(b["in"] + 2 + s, t["in"] + 4 + 2 * s, 8, 2, xht, xlt, turns=it, turns12=12 * it)
                pe.wait_ge(ms_ready, turn_of(NORM_OF["in", l]) + 1)
                pe.wait_ge(cbt_ready, l + 1)
                for k in range(4):
                    ins = nc.tensor.transpose(PS[0:18, 7, 128 * k:128 * k + 128], cbt[:, k, :], ident)
                ins.then_inc(cbT_ready, 1)
                pe.wait_ge(rope_ready, 2 * l + 2)
                pe.wait_ge(tile_taken, t["in"] + 24)
                for s in range(SLOTS):
                    if s > 0 and s <= NH:
                        h, r = s - 1, 4 * l + s - 1
                        pe.wait_ge(ktok_ready, 3 * r + 3)
                        pe.wait_ge(vtok_ready, 2 * r + 2)
                        if h == 0:
                            pe.wait_ge(cout_ready, l + 1)
                        if r > 0:
                            pe.wait_ge(s_new, 2 * r)
                            pe.wait_ge(o_taken, r)

                        def outer(hf):
                            mm(PS[:, 7, :].rearrange("p (b e) -> p b e", b=4), kss, vd[:, 4 * hf:4 * hf + 4, :],
                               start=True, stop=True).then_inc(kv_outer, 1)

                        outer(0)
                        for i in range(2):
                            mm(PS[:, 5, 384:512], ktok[:, 128 * i:128 * i + 128], vtok[:, 128 * i:128 * i + 128],
                               start=i == 0, stop=i == 1)
                        pe.wait_ge(sc_ready, 2 * r + 2)
                        mm(PS[:, 5, 0:256], vtok[:, 0:128], sc[:, 0:256], start=True, stop=False, skip_group_check=True)
                        mm(PS[:, 5, 128:256], vtok[:, 128:256], sc[:, 256:384], start=False, stop=True,
                           skip_group_check=True).then_inc(o_ready, 1)
                        pe.wait_ge(s_new, 2 * r + 1)
                        outer(1)
                    if s < NH + 2:
                        if s > 2:
                            pe.wait_ge(os_taken, 4 * l + s - 2)
                        if s < NH:
                            for i in range(2):
                                nc.tensor.transpose(PS[:, 3, 128 * i:128 * i + 128], Kt[:, s, 128 * i:128 * i + 128], ident)
                            ins = nc.tensor.transpose(PS[0:8, 3, 256:384], Kt[:, s, SEQ:T], ident)
                        if s >= 2:
                            r = 4 * l + s - 2
                            pe.wait_ge(s_new, 2 * r + 2)
                            for i in range(NB):
                                ins = mm(PS[:, 3, 384 + i:385 + i], St[r % 2][:, 128 * i:128 * i + 128],
                                         Qt[:, s - 2, SEQ + i:SEQ + i + 1], start=True, stop=True)
                        ins.then_inc(bank3_ready, 1)
                    if s < NH:
                        for i in range(2):
                            nc.tensor.transpose(PS[:, 6, 128 * i:128 * i + 128], Vt[:, s, 128 * i:128 * i + 128], ident)
                        nc.tensor.transpose(PS[0:8, 6, 256:384], Vt[:, s, SEQ:T], ident).then_inc(vT_ready, 1)
                        mm(PS[:, 4, 0:256], Kt[:, s, 0:128], Qt[:, s, 0:256], start=True, stop=True)
                        mm(PS[:, 4, 256:384], Kt[:, s, 128:256], Qt[:, s, 128:256], start=True, stop=True).then_inc(score_ready, 1)
                    if s == 6:
                        pe.wait_ge(os_taken, 4 * l + 4)
                        pe.wait_ge(o_taken, 4 * l + 4)
                        for h in range(NH):
                            ins = mm(PS[:, 4 + h, 0:T], centre, Qt[:, h, :], start=True, stop=True)
                        ins.then_inc(cent_ready, 1)
                    if s == 7:
                        pe.wait_ge(osq_ready, l + 1)
                        for h in range(NH):
                            for i in range(3):
                                ins = mm(PS[0:TT, 3, 3 * h + i:3 * h + i + 1], rtmp[:, h, TT * i:TT * i + TT],
                                         ones[:, 0:1], start=True, stop=True)
                        ins.then_inc(var_ready, 1)
                    if s == 8:
                        pe.wait_ge(diag_ready, l + 1)
                        for h in range(NH):
                            ins = mm(PS[:, 4 + h, 0:T], ones[0:TT, :], diag[:, 3 * h:3 * h + 3, :], start=True, stop=True)
                        ins.then_inc(rsb_ready, 1)
                    if s < 2:
                        if s == 0:
                            pe.wait_ge(a_lo, l + 1)
                        chunk(b["conv"] + s, t["conv"] + 4 * s, 4, 4, frt[:, 0:4, :], frt[:, 4:8, :])
                    else:
                        chunk(b["gate"] + s - 2, t["gate"] + 2 * s - 4, 8, 2, xht, xlt)
                pe.wait_ge(r_lo, l + 1)
                for i in range(2):
                    chunk(b["ret"] + i, t["ret"] + 4 * i, 4, 4, frt[:, 0:4, :], frt[:, 4:8, :])
                for i in range(4):
                    chunk(b["o"] + i, t["o"] + 2 * i, 8, 2, frt[:, 8:16, :], frt[:, 16:24, :],
                          each=(m_lo, [8 * l + k + 1 for k in range(8)]) if i == 0 else None)
                if l == 0:
                    for hf in range(2):
                        c0, t0 = b["ffn"] + 22 * hf, t[f"gu{hf}"]
                        if hf == 0:
                            chunk(c0, t0, 8, 2, xht, xlt, each=x_split(8))
                            stat(1)
                        else:
                            chunk(c0, t0, 8, 2, xht, xlt)
                        chunk(c0 + 1, t0 + 2, 8, 2, xht, xlt)
                        with pe.Fori(0, 2) as it:
                            for s in range(6):
                                chunk(c0 + 2 + s, t0 + 4 + 2 * s, 8, 2, xht, xlt, turns=it, turns12=12 * it)
                        for i in range(8):
                            chunk(c0 + 14 + i, t[f"down{hf}"] + i, 14, 1, frt[:, 0:14, :], frt[:, 14:28, :],
                                  each=(f_lo, [7 * hf + k // 2 + 1 for k in range(14)]) if i == 0 else None)
                    pw_pe(chunk, 0)
                    ple_pe(pe, chunk, stat, 0)
                else:
                    moe_pe(pe, ready, three, chunk, stat)
            stat(6)
            pe.wait_ge(fin_ready, 8)
            for i in range(3):
                for hf in range(2):
                    if i > 0:
                        pe.wait_ge(out_ready, 2 * i + hf - 1)
                    for k in range(4):
                        ins = nc.tensor.transpose(PS[0:TT, 4 + hf, 128 * k:128 * k + 128],
                                                  x[:, 4 * hf + k, TT * i:TT * i + TT], ident)
                    ins.then_inc(finT_ready, 1)


_INS = ["x_prompt", "x_sample", "state_conv", "state_ret", "p_prompt", "p_sample", "norm_mix_g", "w_in",
        "conv_w", "w_conv_out", "w_ret_out", "w_o", "norm_ffn_g", "w_dense_gu", "w_dense_down",
        "w_router", "w_exp_gu", "w_exp_down", "norm_ple_g", "w_ple", "w_ple_gate", "norm_final_g"]
_OUTS = [("y_prompt", (1, SEQ, D)), ("y_sample", (NB, 1, D)), ("conv_prompt", (DEPTH, 1, CW - 1, DC)),
         ("ret_prompt", (DEPTH, 1, NH, DK, DK)), ("conv_sample", (DEPTH, NB, CW - 1, DC)),
         ("ret_sample", (DEPTH, NB, NH, DK, DK))]


def kernel(**inputs):
    import concourse.bacc as bacc
    from concourse.bass_utils import run_bass_kernel_spmd

    nc = bacc.Bacc("TRN2", target_bir_lowering=False, num_devices=1)
    arrays, A, O = {}, {}, {}
    given = {name: np.ascontiguousarray(inputs[name]) for name in _INS}
    given["constants"] = constants()
    for name, a in given.items():
        arrays[f"in_{name}"] = a
        A[name] = nc.dram_tensor(f"in_{name}", a.shape, mybir.dt.from_np(a.dtype), kind="ExternalInput").ap()
    for name, shape in _OUTS:
        O[name] = nc.dram_tensor(f"out_{name}", shape, mybir.dt.float32, kind="ExternalOutput").ap()
    program(nc, A, O)
    r = run_bass_kernel_spmd(nc, [arrays], core_ids=[0])
    return tuple(r.results[0][f"out_{name}"] for name, _ in _OUTS)
```

```python
import numpy as np
import concourse.bass as bass
from concourse import mybir
from contextlib import ExitStack

D = 1024
SEQ = 256
NB = 8
T = SEQ + NB
KT = D // 128
DC = 512
NH = 4
DK = 128
DR = NH * DK
DFF = 3584
NE = 8
DEPTH = 2
CW = 3
EPS = 1e-6
PAST = 2048
TT = 88
CH = 2048
RAW, CAST = 6, 3
AHEAD = 2
RING = 3

C_ID, C_ONE, C_CENT = 0, 128, 256
C_COS, C_SIN = 384, 384 + T
C_DEC = C_SIN + T
C_KD = C_DEC + NH * SEQ
C_EYE8 = C_KD + NH * 2
C_IOTA = C_EYE8 + 8
C_TRI = C_IOTA + 128
NCONST = C_TRI + TT

GAMMA = [1.0 - 2.0 ** (-5.0 - h) for h in range(NH)]


def constants():
    c = np.zeros((128, NCONST), np.float32)
    c[:, C_ID:C_ID + 128] = np.eye(128)
    c[:, C_ONE:C_ONE + 128] = 1.0
    c[:, C_CENT:C_CENT + 128] = np.eye(128) - 1.0 / DK
    half = DK // 2
    inv = (10000.0 ** (-np.arange(half) / half)).astype(np.float32)
    pos = np.concatenate([np.arange(SEQ), np.full(NB, PAST)]).astype(np.float32)
    ang = (pos[None, :] * inv[:, None]).astype(np.float32).astype(np.float64)
    c[:half, C_COS:C_COS + T] = np.cos(ang)
    c[half:, C_COS:C_COS + T] = np.cos(ang)
    c[:half, C_SIN:C_SIN + T] = np.sin(ang)
    c[half:, C_SIN:C_SIN + T] = -np.sin(ang)
    m = np.arange(128)[:, None]
    l = np.arange(SEQ)[None, :]
    s = DK ** -0.5
    for h in range(NH):
        lg = float(np.log(np.float32(GAMMA[h])))
        d = np.where(l >= m, np.exp(np.maximum(l - m, 0) * lg), 0.0) * s
        c[:, C_DEC + h * SEQ:C_DEC + (h + 1) * SEQ] = d
        for i in range(2):
            c[:, C_KD + 2 * h + i] = np.exp((SEQ - 1 - 128 * i - m[:, 0]) * lg) * s
    c[:8, C_EYE8:C_EYE8 + 8] = np.eye(8)
    c[:, C_IOTA:C_IOTA + 128] = np.arange(128)[None, :]
    t = np.arange(TT)
    c[:TT, C_TRI:C_TRI + TT] = (t[:, None] < t[None, :])
    return c


def chunk_bases():
    b, at = [], 0
    for l in range(DEPTH):
        s = {}
        for name, n in (("in", 14), ("conv", 2), ("gate", 8), ("ret", 2), ("pw", 1), ("o", 4)):
            s[name] = at
            at += n
        s["ffn"] = at
        s["pg"] = at + (44 if l == 0 else 0)
        at = s["pg"] + 4
        b.append(s)
    return b


CB = chunk_bases()
MOE_CHUNKS = 42
MOE_TURNS = MOE_CHUNKS // RAW
SLOTS = 10
ITEMS = 3 * NE


def tile_bases():
    b, at = [], 10
    for l in range(DEPTH):
        s = {}
        rows = [("in", 28), ("conv", 8), ("gate", 16), ("ret", 8), ("pw", 8), ("o", 8)]
        if l == 0:
            rows += [("gu0", 28), ("down0", 8), ("gu1", 28), ("down1", 8)]
        for name, n in rows + [("pg", 8)]:
            s[name] = at
            at += n
        b.append(s)
    return b


TB = tile_bases()
NORM_OF = {("in", 0): 0, ("ffn", 0): 1, ("ple", 0): 2, ("in", 1): 3, ("ffn", 1): 4, ("ple", 1): 5}
GAIN = {0: 0, 3: 8, 1: 16, 4: 24, 2: 32, 5: 40, 6: 48}
CONVW = 56


def program(nc, A, O):
    F32, F32R, I32, U32 = mybir.dt.float32, mybir.dt.float32r, mybir.dt.int32, mybir.dt.uint32
    ALU, ACT = mybir.AluOpType, mybir.ActivationFunctionType
    ds = bass.ds
    es = ExitStack()
    with es:
        def sb(name, shape, dt=F32):
            return es.enter_context(nc.sbuf_tensor(name, shape, dt))

        def sem(name):
            return es.enter_context(nc.semaphore(name))

        raw = sb("raw", [128, RAW, CH])
        whi = sb("whi", [128, CAST, CH], F32R)
        wlo = sb("wlo", [128, CAST, CH], F32R)
        x = sb("x", [128, KT, T])
        xh = sb("xh", [128, KT * T], F32R)
        xl = sb("xl", [128, KT * T], F32R)
        z = sb("z", [128, 28 * T])
        con = sb("con", [128, NCONST])
        idr = sb("idr", [128, 128], F32R)
        vec = sb("vec", [128, 80])
        cst = sb("cst", [128, DEPTH, 4, 16])
        ph = sb("ph", [128, 4, T], F32R)
        pl = sb("pl", [128, 4, T], F32R)
        ub = sb("ub", [128, 4, 2 + SEQ])
        us = sb("us", [128, 4, NB])
        cbt = sb("cbt", [128, 4, 18])
        rstd = sb("rstd", [128, T])
        sq = sb("sq", [128, T])
        sacc = sb("sacc", [128, T])
        FR = 28 * T
        fr_at = nc.sbuf_usable_end - FR * 4
        fr_at -= fr_at % 32
        fr = nc.alloc_sbuf_tensor_at("fr", [128, FR], F32R, offset=fr_at)
        scr = nc.alloc_sbuf_tensor_at("scr", [128, 20 * T], F32, offset=fr_at + 8 * T * 4)
        PS = es.enter_context(nc.psum_tensor("PS", [128, 8, 512], F32))

        ident = con[:, C_ID:C_ID + 128]
        ones = con[:, C_ONE:C_ONE + 128]
        centre = con[:, C_CENT:C_CENT + 128]
        cos = con[:, C_COS:C_COS + T]
        sin = con[:, C_SIN:C_SIN + T]
        dec = con[:, C_DEC:C_DEC + NH * SEQ].rearrange("p (h l) -> p h l", h=NH)
        kd = con[:, C_KD:C_KD + 8]
        eye8 = con[0:8, C_EYE8:C_EYE8 + 8]
        iota = con[0:TT, C_IOTA:C_IOTA + 128]
        iota8 = con[0:TT, C_IOTA:C_IOTA + 8]
        tri = con[0:TT, C_TRI:C_TRI + TT]

        zt = z[:, :].rearrange("p (t c) -> p t c", c=T)
        frt = fr[:, :].rearrange("p (t c) -> p t c", c=T)
        xht = xh[:, :].rearrange("p (t c) -> p t c", c=T)
        xlt = xl[:, :].rearrange("p (t c) -> p t c", c=T)
        xtok = z[0:TT, 0:3 * D].rearrange("p (t f) -> p t f", t=3)
        ptok = scr[0:TT, 0:3 * 512].rearrange("p (t f) -> p t f", t=3)
        vrow = z[0:56, 4608:4736]
        wrow = z[0:24, 5760:5888]
        crow = z[0:16, 4736:4736 + 1024].rearrange("p (l f) -> p l f", l=DEPTH)
        CBt, CCt, CHt = zt[:, 0:4, :], zt[:, 4:8, :], zt[:, 8:12, :]
        Qt, Kt, Vt, Gt = zt[:, 12:16, :], zt[:, 16:20, :], zt[:, 20:24, :], zt[:, 24:28, :]
        rtmp = scr[:, 0:4 * T].rearrange("p (h t) -> p h t", h=4)
        ktok, vtok = scr[:, 0:256], scr[:, 256:512]
        sc = scr[:, 512:896]
        vd = scr[0:8, 896:1920].rearrange("p (b e) -> p b e", b=8)
        kss = scr[0:8, 1920:2048]
        St = [scr[:, 2112 + 1024 * i:3136 + 1024 * i] for i in range(2)]
        so = scr[:, 4160:4672].rearrange("p (h e) -> p h e", h=4)
        cout = scr[0:18, 4672:5184]
        diag = scr[0:TT, 1056:2112].rearrange("p (n c) -> p n c", c=TT)
        gdiag = scr[:, 0:1024].rearrange("p (k c) -> p k c", k=KT)
        frs = sb("frs", [TT, 3, 3])
        FIN_BANK = ((3, 4), (5, 6), (7, 0))
        gstat = scr[0:TT, 5184:5208].rearrange("p (a n) -> p a n", a=2)
        htok_h = fr[0:TT, 0:3072].rearrange("p (t f) -> p t f", t=3)
        htok_l = fr[0:TT, 3072:6144].rearrange("p (t f) -> p t f", t=3)
        actT_h, actT_l = fr[:, 6144:6656], fr[:, 6656:7168]
        gx = z[:, 3072:3072 + D]
        gh, gl = xh[:, 0:D], xl[:, 0:D]
        yh, yl = xh[:, D:2 * D], xl[:, D:2 * D]
        sel = ph[0:TT, 0:2, :].rearrange("p a t -> p (a t)")[:, 0:384].rearrange("p (i s) -> p i s", i=3)
        selT = pl[:, 0, :]
        sgm, aam = z[:, 0:512], z[:, 512:1024]
        wrr = sb("wrr", [128, 64])
        rt = z[0:TT, 1600:2200]
        wrh = sb("wrh", [128, 64], F32R)
        wrl = sb("wrl", [128, 64], F32R)
        lgT = z[0:NE, 2400:2400 + T]
        posm = sb("posm", [TT, 3, ITEMS + 1])
        rg = sb("rg", [TT, 3, 2 + ITEMS])
        srs = sb("srs", [128, 1])
        passes = sb("passes", [1, 2], I32)
        idx = sb("idx", [TT, 3, 8], U32)

        raw_landed = [sem(f"raw_landed{i}") for i in range(RAW)]
        hi_done, lo_done, chunk_begun = sem("hi_done"), sem("lo_done"), sem("chunk_begun")
        in_con, in_id, in_x, in_wr = sem("in_con"), sem("in_id"), sem("in_x"), sem("in_wr")
        in_vec, in_crow, in_p, p_ready, p_lo = (sem("in_vec"), sem("in_crow"), sem("in_p"),
                                                sem("p_ready"), sem("p_lo"))
        tile_ready, tile_taken = sem("tile_ready"), sem("tile_taken")
        idr_done, pad_done = sem("idr_done"), sem("pad_done")
        p_hi = sem("p_hi")
        x_ready, xh_ready, xl_ready = sem("x_ready"), sem("xh_ready"), sem("xl_ready")
        pool_chain, dve_chain = sem("pool_chain"), sem("dve_chain")
        sq_ready, stat_ready, root_ready, rstd_ready = (sem("sq_ready"), sem("stat_ready"),
                                                        sem("root_ready"), sem("rstd_ready"))
        u_ready, y_conv, a32, a_hi, a_lo = (sem("u_ready"), sem("y_conv"), sem("a32"), sem("a_hi"),
                                            sem("a_lo"))
        cbt_ready, cbT_ready, cout_ready, cout_sent = (sem("cbt_ready"), sem("cbT_ready"),
                                                       sem("cout_ready"), sem("cout_sent"))
        rope_ready, bank3_ready, vT_ready, ktok_ready, vtok_ready = (
            sem("rope_ready"), sem("bank3_ready"), sem("vT_ready"), sem("ktok_ready"), sem("vtok_ready"))
        score_ready, sc_ready, so_ready, so_sent = (
            sem("score_ready"), sem("sc_ready"), sem("so_ready"), sem("so_sent"))
        kv_outer, s_new = sem("kv_outer"), sem("s_new")
        s_in = [sem("s_in0"), sem("s_in1")]
        s_sent = [sem("s_sent0"), sem("s_sent1")]
        o_ready, o_taken, os_taken, cent_ready, oc_ready, osq_ready, og_ready = (
            sem("o_ready"), sem("o_taken"), sem("os_taken"), sem("cent_ready"), sem("oc_ready"),
            sem("osq_ready"), sem("og_ready"))
        var_ready, groot_ready, diag_ready, rsb_ready = (
            sem("var_ready"), sem("groot_ready"), sem("diag_ready"), sem("rsb_ready"))
        gsilu_ready, r32, r_hi, r_lo = sem("gsilu_ready"), sem("r32"), sem("r_hi"), sem("r_lo")
        gsig, a_gated, m32, m_hi, m_lo = sem("gsig"), sem("a_gated"), sem("m32"), sem("m_hi"), sem("m_lo")
        f_silu, f_act, f_hi, f_lo = sem("f_silu"), sem("f_act"), sem("f_hi"), sem("f_lo")
        psig = sem("psig")
        wr_hi, wr_lo = sem("wr_hi"), sem("wr_lo")
        tok_ready, tokh_done, tokl_done = sem("tok_ready"), sem("tokh_done"), sem("tokl_done")
        logit_ready, route_act, route_dve, rank_ready, routed = (
            sem("logit_ready"), sem("route_act"), sem("route_dve"), sem("rank_ready"), sem("routed"))
        sel_ready, gath_ready, gx_left, gx_right = (sem("sel_ready"), sem("gath_ready"), sem("gx_left"),
                                                    sem("gx_right"))
        gT_ready, gh_done, gl_done = sem("gT_ready"), sem("gh_done"), sem("gl_done")
        table_ready, slot_rs, slot_gate, selT_ready, selT_done = (
            sem("table_ready"), sem("slot_rs"), sem("slot_gate"), sem("selT_ready"), sem("selT_done"))
        g_ready, u_rdy, sg_done, aa_done = (sem("g_ready"), sem("u_rdy"), sem("sg_done"), sem("aa_done"))
        aT_ready, aTh_done, aTl_done = sem("aT_ready"), sem("aTh_done"), sem("aTl_done")
        y_ready, yh_done, yl_done = sem("y_ready"), sem("yh_done"), sem("yl_done")
        scat_ready, scat_taken, moe_done = sem("scat_ready"), sem("scat_taken"), sem("moe_done")
        gdiag_done, finT_ready, frs_ready, out_left, out_right, out_sent = (
            sem("gdiag_done"), sem("finT_ready"), sem("frs_ready"), sem("out_left"),
            sem("out_right"), sem("out_sent"))
        sq2_ready, lgT_ready, lgT_done, count_ready = (sem("sq2_ready"), sem("lgT_ready"),
                                                       sem("lgT_done"), sem("count_ready"))

        sq_root = sb("sq_root", [128, T])
        nwt = sb("nwt", [128, T])
        epsb = sb("epsb", [128, 1])
        sgate = sb("sgate", [128, 1])
        eps_done, pprod = sem("eps_done"), sem("pprod")
        ms_ready = sem("ms_ready")

        def x_at(norm, j):
            if norm == 5:
                return moe_done, 1
            if norm in (3, 6):
                return x_ready, 8 * (norm // 3 - 1) + j + 1
            base = {0: 1, 1: TB[0]["o"], 2: TB[0]["down1"], 4: TB[1]["o"]}[norm]
            return tile_taken, base + j + 1

        def turn_of(norm):
            return norm if norm < 4 else norm - 1

        assert nc.sbuf_base <= fr_at, (nc.sbuf_base, fr_at)
        block = es.enter_context(nc.Block())

        def ple_loads(sp, load, rows, l, turns):
            b = CB[l]
            for i in range(4):
                load(b["pg"] + i, rows(A["w_ple_gate"][l], 8)[:, :, 256 * i:256 * i + 256], turns)


        def moe_loads(sp, load, ps):
            b = CB[1]["ffn"]
            gu = A["w_exp_gu"].rearrange("o e (k p) n -> (o e) p k n", p=128)
            dn = A["w_exp_down"].rearrange("o e (k p) n -> (o e) p k n", p=128)
            with sp.Fori(0, NE) as e:
                t0 = (ps * NE + e) * MOE_TURNS

                def up(c, s, j, turns):
                    col = (s // 2) * DFF
                    src = gu[ds(e, 1), :, 4 * (s % 2):4 * (s % 2) + 4, ds(j * 512 + col, 512)]
                    load(c, src.rearrange("o p k n -> (o p) k n"), turns)

                def down(c, s, j, turns):
                    src = dn[ds(e, 1), :, ds(j * 4 + 2 * s, 2), :]
                    load(c, src.rearrange("o p k n -> (o p) k n"), turns)

                for s in range(4):
                    up(b + s, s, 0, t0)
                with sp.Fori(0, 6) as i:
                    for s in range(4):
                        up(b + 4 + s, s, i + 1, t0 + i)
                    for s in range(2):
                        down(b + 8 + s, s, i, t0 + i)
                for s in range(2):
                    down(b + 40 + s, s, 6, t0)


        def ffn_tiles(q):
            q = q % 3
            return [zt[:, 6 * q + 2 * i:6 * q + 2 * i + 2, :] for i in range(3)]


        @block.sync
        def _(sp):
            def load(c, src, turns=0, width=CH):
                if not (isinstance(turns, int) and c + RAW * turns < RAW):
                    sp.wait_ge(lo_done, (turns - 1) * RAW + c + 1)
                k = src.shape[1] if len(src.shape) == 3 else 1
                dst = raw[:, c % RAW, 0:width].rearrange("p (k n) -> p k n", k=k)
                sp.dma_start(dst, src).then_inc(raw_landed[c % RAW], 16)

            sp.dma_start(con[:, 0:256], A["constants"][:, 0:256]).then_inc(in_id, 16)
            xp = A["x_prompt"].rearrange("b t f -> (b t) f")
            xs = A["x_sample"].rearrange("b t f -> (b t) f")
            sp.dma_start(xtok[:, 0:2, :], xp[0:2 * TT, :].rearrange("(i p) f -> p i f", p=TT)).then_inc(in_x, 16)
            sp.dma_start(xtok[0:SEQ - 2 * TT, 2, :], xp[2 * TT:SEQ, :]).then_inc(in_x, 16)
            sp.dma_start(xtok[SEQ - 2 * TT:TT, 2, :], xs).then_inc(in_x, 16)

            def rows(w, nk):
                return w.rearrange("(k p) n -> p k n", p=128)[:, 0:nk, :]

            for l in range(DEPTH):
                b = CB[l]
                win = rows(A["w_in"][l], 8)
                if l == 0:
                    for i in range(14):
                        load(b["in"] + i, win[:, :, 256 * i:256 * i + 256])
                        if i == 1:
                            sp.dma_start(con[:, 256:], A["constants"][:, 256:]).then_inc(in_con, 16)
                else:
                    for i in range(2):
                        load(b["in"] + i, win[:, :, 256 * i:256 * i + 256])
                    with sp.Fori(0, 2) as it:
                        for s in range(6):
                            load(b["in"] + 2 + s, win[:, :, ds(it * 1536 + 512 + 256 * s, 256)], it)
                for i in range(2):
                    load(b["conv"] + i, rows(A["w_conv_out"][l], 4)[:, :, 512 * i:512 * i + 512])
                for i in range(8):
                    at = 3 * DC + 4 * DR + 256 * i
                    load(b["gate"] + i, win[:, :, at:at + 256])
                for i in range(2):
                    load(b["ret"] + i, rows(A["w_ret_out"][l], 4)[:, :, 512 * i:512 * i + 512])
                load(b["pw"], rows(A["w_ple"][l], 2))
                for i in range(4):
                    load(b["o"] + i, rows(A["w_o"][l], 8)[:, :, 256 * i:256 * i + 256])
                if l == 0:
                    gu = rows(A["w_dense_gu"][0], 8)
                    dn = A["w_dense_down"][0].rearrange("(k p) n -> p k n", p=128)
                    for hf in range(2):
                        c0 = b["ffn"] + 22 * hf
                        for i in range(2):
                            load(c0 + i, gu[:, :, DFF * i + 1792 * hf:][:, :, 0:256])
                        with sp.Fori(0, 2) as it:
                            for s in range(6):
                                at = (s % 2) * DFF + 1792 * hf + 256 * (1 + s // 2)
                                load(c0 + 2 + s, gu[:, :, ds(it * 768 + at, 256)], it)
                        for i in range(8):
                            load(c0 + 14 + i, dn[:, 14 * hf:14 * hf + 14, 128 * i:128 * i + 128],
                                 width=14 * 128)
                    ple_loads(sp, load, rows, l, 0)
                else:
                    moe_loads(sp, load, 0)
                    sp.wait_ge(routed, 1)
                    n = sp.value_load(passes[0:1, 0:1], min_val=1, max_val=3)
                    with sp.If(n > 1):
                        with sp.Fori(1, n) as ps:
                            moe_loads(sp, load, ps)
                    with sp.Else():
                        sp.nop()
                    ple_loads(sp, load, rows, l, n * (NE * MOE_TURNS))
            for i in range(3):
                for hf, half in enumerate((out_left, out_right)):
                    cols = slice(512 * hf, 512 * hf + 512)
                    sp.wait_ge(half, i + 1)
                    if i < 2:
                        sp.dma_start(O["y_prompt"][0, TT * i:TT * i + TT, cols], xtok[:, i, cols]).then_inc(out_sent, 16)
                    else:
                        sp.dma_start(O["y_prompt"][0, 2 * TT:SEQ, cols], xtok[0:80, 2, cols]).then_inc(out_sent, 16)
                        sp.dma_start(O["y_sample"][:, 0, cols], xtok[80:88, 2, cols]).then_inc(out_sent, 16)
            sp.wait_ge(out_sent, 128)

        @block.gpsimd
        def _(pool):
            n_chain = [0]

            def link(ins):
                n_chain[0] += 1
                ins.then_inc(pool_chain, 1)
                pool.wait_ge(pool_chain, n_chain[0])

            def squares(norm):
                tiles = {0: 5, 5: 5, 6: 6}.get(norm, KT)
                for j in range(tiles):
                    pool.wait_ge(*x_at(norm, j))
                    if j == 0:
                        if norm not in (0, 5):
                            pool.wait_ge(stat_ready, turn_of(norm))
                        link(pool.tensor_tensor(sacc[:, :], x[:, 0, :], x[:, 0, :], ALU.mult))
                    else:
                        link(pool.tensor_tensor(sq[:, :], x[:, j, :], x[:, j, :], ALU.mult))
                        ins = pool.tensor_tensor(sacc[:, :], sacc[:, :], sq[:, :], ALU.add)
                        if j == tiles - 1:
                            ins.then_inc(sq_ready, 1)
                            pool.wait_ge(sq_ready, norm + 1)
                        else:
                            link(ins)

            pp = A["p_prompt"].rearrange("l b t f -> (b t) l f")
            ps_ = A["p_sample"].rearrange("l b t f -> (b t) l f")
            for i in range(2):
                pool.dma_start(ptok[:, i, :].rearrange("p (l f) -> p l f", l=2), pp[TT * i:TT * i + TT]).then_inc(in_p, 16)
            pool.dma_start(ptok[0:80, 2, :].rearrange("p (l f) -> p l f", l=2), pp[2 * TT:SEQ]).then_inc(in_p, 16)
            pool.dma_start(ptok[80:88, 2, :].rearrange("p (l f) -> p l f", l=2), ps_).then_inc(in_p, 16)
            pool.dma_start(wrr[:, :].rearrange("p (k n) -> p k n", n=NE), A["w_router"][0].rearrange("(k p) n -> p k n", p=128)).then_inc(in_wr, 16)
            pool.memset(ub[:, :, 0:2], 0.0).then_inc(pad_done, 1)
            pool.wait_ge(pad_done, 1)
            squares(0)
            for l in range(DEPTH):
                t = TB[l]
                if l > 0:
                    pool.wait_ge(chunk_begun, CB[l]["in"] + 1)
                    pool.wait_ge(so_sent, 16 * l)
                    pool.wait_ge(cout_sent, 32 * l)

                def load_state(h):
                    r = 4 * l + h
                    if r >= 2:
                        pool.wait_ge(s_sent[r % 2], 16 * (r // 2))
                        pool.wait_ge(bank3_ready, 6 * l + h + 1 if h >= 2 else 6 * l - 6 + h + 5)
                    pool.dma_start(St[r % 2].rearrange("p (b e) -> p b e", b=8),
                                   A["state_ret"][l, :, h, :, :].rearrange("b d e -> d b e")).then_inc(s_in[r % 2], 16)

                load_state(0)
                load_state(1)
                pool.wait_ge(tile_taken, t["in"] + 12)
                if l > 0:
                    pool.wait_ge(y_conv, l)
                    pool.wait_ge(cbt_ready, l)
                pool.tensor_tensor(ub[:, :, 2:2 + SEQ], CCt[:, :, 0:SEQ], CHt[:, :, 0:SEQ], ALU.mult).then_inc(u_ready, 1)
                pool.tensor_tensor(us[:, :, :], CCt[:, :, SEQ:T], CHt[:, :, SEQ:T], ALU.mult).then_inc(u_ready, 1)
                pool.wait_ge(u_ready, 2 * l + 2)
                if l > 0:
                    pool.wait_ge(cbT_ready, l)
                new = cbt[:, :, 2:18].rearrange("p k (b w) -> p k b w", w=2)
                old = cst[:, l, :, :].rearrange("p k (b w) -> p k b w", w=2)
                pool.tensor_copy(cbt[:, :, 0:2], ub[:, :, SEQ:SEQ + 2]).then_inc(pad_done, 1)
                pool.tensor_copy(new[:, :, :, 0], old[:, :, :, 1]).then_inc(pad_done, 1)
                pool.tensor_copy(new[:, :, :, 1], us[:, :, :]).then_inc(pad_done, 1)
                pool.wait_ge(pad_done, 1 + 3 * (l + 1))
                pool.nop().then_inc(cbt_ready, 1)
                pool.wait_ge(y_conv, l + 1)
                pool.tensor_tensor(CHt, CBt, CCt, ALU.mult).then_inc(a32, 1)
                pool.wait_ge(cout_ready, l + 1)
                pool.dma_start(O["conv_prompt"][l, 0, :, :], cout[0:2, :]).then_inc(cout_sent, 16)
                pool.dma_start(O["conv_sample"][l].rearrange("b w c -> (b w) c"), cout[2:18, :]).then_inc(cout_sent, 16)
                for h in range(NH):
                    r = 4 * l + h
                    pool.wait_ge(s_new, 2 * r + 2)
                    pool.dma_start(O["ret_sample"][l, :, h, :, :].rearrange("b d e -> d b e"),
                                   St[r % 2].rearrange("p (b e) -> p b e", b=8)).then_inc(s_sent[r % 2], 16)
                    if h + 2 < NH:
                        load_state(h + 2)
                pool.wait_ge(so_ready, 4 * l + 4)
                pool.dma_start(O["ret_prompt"][l, 0, :, :, :].rearrange("h d e -> d h e"), so).then_inc(so_sent, 16)
                pool.wait_ge(oc_ready, l + 1)
                pool.tensor_tensor(rtmp, Qt, Qt, ALU.mult).then_inc(osq_ready, 1)
                pool.wait_ge(gsilu_ready, l + 1)
                pool.tensor_tensor(Qt, Qt, Gt, ALU.mult).then_inc(og_ready, 1)
                pool.wait_ge(a_gated, 8 * (l + 1))
                for j in range(KT):
                    pool.wait_ge(tile_taken, t["ret"] + j + 1)
                    pool.tensor_tensor(zt[:, j, :], zt[:, j, :], zt[:, 16 + j, :], ALU.add).then_inc(m32, 1)
                squares(1 + 3 * l)
                if l == 0:
                    squares(2)
                    squares(3)
            squares(5)
            squares(6)
            pool.wait_ge(cout_sent, 32 * DEPTH)
            pool.wait_ge(so_sent, 16 * DEPTH)
            for i in range(2):
                pool.wait_ge(s_sent[i], 16 * 2 * DEPTH)

        def dense_act(act, cast, root, split_x):
            b, t = CB[0], TB[0]

            def pair(q, c, tile, turns=0):
                gb = ffn_tiles(q)[0]
                cast(c + AHEAD, turns)
                act.wait_ge(tile_taken, tile + 2 + 12 * turns)
                nc.scalar.activation(gb, gb, ACT.Silu).then_inc(f_silu, 1)
                cast(c + 1 + AHEAD, turns)

            def hi(q, pos, turns=0):
                act.wait_ge(f_act, 1 + q + 3 * turns)
                dst = frt[:, ds(turns * 6 + 2 * pos, 2), :]
                nc.scalar.activation(dst, ffn_tiles(q)[2], ACT.Copy).then_inc(f_hi, 1)

            for hf in range(2):
                c0 = b["ffn"] + 22 * hf
                t0 = t[f"gu{hf}"]
                if hf == 0:
                    cast(c0 + AHEAD)
                    root(1)
                    act.wait_ge(tile_taken, t0 + 2)
                    nc.scalar.activation(ffn_tiles(0)[0], ffn_tiles(0)[0], ACT.Silu).then_inc(f_silu, 1)
                    cast(c0 + 1 + AHEAD)
                else:
                    pair(7, c0, t0)
                with act.Fori(0, 2) as it:
                    for q in range(3):
                        pair(7 * hf + 1 + q, c0 + 2 + 2 * q, t0 + 4 + 4 * q, it)
                        hi(7 * hf + q, q, it)
                hi(7 * hf + 6, 6)
                for i in range(8):
                    cast(c0 + 14 + i + AHEAD)
                    if hf == 1 and i > 0:
                        split_x(2, (i - 1,))
            split_x(2, (7,))


        def ple_act(act, cast, root, split_x, l, turns=0):
            b, t = CB[l], TB[l]
            last = l == DEPTH - 1
            norm = NORM_OF["ple", l]

            def sigmoids(i):
                for j in (2 * i, 2 * i + 1):
                    act.wait_ge(tile_taken, t["pg"] + j + 1)
                    nc.scalar.activation(zt[:, 8 + j, :], zt[:, 8 + j, :], ACT.Sigmoid).then_inc(psig, 1)

            for i in range(4):
                if not (last and i + AHEAD >= 4):
                    cast(b["pg"] + i + AHEAD, turns)
                if i == 0:
                    root(norm)
                if last and i == 1:
                    for k in range(KT):
                        nc.scalar.activation(gdiag[:, k, :], ident, ACT.Copy,
                                             scale=vec[:, GAIN[6] + k:GAIN[6] + k + 1]).then_inc(gdiag_done, 1)
                if i > 0:
                    sigmoids(i - 1)
            sigmoids(3)
            if not last:
                act.wait_ge(tile_ready, t["pg"] + 8)
                split_x(3)


        def after(eng, sem_, n):
            if not (isinstance(n, int) and n <= 0):
                eng.wait_ge(sem_, n)


        def moe_act(act, cast, root, split_x):
            b = CB[1]["ffn"]
            act.wait_ge(in_wr, 16)
            nc.scalar.activation(wrh[:, :], wrr[:, :], ACT.Copy).then_inc(wr_hi, 1)
            act.wait_ge(logit_ready, 1)
            nc.scalar.activation(rt[:, 0:3], PS[0:TT, 7, 24:27], ACT.Sqrt, bias=epsb[0:TT, :],
                                 scale=1.0 / D).then_inc(route_act, 1)
            def token(i):
                act.wait_ge(tok_ready, 2 * i + 1)
                nc.scalar.activation(htok_h[:, i // 2, 512 * (i % 2):512 * (i % 2) + 512],
                                     PS[0:TT, 3 + i % 2, :], ACT.Copy).then_inc(tokh_done, 1)

            for i in range(6):
                token(i)
            act.wait_ge(route_dve, 1)
            nc.scalar.activation(rt[:, 60:66], rt[:, 54:60], ACT.Exp).then_inc(route_act, 1)

            def gathered(it):
                act.wait_ge(gath_ready, it * 2 + 1)
                nc.scalar.activation(gx[:, 0:512], PS[:, 5, :], ACT.Copy).then_inc(gx_left, 1)

            def turned(it):
                for i in range(2):
                    act.wait_ge(gT_ready, it * 2 + i + 1)
                    nc.scalar.activation(gh[:, 512 * i:512 * i + 512], PS[:, 5 + i, :], ACT.Copy).then_inc(gh_done, 1)

            def gate(m):
                act.wait_ge(g_ready, m + 1)
                nc.scalar.activation(sgm, PS[:, 2, :], ACT.Silu, scale=srs[:, 0:1]).then_inc(sg_done, 1)

            def hi(m):
                act.wait_ge(aT_ready, m + 1)
                nc.scalar.activation(actT_h, PS[:, 4, :], ACT.Copy).then_inc(aTh_done, 1)

            def full(c, turns, m):
                for s in range(6):
                    cast(c + s + AHEAD, turns)
                    if s == 1:
                        act.wait_ge(aa_done, m)
                        gate(m)
                        hi(m - 1)

            def item(it, before):
                t0 = it * MOE_TURNS
                if before is not None:
                    act.wait_ge(y_ready, before + 1)
                    for i in range(2):
                        nc.scalar.activation(yh[:, 512 * i:512 * i + 512], PS[:, i, :], ACT.Copy,
                                             scale=sgate[:, 0:1]).then_inc(yh_done, 1)
                for s in range(4):
                    cast(b + s + AHEAD, t0)
                    if s == 1:
                        act.wait_ge(slot_rs, it + 1)
                        after(act, aa_done, it * 7)
                        gate(it * 7)
                full(b + 4, t0, it * 7 + 1)
                with act.Fori(0, 5) as j:
                    full(b + 10, t0 + j, it * 7 + 2 + j)
                gathered(it + 1)
                hi(it * 7 + 6)
                turned(it + 1)
                for s in range(2):
                    cast(b + 40 + s + AHEAD, t0)

            act.wait_ge(routed, 1)
            n = act.value_load(passes[0:1, 0:1], min_val=1, max_val=3)
            last = act.value_load(passes[0:1, 1:2], min_val=NE - 1, max_val=ITEMS - 1)
            gathered(0)
            turned(0)
            item(0, None)
            with act.Fori(0, last) as before:
                item(before + 1, before)
            act.wait_ge(y_ready, last + 1)
            for i in range(2):
                nc.scalar.activation(yh[:, 512 * i:512 * i + 512], PS[:, i, :], ACT.Copy,
                                     scale=sgate[:, 0:1]).then_inc(yh_done, 1)
            split_x(5)
            ple_act(act, cast, root, split_x, 1, n * (NE * MOE_TURNS))


        def slot_chunk(b, s):
            return (b["conv"] if s < 2 else b["gate"] - 2) + s


        def gate_tile(n):
            return zt[:, 8 + n % 4, :] if n < 8 else zt[:, 8 + n, :]


        @block.scalar
        def _(act):
            def cast(c, turns=0):
                act.wait_ge(raw_landed[c % RAW], 16 * (c // RAW + 1) + 16 * turns)
                if not (isinstance(turns, int) and c + RAW * turns < CAST):
                    act.wait_ge(chunk_begun, RAW * turns + c - CAST + 2)
                nc.scalar.activation(whi[:, c % CAST, :], raw[:, c % RAW, :], ACT.Copy).then_inc(hi_done, 1)

            def split_x(norm, tiles=range(KT)):
                for j in tiles:
                    act.wait_ge(*x_at(norm, j))
                    nc.scalar.activation(xht[:, j, :], x[:, j, :], ACT.Copy,
                                         scale=vec[:, GAIN[norm] + j:GAIN[norm] + j + 1]).then_inc(xh_ready, 1)

            def root(norm):
                k = turn_of(norm)
                act.wait_ge(stat_ready, k + 1)
                if k > 0:
                    act.wait_ge(rstd_ready, k)
                nc.scalar.activation(sq_root[:, :], PS[:, 3, 0:T], ACT.Sqrt, bias=epsb[:, :],
                                     scale=1.0 / D).then_inc(root_ready, 1)

            act.dma_start(vrow[0:16, :], A["norm_mix_g"].rearrange("l (k p) -> (l k) p", p=128)).then_inc(in_vec, 16)
            act.dma_start(vrow[16:32, :], A["norm_ffn_g"].rearrange("l (k p) -> (l k) p", p=128)).then_inc(in_vec, 16)
            act.dma_start(vrow[32:48, :], A["norm_ple_g"].rearrange("l (k p) -> (l k) p", p=128)).then_inc(in_vec, 16)
            act.dma_start(vrow[48:56, :], A["norm_final_g"].rearrange("(k p) -> k p", p=128)).then_inc(in_vec, 16)
            act.dma_start(wrow, A["conv_w"].rearrange("l w (k p) -> (l w k) p", p=128)).then_inc(in_crow, 16)
            act.dma_start(crow, A["state_conv"].rearrange("l b w c -> (b w) l c")).then_inc(in_crow, 16)
            act.wait_ge(in_id, 16)
            nc.scalar.activation(idr[:, :], ident, ACT.Copy).then_inc(idr_done, 1)
            act.wait_ge(eps_done, 1)
            act.wait_ge(tile_taken, 1)
            split_x(0, range(0, 1))
            cast(0)
            split_x(0, range(1, 8))
            cast(1)
            for l in range(DEPTH):
                b, t = CB[l], TB[l]
                mixn = NORM_OF["in", l]
                cast(b["in"] + AHEAD)
                root(mixn)
                for i in range(1, 14):
                    cast(b["in"] + i + AHEAD)
                    if l == 0 and i == 2:
                        act.wait_ge(p_ready, 1)
                        nc.scalar.activation(ph[:, :, :], PS[:, 4:8, 0:T], ACT.Copy).then_inc(p_hi, 1)
                act.wait_ge(a32, l + 1)
                nc.scalar.activation(fr[:, 0:4 * T], CHt, ACT.Copy).then_inc(a_hi, 1)
                act.wait_ge(cbT_ready, l + 1)
                if l > 0:
                    act.wait_ge(cout_sent, 32 * l)
                    act.wait_ge(so_sent, 16 * l)
                nc.scalar.activation(cout, PS[0:18, 7, 0:512], ACT.Copy).then_inc(cout_ready, 1)

                def sigmoids(s):
                    for n in (2 * s - 4, 2 * s - 3):
                        act.wait_ge(tile_taken, t["gate"] + n + 1)
                        g = gate_tile(n)
                        nc.scalar.activation(g, g, ACT.Sigmoid).then_inc(gsig, 1)

                for s in range(SLOTS):
                    if s < NH:
                        h = s
                        act.wait_ge(bank3_ready, 6 * l + s + 1)
                        for i in range(2):
                            nc.scalar.activation(ktok[:, 128 * i:128 * i + 128], PS[:, 3, 128 * i:128 * i + 128], ACT.Copy,
                                                 scale=kd[:, 2 * h + i:2 * h + i + 1]).then_inc(ktok_ready, 1)
                        nc.scalar.activation(kss, PS[0:8, 3, 256:384], ACT.Copy, scale=float(DK ** -0.5)).then_inc(ktok_ready, 1)
                    if 2 <= s < NH + 2:
                        act.wait_ge(bank3_ready, 6 * l + s + 1)
                        nc.scalar.activation(Qt[:, s - 2, SEQ:T], PS[:, 3, 384:384 + NB], ACT.Copy).then_inc(os_taken, 1)
                    if 1 <= s < NH + 1:
                        act.wait_ge(o_ready, 4 * l + s)
                        nc.scalar.activation(so[:, s - 1, :], PS[:, 5, 384:512], ACT.Copy).then_inc(so_ready, 1)
                        nc.scalar.activation(Qt[:, s - 1, 0:SEQ], PS[:, 5, 0:SEQ], ACT.Copy).then_inc(o_taken, 1)
                    if s == 6:
                        act.wait_ge(cent_ready, l + 1)
                        nc.scalar.activation(Qt, PS[:, 4:8, 0:T], ACT.Copy).then_inc(oc_ready, 1)
                    if s == 7:
                        act.wait_ge(var_ready, l + 1)
                        nc.scalar.activation(gstat[:, 0, :], PS[0:TT, 3, 0:12], ACT.Sqrt, bias=epsb[0:TT, :],
                                             scale=1.0 / DK).then_inc(groot_ready, 1)
                    cast(slot_chunk(b, s) + AHEAD)
                    if s > 2:
                        sigmoids(s - 1)
                    if s == 4:
                        nc.scalar.activation(Gt, Gt, ACT.Silu).then_inc(gsilu_ready, 1)
                    if s == 8:
                        act.wait_ge(r32, l + 1)
                        nc.scalar.activation(fr[:, 0:4 * T], Qt, ACT.Copy).then_inc(r_hi, 1)
                sigmoids(9)
                for i in range(2):
                    act.wait_ge(s_sent[i], 32 * (l + 1))
                act.wait_ge(so_sent, 16 * (l + 1))
                act.wait_ge(cout_sent, 32 * (l + 1))
                def m_round(j):
                    act.wait_ge(m32, 8 * l + j + 1)
                    nc.scalar.activation(frt[:, 8 + j, :], zt[:, j, :], ACT.Copy).then_inc(m_hi, 1)

                def take_pw(j):
                    p = t["pw"] + j
                    act.wait_ge(tile_ready, p + 1)
                    nc.scalar.activation(zt[:, 20 + j, :], PS[:, p % RING, 0:T], ACT.Copy).then_inc(tile_taken, 1)

                for i in range(2):
                    cast(b["ret"] + i + AHEAD)
                    for j in range(4 * i, 4 * i + 4 - i):
                        m_round(j)
                act.wait_ge(tile_taken, t["pw"])
                take_pw(0)
                m_round(7)
                take_pw(1)
                take_pw(2)
                cast(b["pw"] + AHEAD)
                for j in range(3, KT):
                    take_pw(j)
                for i in range(4):
                    cast(b["o"] + i + AHEAD)
                    split_x(NORM_OF["ffn", l], range(max(2 * i - 1, 0), 2 * i + 1))
                split_x(NORM_OF["ffn", l], (7,))
                if l == 0:
                    dense_act(act, cast, root, split_x)
                    ple_act(act, cast, root, split_x, 0)
                else:
                    moe_act(act, cast, root, split_x)
            act.wait_ge(stat_ready, 6)
            nc.scalar.activation(frs[:, 0, :], PS[0:TT, 1, 0:3], ACT.Sqrt, bias=epsb[0:TT, :],
                                 scale=1.0 / D).then_inc(root_ready, 1)
            act.wait_ge(frs_ready, 1)
            for i in range(3):
                act.wait_ge(finT_ready, 1)
                nc.scalar.activation(xtok[:, i, 0:512], PS[0:TT, FIN_BANK[i][0], :], ACT.Copy,
                                     scale=frs[:, 1, i:i + 1]).then_inc(out_left, 1)


        def dense_dve(dve, v, cast, recip, take, split_x):
            b, t = CB[0], TB[0]

            def pair(q, c, p, turns=0, first=False, pos=None):
                gb, ub_, ab = ffn_tiles(q)
                cast(c + AHEAD, turns)
                if first:
                    recip(1)
                for s in range(2):
                    take(p + s, gb[:, s, :], rstd[:, :], turns12=12 * turns)
                if pos is not None:
                    product(q - 1, p - 4, turns)
                cast(c + 1 + AHEAD, turns)
                if pos is not None:
                    rest(q - 1, pos, turns)
                for s in range(2):
                    take(p + 2 + s, ub_[:, s, :], rstd[:, :], turns12=12 * turns)

            def product(q, p, turns=0):
                gb, ub_, ab = ffn_tiles(q)
                dve.wait_ge(f_silu, q + 1 + 3 * turns)
                dve.wait_ge(tile_taken, p + 4 + 12 * turns)
                v.tensor_tensor(ab, gb, ub_, ALU.mult).then_inc(f_act, 1)

            def rest(q, pos, turns=0):
                ab = ffn_tiles(q)[2]
                dve.wait_ge(f_act, q + 1 + 3 * turns)
                dve.wait_ge(f_hi, q + 1 + 3 * turns)
                v.tensor_tensor(frt[:, ds(turns * 6 + 14 + 2 * pos, 2), :], ab,
                                frt[:, ds(turns * 6 + 2 * pos, 2), :].bitcast(F32), ALU.subtract).then_inc(f_lo, 1)

            for hf in range(2):
                c0, t0 = b["ffn"] + 22 * hf, t[f"gu{hf}"]
                pair(7 * hf, c0, t0, first=(hf == 0))
                with dve.Fori(0, 2) as it:
                    for q in range(3):
                        pair(7 * hf + 1 + q, c0 + 2 + 2 * q, t0 + 4 + 4 * q, it, pos=q)
                product(7 * hf + 6, t0 + 24)
                rest(7 * hf + 6, 6)
                for i in range(8):
                    cast(c0 + 14 + i + AHEAD)
                    if hf == 1 and i > 0:
                        split_x(16, 2, i - 1)
                    p = t[f"down{hf}"] + i
                    dve.wait_ge(tile_ready, p + 1)
                    v.tensor_tensor(x[:, i, :], PS[:, p % RING, 0:T], x[:, i, :], ALU.add).then_inc(tile_taken, 1)
                    dve.wait_ge(tile_taken, p + 1)
            split_x(16, 2, 7)


        def ple_dve(dve, v, cast, recip, take, split_x, l, turns=0):
            b, t = CB[l], TB[l]
            last = l == DEPTH - 1

            def add(i):
                for j in (2 * i, 2 * i + 1):
                    n = 8 * l + j
                    dve.wait_ge(psig, n + 1)
                    v.tensor_tensor(zt[:, 8 + j, :], zt[:, 20 + j, :], zt[:, 8 + j, :], ALU.mult).then_inc(pprod, 1)
                    dve.wait_ge(pprod, n + 1)
                    v.tensor_tensor(x[:, j, :], x[:, j, :], zt[:, 8 + j, :], ALU.add).then_inc(x_ready, 1)
                    dve.wait_ge(x_ready, n + 1)

            for i in range(4):
                if not (last and i + AHEAD >= 4):
                    cast(b["pg"] + i + AHEAD, turns)
                if i == 0:
                    recip(NORM_OF["ple", l])
                take(t["pg"] + 2 * i, zt[:, 8 + 2 * i, :], rstd[:, :])
                if i > 0:
                    add(i - 1)
                take(t["pg"] + 2 * i + 1, zt[:, 9 + 2 * i, :], rstd[:, :])
            add(3)
            if not last:
                for j in range(KT):
                    split_x(24, 3, j)


        def moe_dve(dve, v, cast, recip, take, split_x, link, n_chain, newton, more_squares):
            b = CB[1]["ffn"]
            dve.wait_ge(wr_hi, 1)
            v.tensor_tensor(wrl[:, :], wrr[:, :], wrh[:, :].bitcast(F32), ALU.subtract).then_inc(wr_lo, 1)
            dve.wait_ge(lgT_ready, 1)
            v.tensor_copy(lgT, PS[0:NE, 7, 0:T]).then_inc(lgT_done, 1)
            dve.wait_ge(route_act, 1)
            v.memset(rg[:, :, 1:2], 0.0).then_inc(dve_chain, 1)
            n_chain[0] += 1
            link(v.tensor_scalar(rt[:, 232:235], PS[0:TT, 7, 24:27], 1.0 / D, EPS, ALU.mult, ALU.add))
            link(v.reciprocal(rg[:, :, 0], rt[:, 0:3]))
            newton(rg[:, :, 0], rt[:, 232:235])
            lg = rt[:, 3:27].rearrange("p (t e) -> p t e", t=3)
            top = rt[:, 27:51].rearrange("p (t e) -> p t e", t=3)
            dif = rt[:, 54:60].rearrange("p (t e) -> p t e", t=3)
            ex = rt[:, 60:66].rearrange("p (t e) -> p t e", t=3)
            idf = rt[:, 66:90].rearrange("p (t e) -> p t e", t=3)
            den, rden = rt[:, 90:93], rt[:, 93:96]
            gt = rt[:, 96:102].rearrange("p (t e) -> p t e", t=3)
            eq = rt[:, 102:150].rearrange("p (i t e) -> p i t e", i=2, t=3)
            mask = rt[:, 150:174].rearrange("p (t e) -> p t e", t=3)
            gm = rt[:, 174:222].rearrange("p (i t e) -> p i t e", i=2, t=3)
            cnt = rt[0:1, 222:232]
            link(v.tensor_tensor(lg, PS[0:TT, 7, 0:24].rearrange("p (t e) -> p t e", t=3),
                                 rg[:, :, 0:1].to_broadcast([TT, 3, 8]), ALU.mult))
            for i in range(3):
                v.max(top[:, i, :], lg[:, i, :]).then_inc(dve_chain, 1)
            n_chain[0] += 3
            dve.wait_ge(dve_chain, n_chain[0])
            for i in range(3):
                v.max_index(idx[:, i, :], top[:, i, :], lg[:, i, :]).then_inc(dve_chain, 1)
            n_chain[0] += 3
            v.tensor_tensor(dif, top[:, :, 0:2], top[:, :, 0:1].to_broadcast([TT, 3, 2]),
                            ALU.subtract).then_inc(route_dve, 1)
            dve.wait_ge(dve_chain, n_chain[0])
            link(v.tensor_copy(idf[:, :, :], idx[:, :, :]))

            def token_rest(i):
                dve.wait_ge(tok_ready, 2 * i + 2)
                dve.wait_ge(tokh_done, i + 1)
                v.tensor_copy(htok_l[:, i // 2, 512 * (i % 2):512 * (i % 2) + 512],
                              PS[0:TT, 5 + i % 2, :]).then_inc(tokl_done, 1)

            token_rest(0)
            for i in range(2):
                ins = v.tensor_tensor(eq[:, i], iota8.unsqueeze(1).to_broadcast([TT, 3, 8]),
                                      idf[:, :, i:i + 1].to_broadcast([TT, 3, 8]), ALU.is_equal)
                ins.then_inc(dve_chain, 1)
            n_chain[0] += 2
            dve.wait_ge(dve_chain, n_chain[0])
            v.tensor_tensor(mask, eq[:, 0], eq[:, 1], ALU.add).then_inc(route_dve, 1)
            for i in range(1, 6):
                token_rest(i)
            dve.wait_ge(route_dve, 2)
            dve.wait_ge(rank_ready, 1)
            link(v.tensor_scalar(posm[:, :, 0:NE], PS[0:TT, 7, 32:56].rearrange("p (t e) -> p t e", t=3),
                                 10000.0, None, ALU.add))
            link(v.tensor_tensor(posm[:, :, 0:NE], posm[:, :, 0:NE], mask, ALU.mult))
            link(v.tensor_scalar(posm[:, :, 0:NE], posm[:, :, 0:NE], -10000.0, None, ALU.add))

            def select(it):
                for i in range(3):
                    v.tensor_scalar(sel[:, i, :], iota, posm[:, i, it if isinstance(it, slice) else ds(it, 1)],
                                    None, ALU.is_equal).then_inc(sel_ready, 1)

            select(slice(0, 1))
            dve.wait_ge(route_act, 2)
            link(v.tensor_tensor(den, ex[:, :, 0], ex[:, :, 1], ALU.add))
            link(v.reciprocal(rden, den))
            link(v.tensor_tensor(gt, ex, rden.unsqueeze(2).to_broadcast([TT, 3, 2]), ALU.mult))
            for i in range(2):
                link(v.tensor_tensor(gm[:, i], eq[:, i], gt[:, :, i:i + 1].to_broadcast([TT, 3, 8]), ALU.mult))
            for ps in range(3):
                v.tensor_tensor(rg[:, :, 2 + NE * ps:2 + NE * ps + NE], gm[:, 0], gm[:, 1], ALU.add).then_inc(dve_chain, 1)
            n_chain[0] += 3
            dve.wait_ge(count_ready, 1)
            link(v.max(cnt[:, 0:8], PS[0:1, 0, 0:8]))
            link(v.tensor_scalar(cnt[:, 8:9], cnt[:, 0:1], 128.5, 1.0, ALU.is_gt, ALU.add))
            link(v.scalar_tensor_tensor(cnt[:, 9:10], cnt[:, 0:1], 256.5, cnt[:, 8:9], ALU.is_gt, ALU.add))
            v.tensor_scalar(passes[:, 1:2], cnt[:, 9:10], float(NE), -1.0, ALU.mult, ALU.add).then_inc(dve_chain, 1)
            v.tensor_copy(passes[:, 0:1], cnt[:, 9:10]).then_inc(dve_chain, 1)
            for ps in range(1, 3):
                v.tensor_scalar(posm[:, :, NE * ps:NE * ps + NE], posm[:, :, 0:NE], -128.0 * ps, None,
                                ALU.add).then_inc(dve_chain, 1)
            v.tensor_scalar(posm[:, :, ITEMS:ITEMS + 1], posm[:, :, 0:1], -384.0, None, ALU.add).then_inc(dve_chain, 1)
            n_chain[0] += 5
            dve.wait_ge(dve_chain, n_chain[0])
            dve.nop().then_inc(routed, 1)

            def gathered(it):
                dve.wait_ge(gath_ready, it * 2 + 2)
                v.tensor_copy(gx[:, 512:1024], PS[:, 6, :]).then_inc(gx_right, 1)

            def turned(it):
                for i in range(2):
                    dve.wait_ge(gh_done, it * 2 + i + 1)
                    v.tensor_tensor(gl[:, 512 * i:512 * i + 512], PS[:, 5 + i, :],
                                    gh[:, 512 * i:512 * i + 512].bitcast(F32), ALU.subtract).then_inc(gl_done, 1)

            def outputs(it):
                for i in range(2):
                    dve.wait_ge(yh_done, it * 2 + i + 1)
                    v.scalar_tensor_tensor(yl[:, 512 * i:512 * i + 512], PS[:, i, :], sgate[:, 0:1],
                                           yh[:, 512 * i:512 * i + 512].bitcast(F32),
                                           ALU.mult, ALU.subtract).then_inc(yl_done, 1)

            def scattered(it, tiles, banks=(5, 6)):
                for j in tiles:
                    dve.wait_ge(scat_ready, it * 8 + j + 1)
                    v.tensor_tensor(x[:, j, :], PS[:, banks[j % len(banks)], 0:T], x[:, j, :], ALU.add).then_inc(scat_taken, 1)

            def product(m):
                dve.wait_ge(u_rdy, m + 1)
                dve.wait_ge(sg_done, m + 1)
                v.scalar_tensor_tensor(aam, PS[:, 3, :], srs[:, 0:1], sgm, ALU.mult, ALU.mult).then_inc(aa_done, 1)

            def lo(m):
                dve.wait_ge(aTh_done, m + 1)
                v.tensor_tensor(actT_l, PS[:, 4, :], actT_h.bitcast(F32), ALU.subtract).then_inc(aTl_done, 1)

            def full(c, turns, m):
                for s in range(6):
                    if s == 2:
                        lo(m - 1)
                    cast(c + s + AHEAD, turns)
                    if s == 4:
                        product(m)

            def item(it, before):
                t0 = it * MOE_TURNS
                back = (lambda tiles: scattered(before, tiles)) if before is not None else (lambda tiles: None)
                if before is not None:
                    outputs(before)
                cast(b + AHEAD, t0)
                cast(b + 1 + AHEAD, t0)
                back((0, 1))
                dve.wait_ge(table_ready, it + 1)
                v.tensor_copy(srs[:, :], PS[:, 7, 0:1]).then_inc(slot_rs, 1)
                v.tensor_copy(sgate[:, :], PS[:, 7, 2:3] if before is None else PS[:, 7, ds(it + 2, 1)]).then_inc(slot_gate, 1)
                cast(b + 2 + AHEAD, t0)
                back((2, 3))
                cast(b + 3 + AHEAD, t0)
                dve.wait_ge(slot_rs, it + 1)
                product(it * 7)
                back((4, 5))
                cast(b + 4 + AHEAD, t0)
                back((6, 7))
                dve.wait_ge(selT_ready, it + 1)
                v.tensor_copy(selT, PS[:, 7, 128:128 + T]).then_inc(selT_done, 1)
                select(slice(1, 2) if before is None else it + 1)
                cast(b + 5 + AHEAD, t0)
                lo(it * 7)
                for s in range(2, 6):
                    cast(b + 4 + s + AHEAD, t0)
                    if s == 4:
                        product(it * 7 + 1)
                with dve.Fori(0, 5) as j:
                    full(b + 10, t0 + j, it * 7 + 2 + j)
                gathered(it + 1)
                lo(it * 7 + 6)
                turned(it + 1)
                for s in range(2):
                    cast(b + 40 + s + AHEAD, t0)

            dve.wait_ge(routed, 1)
            n = dve.value_load(passes[0:1, 0:1], min_val=1, max_val=3)
            last = dve.value_load(passes[0:1, 1:2], min_val=NE - 1, max_val=ITEMS - 1)
            gathered(0)
            turned(0)
            item(0, None)
            with dve.Fori(0, last) as before:
                item(before + 1, before)
            outputs(last)
            scattered(last, range(KT), (5, 6, 2, 3, 4))
            dve.wait_ge(scat_taken, last * 8 + 8)
            dve.nop().then_inc(moe_done, 1)
            for j in range(KT):
                split_x(40, 5, j)
                if j == 4:
                    more_squares()
            ple_dve(dve, v, cast, recip, take, split_x, 1, n * (NE * MOE_TURNS))


        @block.vector
        def _(dve):
            v = nc.vector
            n_chain = [0]

            def link(ins):
                n_chain[0] += 1
                ins.then_inc(dve_chain, 1)
                dve.wait_ge(dve_chain, n_chain[0])

            def cast(c, turns=0):
                dve.wait_ge(hi_done, RAW * turns + c + 1)
                v.tensor_tensor(wlo[:, c % CAST, :], raw[:, c % RAW, :],
                                whi[:, c % CAST, :].bitcast(F32), ALU.subtract).then_inc(lo_done, 1)

            def split_x(n8, norm, j):
                dve.wait_ge(xh_ready, n8 + j + 1)
                v.scalar_tensor_tensor(xlt[:, j, :], x[:, j, :], vec[:, GAIN[norm] + j:GAIN[norm] + j + 1],
                                       xht[:, j, :].bitcast(F32), ALU.mult, ALU.subtract).then_inc(xl_ready, 1)

            def newton(y, ms, last=None):
                link(v.tensor_tensor(ms, ms, y, ALU.mult))
                link(v.scalar_tensor_tensor(ms, ms, -0.5, y, ALU.mult, ALU.mult))
                if last is None:
                    link(v.scalar_tensor_tensor(y, ms, 1.5, y, ALU.add, ALU.mult))
                else:
                    v.scalar_tensor_tensor(y, ms, 1.5, y, ALU.add, ALU.mult).then_inc(last, 1)

            def more_squares():
                v.tensor_tensor(nwt[:, :], x[:, 5, :], x[:, 5, :], ALU.mult).then_inc(dve_chain, 1)
                n_chain[0] += 1
                for j in (6, 7):
                    link(v.tensor_tensor(sq_root[:, :], x[:, j, :], x[:, j, :], ALU.mult))
                    ins = v.tensor_tensor(nwt[:, :], nwt[:, :], sq_root[:, :], ALU.add)
                    if j == 6:
                        link(ins)
                ins.then_inc(sq2_ready, 1)

            def recip(norm):
                k = turn_of(norm)
                dve.wait_ge(root_ready, k + 1)
                v.tensor_scalar(nwt[:, :], PS[:, 3, 0:T], 1.0 / D, EPS, ALU.mult, ALU.add).then_inc(ms_ready, 1)
                link(v.reciprocal(rstd[:, :], sq_root[:, :]))
                dve.wait_ge(ms_ready, k + 1)
                newton(rstd[:, :], nwt[:, :], rstd_ready)
                dve.wait_ge(rstd_ready, k + 1)

            def take(p, dst, in1, op=ALU.mult, turns12=0):
                dve.wait_ge(tile_ready, p + 1 + turns12)
                v.tensor_tensor(dst, PS[:, p % RING, 0:T], in1, op).then_inc(tile_taken, 1)

            v.memset(epsb[:, :], EPS).then_inc(eps_done, 1)
            dve.wait_ge(tile_ready, 1)
            v.tensor_copy(vec[:, 0:56], PS[:, 0, 0:56]).then_inc(tile_taken, 1)
            for j in range(KT):
                dve.wait_ge(tile_ready, 2 + j)
                v.tensor_copy(x[:, j, :], PS[:, (1 + j) % RING, 0:T]).then_inc(tile_taken, 1)
                dve.wait_ge(tile_taken, 2 + j)
            cast(0)
            for j in range(KT):
                split_x(0, 0, j)
            more_squares()
            dve.wait_ge(tile_ready, 10)
            v.tensor_copy(vec[:, 56:80], PS[:, 9 % RING, 128:152]).then_inc(dve_chain, 1)
            n_chain[0] += 1
            v.tensor_copy(cst[:, :, :, :].rearrange("p l k c -> p (l k c)"), PS[:, 9 % RING, 0:128]).then_inc(tile_taken, 1)
            cast(1)
            dve.wait_ge(in_con, 16)

            for l in range(DEPTH):
                b, t = CB[l], TB[l]
                mixn = NORM_OF["in", l]

                def w_in(i):
                    cast(b["in"] + i + AHEAD)
                    if i == 0:
                        recip(mixn)
                    for s in range(2):
                        take(t["in"] + 2 * i + s, zt[:, 2 * i + s, :], rstd[:, :])
                    if l == 0 and i == 2:
                        dve.wait_ge(p_hi, 1)
                        v.tensor_tensor(pl[:, :, :], PS[:, 4:8, 0:T], ph[:, :, :].bitcast(F32), ALU.subtract).then_inc(p_lo, 1)

                def rope(X, half, n):
                    def tab(a, lo):
                        return a[lo:lo + 64, :].unsqueeze(1).to_broadcast([64, 4, T])
                    if half == 0:
                        v.tensor_tensor(rtmp[0:64], X[64:128], tab(sin, 64), ALU.mult).then_inc(dve_chain, 1)
                        n_chain[0] += 1
                        link(v.tensor_tensor(rtmp[64:128], X[0:64], tab(sin, 0), ALU.mult))
                    else:
                        link(v.tensor_tensor(X, X, cos.unsqueeze(1).to_broadcast([128, 4, T]), ALU.mult))
                        v.tensor_tensor(X, X, rtmp, ALU.add).then_inc(rope_ready, 1)
                        dve.wait_ge(rope_ready, n)

                old = cst[:, l, :, :].rearrange("p k (b w) -> p k b w", w=2)

                def conv(tap):
                    for j in range(4):
                        w = vec[:, CONVW + 12 * l + 4 * tap + j:CONVW + 12 * l + 4 * tap + j + 1]
                        yp, ys = CCt[:, j, 0:SEQ], CCt[:, j, SEQ:T]
                        if tap == 2:
                            v.tensor_scalar(yp, ub[:, j, 2:2 + SEQ], w, None, ALU.mult).then_inc(dve_chain, 1)
                            ins = v.tensor_scalar(ys, us[:, j, :], w, None, ALU.mult)
                        else:
                            v.scalar_tensor_tensor(yp, ub[:, j, tap:tap + SEQ], w, yp, ALU.mult, ALU.add).then_inc(dve_chain, 1)
                            ins = v.scalar_tensor_tensor(ys, old[:, j, :, tap], w, ys, ALU.mult, ALU.add)
                        n_chain[0] += 2
                        ins.then_inc(dve_chain, 1)
                    dve.wait_ge(dve_chain, n_chain[0])

                for i in range(14):
                    w_in(i)
                    if i in (6, 7, 8):
                        if i == 6:
                            dve.wait_ge(u_ready, 2 * l + 2)
                        conv(8 - i)
                        if i == 8:
                            dve.nop().then_inc(y_conv, 1)
                    elif i in (9, 10):
                        rope(Qt, i - 9, 2 * l + 1)
                    elif i in (11, 12):
                        rope(Kt, i - 11, 2 * l + 2)
                dve.wait_ge(a_hi, l + 1)
                v.tensor_tensor(fr[:, 4 * T:8 * T].rearrange("p (k t) -> p k t", k=4), CHt,
                                frt[:, 0:4, :].bitcast(F32), ALU.subtract).then_inc(a_lo, 1)

                def gated(s):
                    for n in (2 * s - 4, 2 * s - 3):
                        dve.wait_ge(gsig, 16 * l + n + 1)
                        v.tensor_tensor(zt[:, n, :], zt[:, n, :], gate_tile(n), ALU.mult).then_inc(a_gated, 1)

                for s in range(SLOTS):
                    if 1 <= s < NH + 1:
                        r = 4 * l + s - 1
                        def state(hf):
                            dve.wait_ge(kv_outer, 2 * r + hf + 1)
                            S = St[r % 2][:, 512 * hf:512 * hf + 512]
                            v.scalar_tensor_tensor(S, S, float(np.float32(GAMMA[s - 1])), PS[:, 7, :],
                                                   ALU.mult, ALU.add).then_inc(s_new, 1)
                        dve.wait_ge(s_in[r % 2], 16 * (r // 2 + 1))
                        state(0)
                    if s < NH:
                        dve.wait_ge(vT_ready, 4 * l + s + 1)
                        v.tensor_copy(vtok, PS[:, 6, 0:256]).then_inc(vtok_ready, 1)
                        v.tensor_tensor(vd, PS[0:8, 6, 256:384].unsqueeze(1).to_broadcast([8, 8, 128]),
                                        eye8.unsqueeze(2).to_broadcast([8, 8, 128]), ALU.mult).then_inc(vtok_ready, 1)
                        dve.wait_ge(score_ready, 4 * l + s + 1)
                        v.tensor_tensor(sc[:, 0:256], PS[:, 4, 0:256], dec[:, s, :], ALU.mult).then_inc(sc_ready, 1)
                        v.tensor_tensor(sc[:, 256:384], PS[:, 4, 256:384], dec[:, s, 0:128], ALU.mult).then_inc(sc_ready, 1)
                    if 1 <= s < NH + 1:
                        state(1)
                    if s == 7:
                        dve.wait_ge(groot_ready, l + 1)
                        link(v.reciprocal(gstat[:, 1, :], gstat[:, 0, :]))
                        link(v.tensor_scalar(gstat[:, 0, :], PS[0:TT, 3, 0:12], 1.0 / DK, EPS, ALU.mult, ALU.add))
                        newton(gstat[:, 1, :], gstat[:, 0, :])
                        v.tensor_tensor(diag, ident[0:TT, 0:TT].unsqueeze(1).to_broadcast([TT, 12, TT]),
                                        gstat[:, 1, :].unsqueeze(2).to_broadcast([TT, 12, TT]), ALU.mult).then_inc(diag_ready, 1)
                    if s == 8:
                        dve.wait_ge(rsb_ready, l + 1)
                        dve.wait_ge(og_ready, l + 1)
                        v.tensor_tensor(Qt, Qt, PS[:, 4:8, 0:T], ALU.mult).then_inc(r32, 1)
                    cast(slot_chunk(b, s) + AHEAD)
                    if 3 <= s < 7:
                        gated(s - 1)
                    if s == 0:
                        dve.wait_ge(a32, l + 1)
                    if s == 9:
                        dve.wait_ge(r32, l + 1)
                        dve.wait_ge(r_hi, l + 1)
                        v.tensor_tensor(fr[:, 4 * T:8 * T].rearrange("p (k t) -> p k t", k=4), Qt,
                                        frt[:, 0:4, :].bitcast(F32), ALU.subtract).then_inc(r_lo, 1)
                    if s < 2:
                        for j in range(4 * s, 4 * s + 4):
                            p = t["conv"] + j
                            dve.wait_ge(tile_ready, p + 1)
                            v.tensor_copy(zt[:, j, :], PS[:, p % RING, 0:T]).then_inc(tile_taken, 1)
                    else:
                        for n in (2 * s - 4, 2 * s - 3):
                            take(t["gate"] + n, gate_tile(n), rstd[:, :])
                def m_rest(j):
                    dve.wait_ge(m_hi, 8 * l + j + 1)
                    v.tensor_tensor(frt[:, 16 + j, :], zt[:, j, :], frt[:, 8 + j, :].bitcast(F32),
                                    ALU.subtract).then_inc(m_lo, 1)

                dve.wait_ge(a_gated, 8 * (l + 1))
                for i in range(2):
                    for j in range(4 * i, 4 * i + 4):
                        if j % 4 == 2:
                            cast(b["ret"] + i + AHEAD)
                        p = t["ret"] + j
                        rg_ = zt[:, 16 + j, :]
                        dve.wait_ge(gsig, 16 * l + 8 + j + 1)
                        dve.wait_ge(tile_ready, p + 1)
                        v.tensor_tensor(rg_, PS[:, p % RING, 0:T], rg_, ALU.mult).then_inc(tile_taken, 1)
                        if j >= 2:
                            m_rest(j - 2)
                m_rest(6)
                m_rest(7)
                cast(b["pw"] + AHEAD)
                dve.wait_ge(tile_taken, t["o"])
                fn = NORM_OF["ffn", l]
                for i in range(4):
                    cast(b["o"] + i + AHEAD)
                    if i > 0:
                        split_x(8 * (1 + 3 * l), fn, 2 * i - 1)
                    for j in (2 * i, 2 * i + 1):
                        p = t["o"] + j
                        dve.wait_ge(tile_ready, p + 1)
                        v.tensor_tensor(x[:, j, :], PS[:, p % RING, 0:T], x[:, j, :], ALU.add).then_inc(tile_taken, 1)
                        dve.wait_ge(tile_taken, p + 1)
                    split_x(8 * (1 + 3 * l), fn, 2 * i)
                split_x(8 * (1 + 3 * l), fn, 7)
                if l == 0:
                    dense_dve(dve, v, cast, recip, take, split_x)
                    ple_dve(dve, v, cast, recip, take, split_x, 0)
                else:
                    moe_dve(dve, v, cast, recip, take, split_x, link, n_chain, newton, more_squares)
            v.tensor_tensor(nwt[:, :], x[:, 6, :], x[:, 6, :], ALU.mult).then_inc(sq2_ready, 1)
            v.tensor_tensor(sq_root[:, :], x[:, 7, :], x[:, 7, :], ALU.mult).then_inc(sq2_ready, 1)
            dve.wait_ge(root_ready, 6)
            link(v.tensor_scalar(frs[:, 2, :], PS[0:TT, 1, 0:3], 1.0 / D, EPS, ALU.mult, ALU.add))
            link(v.reciprocal(frs[:, 1, :], frs[:, 0, :]))
            newton(frs[:, 1, :], frs[:, 2, :], frs_ready)
            dve.wait_ge(frs_ready, 1)
            for i in range(3):
                dve.wait_ge(finT_ready, 1)
                v.tensor_scalar(xtok[:, i, 512:1024], PS[0:TT, FIN_BANK[i][1], :], frs[:, 1, i:i + 1], None,
                                ALU.mult).then_inc(out_right, 1)


        def x_split(n8):
            return xl_ready, [n8 + k + 1 for k in range(KT)]


        def pw_pe(chunk, l):
            b, t = CB[l], TB[l]
            chunk(b["pw"], t["pw"], 2, 8, ph[:, 2 * l:2 * l + 2, :], pl[:, 2 * l:2 * l + 2, :])


        def ple_pe(pe, chunk, stat, l, turns=0):
            b, t = CB[l], TB[l]
            for i in range(4):
                chunk(b["pg"] + i, t["pg"] + 2 * i, 8, 2, xht, xlt, turns=turns,
                      each=(x_split({0: 16, 1: 40}[l]) if i == 0 else None),
                      norm=2 if (l, i) == (0, 0) else None)
                if (l, i) == (1, 0):
                    stat(5)


        def moe_pe(pe, ready, three, chunk, stat):
            mm = nc.tensor.matmul
            b = CB[1]["ffn"]
            pe.wait_ge(wr_lo, 1)
            pe.wait_ge(idr_done, 1)
            for k in range(KT):
                pe.wait_ge(xl_ready, 32 + k + 1)
                ins = three(PS[0:NE, 7, 0:T], wrh[:, 8 * k:8 * k + 8], wrl[:, 8 * k:8 * k + 8],
                            xht[:, k, :], xlt[:, k, :], k == 0, k == KT - 1)
            ins.then_inc(lgT_ready, 1)
            pe.wait_ge(lgT_done, 1)
            for i in range(3):
                nc.tensor.transpose(PS[0:TT, 7, 8 * i:8 * i + 8], lgT[:, TT * i:TT * i + TT], con[0:8, C_ID:C_ID + 8])
            pe.wait_ge(sq_ready, 5)
            for i in range(3):
                ins = mm(PS[0:TT, 7, 24 + i:25 + i], sacc[:, TT * i:TT * i + TT], ones[:, 0:1], start=True, stop=True)
            ins.then_inc(logit_ready, 1)

            def places():
                pe.wait_ge(route_dve, 2)
                mask = rt[:, 150:174].rearrange("p (t e) -> p t e", t=3)
                for i in range(3):
                    for j in range(i + 1):
                        ins = mm(PS[0:TT, 7, 32 + 8 * i:40 + 8 * i], tri if j == i else con[0:TT, C_ONE:C_ONE + TT],
                           mask[:, j, :], start=j == 0, stop=j == i)
                ins.then_inc(rank_ready, 1)
                pe.wait_ge(tile_taken, TB[1]["o"] + 8)
                for j in range(3):
                    ins = mm(PS[0:TT, 0, 0:8], con[0:TT, C_ONE:C_ONE + TT], mask[:, j, :], start=j == 0, stop=j == 2)
                ins.then_inc(count_ready, 1)

            for i in range(6):
                for (src, bank, done) in ((xht, 3 + i % 2, tokh_done), (xlt, 5 + i % 2, tokl_done)):
                    if i > 1:
                        pe.wait_ge(done, i - 1)
                    for k in range(4):
                        ins = mm(PS[0:TT, bank, 128 * k:128 * k + 128],
                                 src[:, 4 * (i % 2) + k, TT * (i // 2):TT * (i // 2) + TT], idr[:, :],
                                 start=True, stop=True)
                    ins.then_inc(tok_ready, 1)
            places()

            def gather(it):
                pe.wait_ge(sel_ready, it * 3 + 3)
                for h in range(2):
                    for n, tok in enumerate((htok_h, htok_l)):
                        for i in range(3):
                            ins = mm(PS[:, 5 + h, :], sel[:, i, :], tok[:, i, 512 * h:512 * h + 512],
                                     start=n == 0 and i == 0, stop=n == 1 and i == 2)
                    ins.then_inc(gath_ready, 1)

            def turn_operands(it):
                for h, done in enumerate((gx_left, gx_right)):
                    pe.wait_ge(done, it + 1)
                    for k in range(4):
                        ins = nc.tensor.transpose(PS[:, 5 + h, 128 * k:128 * k + 128],
                                                  gx[:, 512 * h + 128 * k:512 * h + 128 * k + 128], ident)
                    ins.then_inc(gT_ready, 1)

            def up(c, s, bank, turns, done=None):
                ready(c + s, turns)
                for k in range(4):
                    kk = 4 * s + k
                    wh = whi[:, (c + s) % CAST, 512 * k:512 * k + 512]
                    wl = wlo[:, (c + s) % CAST, 512 * k:512 * k + 512]
                    ins = mm(PS[:, bank, :], gh[:, 128 * kk:128 * kk + 128], wh, start=kk == 0, stop=False)
                    if k == 0:
                        ins.then_inc(chunk_begun, 1)
                    mm(PS[:, bank, :], gh[:, 128 * kk:128 * kk + 128], wl, start=False, stop=False)
                    ins = mm(PS[:, bank, :], gl[:, 128 * kk:128 * kk + 128], wh, start=False, stop=kk == 7)
                if s == 1:
                    ins.then_inc(done, 1)

            def down(c, turns, first, last):
                for s in range(2):
                    ready(c + s, turns)
                    for k in range(2):
                        kk = 2 * s + k
                        ah = actT_h[:, 128 * kk:128 * kk + 128]
                        al = actT_l[:, 128 * kk:128 * kk + 128]
                        for h in range(2):
                            at = 1024 * k + 512 * h
                            wh, wl = whi[:, (c + s) % CAST, at:at + 512], wlo[:, (c + s) % CAST, at:at + 512]
                            ins = mm(PS[:, h, :], ah, wh, start=first and kk == 0, stop=False)
                            if k == 0 and h == 0:
                                ins.then_inc(chunk_begun, 1)
                            mm(PS[:, h, :], ah, wl, start=False, stop=False)
                            ins = mm(PS[:, h, :], al, wh, start=False, stop=last and kk == 3)
                if last:
                    ins.then_inc(y_ready, 1)

            def turn(m):
                pe.wait_ge(aa_done, m + 1)
                for k in range(4):
                    ins = nc.tensor.transpose(PS[:, 4, 128 * k:128 * k + 128], aam[:, 128 * k:128 * k + 128], ident)
                ins.then_inc(aT_ready, 1)

            def scatter(it, tiles, banks=(5, 6)):
                for j in tiles:
                    out = PS[:, banks[j % len(banks)], 0:T]
                    if j >= len(banks):
                        pe.wait_ge(scat_taken, it * 8 + j - len(banks) + 1)
                    mm(out, yh[:, 128 * j:128 * j + 128], selT, start=True, stop=False)
                    mm(out, yl[:, 128 * j:128 * j + 128], selT, start=False, stop=True).then_inc(scat_ready, 1)

            def rest(c, turns, m, first):
                turn(m - 1)
                pe.wait_ge(aa_done, m)
                up(c + 2, 0, 3, turns)
                up(c + 2, 1, 3, turns, u_rdy)
                pe.wait_ge(aTl_done, m)
                down(c + 4, turns, first, False)

            def item(it, before):
                t0 = it * MOE_TURNS
                back = (lambda tiles: scatter(before, tiles)) if before is not None else (lambda tiles: None)
                pe.wait_ge(gh_done, it * 2 + 2)
                pe.wait_ge(gl_done, it * 2 + 1)
                up(b, 0, 2, t0)
                pe.wait_ge(gl_done, it * 2 + 2)
                up(b, 1, 2, t0, g_ready)
                if before is not None:
                    pe.wait_ge(yl_done, before * 2 + 2)
                    pe.wait_ge(selT_done, it)
                back((0, 1))
                for i in range(3):
                    ins = mm(PS[:, 7, 0:2 + ITEMS], sel[:, i, :].bitcast(F32), rg[:, i, :], start=i == 0, stop=i == 2)
                ins.then_inc(table_ready, 1)
                up(b + 2, 0, 3, t0)
                back((2, 3))
                up(b + 2, 1, 3, t0, u_rdy)
                back((4, 5))
                pe.wait_ge(sg_done, it * 7 + 1)
                up(b + 4, 0, 2, t0)
                back((6, 7))
                pe.wait_ge(slot_gate, it + 1)
                for i in range(3):
                    ins = mm(PS[:, 7, 128 + TT * i:128 + TT * i + TT], sel[:, i, :], idr[0:TT, 0:TT], start=True, stop=True)
                ins.then_inc(selT_ready, 1)
                up(b + 4, 1, 2, t0, g_ready)
                rest(b + 4, t0, it * 7 + 1, True)
                with pe.Fori(0, 5) as j:
                    pe.wait_ge(sg_done, it * 7 + 2 + j)
                    up(b + 10, 0, 2, t0 + j)
                    up(b + 10, 1, 2, t0 + j, g_ready)
                    rest(b + 10, t0 + j, it * 7 + 2 + j, False)
                after(pe, scat_taken, it * 8)
                gather(it + 1)
                turn(it * 7 + 6)
                turn_operands(it + 1)
                pe.wait_ge(aTl_done, it * 7 + 7)
                down(b + 40, t0, False, True)

            pe.wait_ge(tokh_done, 6)
            pe.wait_ge(tokl_done, 6)
            gather(0)
            turn_operands(0)
            pe.wait_ge(routed, 1)
            n = pe.value_load(passes[0:1, 0:1], min_val=1, max_val=3)
            last = pe.value_load(passes[0:1, 1:2], min_val=NE - 1, max_val=ITEMS - 1)
            item(0, None)
            with pe.Fori(0, last) as before:
                item(before + 1, before)
            pe.wait_ge(yl_done, last * 2 + 2)
            scatter(last, range(KT), (5, 6, 2, 3, 4))
            pe.wait_ge(moe_done, 1)
            ple_pe(pe, chunk, stat, 1, n * (NE * MOE_TURNS))


        @block.tensor
        def _(pe):
            mm = nc.tensor.matmul

            def ready(c, turns=0):
                pe.wait_ge(lo_done, RAW * turns + c + 1)

            def free(p, turns12=0):
                if p >= RING:
                    pe.wait_ge(tile_taken, p - RING + 1 + turns12)
                return PS[:, p % RING, 0:T]

            def three(out, wh, wl, ah, al, first, last, begins=False):
                ins = mm(out, wh, ah, start=first, stop=False)
                if begins:
                    ins.then_inc(chunk_begun, 1)
                mm(out, wh, al, start=False, stop=False)
                return mm(out, wl, ah, start=False, stop=last)

            def chunk(c, p, nk, nt, ah, al, turns=0, turns12=0, each=None, norm=None):
                ready(c, turns)
                W = nt * 128
                for n in range(nt):
                    out = free(p + n, turns12)
                    for k in range(nk):
                        if each is not None and n == 0:
                            pe.wait_ge(each[0], each[1][k])
                        at = k * W + n * 128
                        ins = three(out, whi[:, c % CAST, at:at + 128], wlo[:, c % CAST, at:at + 128],
                                    ah[:, k, :], al[:, k, :], k == 0, k == nk - 1, n == 0 and k == 0)
                    ins.then_inc(tile_ready, 1)
                    if n == 0 and norm is not None:
                        stat(norm)

            def stat(norm):
                pe.wait_ge(sq_ready, norm + 1)
                if norm > 0:
                    pe.wait_ge(ms_ready, turn_of(norm))
                shared = norm in (0, 5)
                if shared:
                    pe.wait_ge(sq2_ready, 1 + norm // 5)
                    mm(PS[:, 3, 0:T], ones, nwt[:, :], start=True, stop=False)
                mm(PS[:, 3, 0:T], ones, sacc[:, :], start=not shared, stop=True).then_inc(stat_ready, 1)

            pe.wait_ge(in_id, 16)
            pe.wait_ge(in_vec, 64)
            nc.tensor.transpose(PS[:, 0, 0:56], vrow, con[0:56, C_ID:C_ID + 56]).then_inc(tile_ready, 1)
            pe.wait_ge(in_x, 48)
            for j in range(KT):
                out = free(1 + j)
                for i in range(3):
                    ins = nc.tensor.transpose(out[:, TT * i:TT * i + TT], xtok[:, i, 128 * j:128 * j + 128],
                                              con[0:TT, C_ID:C_ID + TT])
                ins.then_inc(tile_ready, 1)
            pe.wait_ge(in_crow, 32)
            free(9)
            nc.tensor.transpose(PS[:, 9 % RING, 128:152], wrow, con[0:24, C_ID:C_ID + 24])
            for l in range(DEPTH):
                for k in range(4):
                    ins = nc.tensor.transpose(PS[:, 9 % RING, (4 * l + k) * 16:(4 * l + k) * 16 + 16],
                                              crow[:, l, 128 * k:128 * k + 128], con[0:16, C_ID:C_ID + 16])
            ins.then_inc(tile_ready, 1)

            for l in range(DEPTH):
                b, t = CB[l], TB[l]
                chunk(b["in"], t["in"], 8, 2, xht, xlt, each=x_split(24 * l),
                      norm=3 if l == 1 else None)
                if l == 0:
                    stat(0)
                chunk(b["in"] + 1, t["in"] + 2, 8, 2, xht, xlt)
                if l == 0:
                    pe.wait_ge(in_p, 64)
                    for j in range(4):
                        for i in range(3):
                            ins = nc.tensor.transpose(PS[:, 4 + j, TT * i:TT * i + TT], ptok[:, i, 128 * j:128 * j + 128],
                                                      con[0:TT, C_ID:C_ID + TT])
                    ins.then_inc(p_ready, 1)
                with pe.Fori(0, 2) as it:
                    for s in range(6):
                        chunk(b["in"] + 2 + s, t["in"] + 4 + 2 * s, 8, 2, xht, xlt, turns=it, turns12=12 * it)
                pe.wait_ge(ms_ready, turn_of(NORM_OF["in", l]) + 1)
                pe.wait_ge(cbt_ready, l + 1)
                pe.wait_ge(p_lo, 1)
                for k in range(4):
                    ins = nc.tensor.transpose(PS[0:18, 7, 128 * k:128 * k + 128], cbt[:, k, :], ident)
                ins.then_inc(cbT_ready, 1)
                pe.wait_ge(rope_ready, 2 * l + 2)
                pe.wait_ge(tile_taken, t["in"] + 24)
                for s in range(SLOTS):
                    if s > 0 and s <= NH:
                        h, r = s - 1, 4 * l + s - 1
                        pe.wait_ge(ktok_ready, 3 * r + 3)
                        pe.wait_ge(vtok_ready, 2 * r + 2)
                        if h == 0:
                            pe.wait_ge(cout_ready, l + 1)
                        if r > 0:
                            pe.wait_ge(s_new, 2 * r)
                            pe.wait_ge(o_taken, r)

                        def outer(hf):
                            mm(PS[:, 7, :].rearrange("p (b e) -> p b e", b=4), kss, vd[:, 4 * hf:4 * hf + 4, :],
                               start=True, stop=True).then_inc(kv_outer, 1)

                        outer(0)
                        for i in range(2):
                            mm(PS[:, 5, 384:512], ktok[:, 128 * i:128 * i + 128], vtok[:, 128 * i:128 * i + 128],
                               start=i == 0, stop=i == 1)
                        pe.wait_ge(sc_ready, 2 * r + 2)
                        mm(PS[:, 5, 0:256], vtok[:, 0:128], sc[:, 0:256], start=True, stop=False, skip_group_check=True)
                        mm(PS[:, 5, 128:256], vtok[:, 128:256], sc[:, 256:384], start=False, stop=True,
                           skip_group_check=True).then_inc(o_ready, 1)
                        pe.wait_ge(s_new, 2 * r + 1)
                        outer(1)
                    if s < NH + 2:
                        if s > 2:
                            pe.wait_ge(os_taken, 4 * l + s - 2)
                        if s < NH:
                            for i in range(2):
                                nc.tensor.transpose(PS[:, 3, 128 * i:128 * i + 128], Kt[:, s, 128 * i:128 * i + 128], ident)
                            ins = nc.tensor.transpose(PS[0:8, 3, 256:384], Kt[:, s, SEQ:T], ident)
                        if s >= 2:
                            r = 4 * l + s - 2
                            pe.wait_ge(s_new, 2 * r + 2)
                            for i in range(NB):
                                ins = mm(PS[:, 3, 384 + i:385 + i], St[r % 2][:, 128 * i:128 * i + 128],
                                         Qt[:, s - 2, SEQ + i:SEQ + i + 1], start=True, stop=True)
                        ins.then_inc(bank3_ready, 1)
                    if s < NH:
                        for i in range(2):
                            nc.tensor.transpose(PS[:, 6, 128 * i:128 * i + 128], Vt[:, s, 128 * i:128 * i + 128], ident)
                        nc.tensor.transpose(PS[0:8, 6, 256:384], Vt[:, s, SEQ:T], ident).then_inc(vT_ready, 1)
                        mm(PS[:, 4, 0:256], Kt[:, s, 0:128], Qt[:, s, 0:256], start=True, stop=True)
                        mm(PS[:, 4, 256:384], Kt[:, s, 128:256], Qt[:, s, 128:256], start=True, stop=True).then_inc(score_ready, 1)
                    if s == 6:
                        pe.wait_ge(os_taken, 4 * l + 4)
                        pe.wait_ge(o_taken, 4 * l + 4)
                        for h in range(NH):
                            ins = mm(PS[:, 4 + h, 0:T], centre, Qt[:, h, :], start=True, stop=True)
                        ins.then_inc(cent_ready, 1)
                    if s == 7:
                        pe.wait_ge(osq_ready, l + 1)
                        for h in range(NH):
                            for i in range(3):
                                ins = mm(PS[0:TT, 3, 3 * h + i:3 * h + i + 1], rtmp[:, h, TT * i:TT * i + TT],
                                         ones[:, 0:1], start=True, stop=True)
                        ins.then_inc(var_ready, 1)
                    if s == 8:
                        pe.wait_ge(diag_ready, l + 1)
                        for h in range(NH):
                            ins = mm(PS[:, 4 + h, 0:T], ones[0:TT, :], diag[:, 3 * h:3 * h + 3, :], start=True, stop=True)
                        ins.then_inc(rsb_ready, 1)
                    if s < 2:
                        if s == 0:
                            pe.wait_ge(a_lo, l + 1)
                        chunk(b["conv"] + s, t["conv"] + 4 * s, 4, 4, frt[:, 0:4, :], frt[:, 4:8, :])
                    else:
                        chunk(b["gate"] + s - 2, t["gate"] + 2 * s - 4, 8, 2, xht, xlt)
                pe.wait_ge(r_lo, l + 1)
                for i in range(2):
                    chunk(b["ret"] + i, t["ret"] + 4 * i, 4, 4, frt[:, 0:4, :], frt[:, 4:8, :])
                pw_pe(chunk, l)
                for i in range(4):
                    chunk(b["o"] + i, t["o"] + 2 * i, 8, 2, frt[:, 8:16, :], frt[:, 16:24, :],
                          each=(m_lo, [8 * l + k + 1 for k in range(8)]) if i == 0 else None)
                if l == 0:
                    for hf in range(2):
                        c0, t0 = b["ffn"] + 22 * hf, t[f"gu{hf}"]
                        if hf == 0:
                            chunk(c0, t0, 8, 2, xht, xlt, each=x_split(8), norm=1)
                        else:
                            chunk(c0, t0, 8, 2, xht, xlt)
                        chunk(c0 + 1, t0 + 2, 8, 2, xht, xlt)
                        with pe.Fori(0, 2) as it:
                            for s in range(6):
                                chunk(c0 + 2 + s, t0 + 4 + 2 * s, 8, 2, xht, xlt, turns=it, turns12=12 * it)
                        for i in range(8):
                            chunk(c0 + 14 + i, t[f"down{hf}"] + i, 14, 1, frt[:, 0:14, :], frt[:, 14:28, :],
                                  each=(f_lo, [7 * hf + k // 2 + 1 for k in range(14)]) if i == 0 else None)
                    ple_pe(pe, chunk, stat, 0)
                else:
                    moe_pe(pe, ready, three, chunk, stat)
            pe.wait_ge(gdiag_done, KT)
            pe.wait_ge(ms_ready, 5)
            pe.wait_ge(tile_taken, TB[1]["pg"] + 8)
            for k in range(KT):
                if k == 6:
                    pe.wait_ge(sq_ready, 7)
                    pe.wait_ge(sq2_ready, 4)
                    for i in range(3):
                        for n, part in enumerate((sacc, nwt, sq_root)):
                            ins = mm(PS[0:TT, 1, i:i + 1], part[:, TT * i:TT * i + TT], ones[:, 0:1],
                                     start=n == 0, stop=n == 2)
                    ins.then_inc(stat_ready, 1)
                pe.wait_ge(x_ready, 8 + k + 1)
                for i in range(3):
                    ins = mm(PS[0:TT, FIN_BANK[i][k // 4], 128 * (k % 4):128 * (k % 4) + 128],
                             x[:, k, TT * i:TT * i + TT], gdiag[:, k, :], start=True, stop=True)
            ins.then_inc(finT_ready, 1)


_INS = ["x_prompt", "x_sample", "state_conv", "state_ret", "p_prompt", "p_sample", "norm_mix_g", "w_in",
        "conv_w", "w_conv_out", "w_ret_out", "w_o", "norm_ffn_g", "w_dense_gu", "w_dense_down",
        "w_router", "w_exp_gu", "w_exp_down", "norm_ple_g", "w_ple", "w_ple_gate", "norm_final_g"]
_OUTS = [("y_prompt", (1, SEQ, D)), ("y_sample", (NB, 1, D)), ("conv_prompt", (DEPTH, 1, CW - 1, DC)),
         ("ret_prompt", (DEPTH, 1, NH, DK, DK)), ("conv_sample", (DEPTH, NB, CW - 1, DC)),
         ("ret_sample", (DEPTH, NB, NH, DK, DK))]


def kernel(**inputs):
    import concourse.bacc as bacc
    from concourse.bass_utils import run_bass_kernel_spmd

    nc = bacc.Bacc("TRN2", target_bir_lowering=False, num_devices=1)
    arrays, A, O = {}, {}, {}
    given = {name: np.ascontiguousarray(inputs[name]) for name in _INS}
    given["constants"] = constants()
    for name, a in given.items():
        arrays[f"in_{name}"] = a
        A[name] = nc.dram_tensor(f"in_{name}", a.shape, mybir.dt.from_np(a.dtype), kind="ExternalInput").ap()
    for name, shape in _OUTS:
        O[name] = nc.dram_tensor(f"out_{name}", shape, mybir.dt.float32, kind="ExternalOutput").ap()
    program(nc, A, O)
    r = run_bass_kernel_spmd(nc, [arrays], core_ids=[0])
    return tuple(r.results[0][f"out_{name}"] for name, _ in _OUTS)
```
